# Optimizing a Trainium2 kernel written in Bass

```python
import jax, jax.numpy as jnp
from jax import lax
import numpy as np

D_MODEL = 1024
BATCH = 1
SEQ = 1024
DEPTH = 2
DEC_BATCH = 8
DEC_SEQ = 1
PAST_LEN = 1024
PAGE_SIZE = 128

N_EVEN = (DEPTH + 1) // 2
N_ODD = DEPTH // 2
EPS = 1e-6

DN_HEADS = 4
DN_DK = 128
DN_DV = 128
DN_CONV = 4
DN_CHUNK = 64
SW_HEADS = 8
SW_KV_HEADS = 2
SW_GROUP = SW_HEADS // SW_KV_HEADS
SW_HD = 64
WINDOW = 128
GLA_HEADS = 4
GLA_DK = 128
GLA_DV = 256
GLA_RANK = 16
GLA_TAU = 16.0
GLA_CHUNK = 64
D_FF = 4 * D_MODEL

DN_QK = DN_HEADS * DN_DK
DN_V = DN_HEADS * DN_DV
DN_CONV_CH = 2 * DN_QK + DN_V
SW_Q = SW_HEADS * SW_HD
SW_KV = SW_KV_HEADS * SW_HD
EVEN_IN = DN_CONV_CH + DN_V + 2 * DN_HEADS + SW_Q + 2 * SW_KV
EVEN_MIX = DN_V + SW_Q
GLA_QK = GLA_HEADS * GLA_DK
GLA_V = GLA_HEADS * GLA_DV
ODD_IN = 2 * GLA_QK + 2 * GLA_V + GLA_RANK

kernel_name = "hybrid_deltanet_swa_gla_step"

def _split(a, sizes):
    out, o = [], 0
    for s in sizes:
        out.append(a[..., o:o + s])
        o += s
    return out

def _pad_time(a, lp):
    pad = lp - a.shape[1]
    if pad == 0:
        return a
    widths = [(0, 0)] * a.ndim
    widths[1] = (0, pad)
    return jnp.pad(a, widths)

def rmsnorm(x, g):
    xf = x.astype(jnp.float32)
    y = xf * lax.rsqrt(jnp.mean(xf * xf, -1, keepdims=True) + EPS)
    return (y * g.astype(jnp.float32)).astype(x.dtype)

def l2norm(x):
    xf = x.astype(jnp.float32)
    return xf * lax.rsqrt(jnp.sum(xf * xf, -1, keepdims=True) + EPS)

def causal_conv(u, buf, w):
    L = u.shape[1]
    ext = jnp.concatenate([buf.astype(u.dtype), u], 1)
    out = ext[:, 0:L] * w[0]
    for i in range(1, DN_CONV):
        out = out + ext[:, i:i + L] * w[i]
    return out, ext[:, ext.shape[1] - (DN_CONV - 1):]

def _to_chunks(a, C, nc):
    B = a.shape[0]
    a = _pad_time(a.astype(jnp.float32), nc * C)
    a = a.reshape((B, nc, C) + a.shape[2:])
    a = jnp.moveaxis(a, 3, 2)
    return jnp.moveaxis(a, 1, 0)

def _from_chunks(o, L):
    nc, B, H, C, d = o.shape
    o = jnp.swapaxes(jnp.moveaxis(o, 0, 1), 2, 3).reshape(B, nc * C, H, d)
    return o[:, :L]

def gated_delta_chunked(q, k, v, g, beta, S0):
    L = q.shape[1]
    C = min(DN_CHUNK, L)
    nc = -(-L // C)
    qc, kc, vc, gc, bc = (_to_chunks(t, C, nc) for t in (q, k, v, g, beta))
    tri_incl = jnp.tril(jnp.ones((C, C), bool))
    tri_strict = jnp.tril(jnp.ones((C, C), jnp.float32), -1)
    eye = jnp.eye(C, dtype=jnp.float32)

    def step(S, inp):
        qi, ki, vi, gi, bi = inp
        G = jnp.cumsum(gi, -1)
        decay = jnp.exp(jnp.where(tri_incl, G[..., :, None] - G[..., None, :], -jnp.inf))
        kb = ki * bi[..., None]
        M = jnp.einsum('bhid,bhjd->bhij', kb, ki) * decay * tri_strict
        T = lax.linalg.triangular_solve(eye + M, jnp.broadcast_to(eye, M.shape),
                                        left_side=True, lower=True, unit_diagonal=True)
        eG = jnp.exp(G)[..., None]
        u = T @ (vi * bi[..., None])
        w = T @ (kb * eG)
        v_new = u - w @ S
        attn = jnp.einsum('bhid,bhjd->bhij', qi, ki) * decay
        o = (qi * eG) @ S + attn @ v_new
        g_last = G[..., -1]
        S = S * jnp.exp(g_last)[..., None, None] + jnp.einsum(
            'bhcd,bhce->bhde', ki * jnp.exp(g_last[..., None] - G)[..., None], v_new)
        return S, o

    S, o = lax.scan(step, S0, (qc, kc, vc, gc, bc))
    return _from_chunks(o, L), S

def gla_chunked(q, k, v, glog, S0):
    L = q.shape[1]
    C = min(GLA_CHUNK, L)
    nc = -(-L // C)
    qc, kc, vc, gc = (_to_chunks(t, C, nc) for t in (q, k, v, glog))
    tri_incl = jnp.tril(jnp.ones((C, C), bool))[:, :, None]

    def step(S, inp):
        qi, ki, vi, gi = inp
        G = jnp.cumsum(gi, axis=2)
        dec = jnp.exp(jnp.where(tri_incl, G[:, :, :, None, :] - G[:, :, None, :, :], -jnp.inf))
        attn = jnp.einsum('bhid,bhjd,bhijd->bhij', qi, ki, dec)
        o = (qi * jnp.exp(G)) @ S + attn @ vi
        gl = G[:, :, -1]
        S = S * jnp.exp(gl)[..., None] + jnp.einsum(
            'bhcd,bhce->bhde', ki * jnp.exp(gl[:, :, None] - G), vi)
        return S, o

    S, o = lax.scan(step, S0, (qc, kc, vc, gc))
    return _from_chunks(o, L), S

def swa_attention(q, k, v, k_past, v_past, sinks, start):
    B, L = q.shape[:2]
    Qb = min(WINDOW, L)
    nb = -(-L // Qb)
    Lp = nb * Qb
    k_all = jnp.concatenate([k_past.astype(k.dtype), _pad_time(k, Lp)], 1)
    v_all = jnp.concatenate([v_past.astype(v.dtype), _pad_time(v, Lp)], 1)
    idx = (jnp.arange(nb) * Qb)[:, None] + jnp.arange(WINDOW + Qb)[None]
    kb = k_all[:, idx]
    vb = v_all[:, idx]
    qb = _pad_time(q, Lp).reshape(B, nb, Qb, SW_KV_HEADS, SW_GROUP, SW_HD)
    qpos = start + jnp.arange(Lp).reshape(nb, Qb)
    kpos = start - WINDOW + idx
    rel = qpos[:, :, None] - kpos[:, None, :]
    valid = (rel >= 0) & (rel < WINDOW) & (kpos[:, None, :] >= 0)
    slopes = jnp.exp2(-8.0 * jnp.arange(1, SW_HEADS + 1, dtype=jnp.float32) / SW_HEADS)
    slopes = slopes.reshape(SW_KV_HEADS, SW_GROUP)[:, :, None, None]
    s = jnp.einsum('bnqkgd,bnskd->bnkgqs', qb, kb).astype(jnp.float32) * (SW_HD ** -0.5)
    s = s - slopes * rel[:, None, None].astype(jnp.float32)
    s = jnp.where(valid[None, :, None, None], s, -jnp.inf)
    sink = sinks.astype(jnp.float32).reshape(SW_KV_HEADS, SW_GROUP)[:, :, None, None]
    m = jnp.maximum(jnp.max(s, -1, keepdims=True), sink)
    p = jnp.exp(s - m)
    p = p / (jnp.sum(p, -1, keepdims=True) + jnp.exp(sink - m))
    o = jnp.einsum('bnkgqs,bnskd->bnqkgd', p.astype(v.dtype), vb)
    o = o.reshape(B, Lp, SW_Q)[:, :L]
    new_k = jnp.concatenate([k_past.astype(k.dtype), k], 1)[:, L:]
    new_v = jnp.concatenate([v_past.astype(v.dtype), v], 1)[:, L:]
    return o, new_k, new_v

def even_mixer(h, start, S0, conv_buf, k_past, v_past, w_in, conv_w, a_log, dt_bias, dn_norm, sinks, w_out):
    B, L, _ = h.shape
    f32 = jnp.float32
    proj = h @ w_in
    qkv, z, a, b, q_sw, k_sw, v_sw = _split(proj, [DN_CONV_CH, DN_V, DN_HEADS, DN_HEADS, SW_Q, SW_KV, SW_KV])
    conv, new_buf = causal_conv(qkv, conv_buf, conv_w)
    conv = jax.nn.silu(conv.astype(f32))
    qd, kd, vd = _split(conv, [DN_QK, DN_QK, DN_V])
    qd = l2norm(qd.reshape(B, L, DN_HEADS, DN_DK)) * (DN_DK ** -0.5)
    kd = l2norm(kd.reshape(B, L, DN_HEADS, DN_DK))
    vd = vd.reshape(B, L, DN_HEADS, DN_DV)
    beta = jax.nn.sigmoid(b.astype(f32))
    g = -jnp.exp(a_log.astype(f32)) * jax.nn.softplus(a.astype(f32) + dt_bias.astype(f32))
    o_dn, S = gated_delta_chunked(qd, kd, vd, g, beta, S0.astype(f32))
    o_dn = rmsnorm(o_dn, dn_norm) * jax.nn.silu(z.astype(f32)).reshape(B, L, DN_HEADS, DN_DV)
    o_dn = o_dn.reshape(B, L, DN_V).astype(h.dtype)
    o_sw, new_k, new_v = swa_attention(q_sw.reshape(B, L, SW_HEADS, SW_HD),
                                       k_sw.reshape(B, L, SW_KV_HEADS, SW_HD),
                                       v_sw.reshape(B, L, SW_KV_HEADS, SW_HD),
                                       k_past, v_past, sinks, start)
    out = jnp.concatenate([o_dn, o_sw.astype(h.dtype)], -1) @ w_out
    return out, S.astype(h.dtype), new_buf, new_k, new_v

def odd_mixer(h, S0, w_in, w_gate_up, b_gate, gla_norm, w_out):
    B, L, _ = h.shape
    f32 = jnp.float32
    proj = h @ w_in
    q, k, v, r, gdown = _split(proj, [GLA_QK, GLA_QK, GLA_V, GLA_V, GLA_RANK])
    glog = jax.nn.log_sigmoid((gdown @ w_gate_up + b_gate).astype(f32)) / GLA_TAU
    q = q.astype(f32).reshape(B, L, GLA_HEADS, GLA_DK) * (GLA_DK ** -0.5)
    k = k.astype(f32).reshape(B, L, GLA_HEADS, GLA_DK)
    v = v.astype(f32).reshape(B, L, GLA_HEADS, GLA_DV)
    o, S = gla_chunked(q, k, v, glog.reshape(B, L, GLA_HEADS, GLA_DK), S0.astype(f32))
    o = rmsnorm(o, gla_norm) * jax.nn.silu(r.astype(f32)).reshape(B, L, GLA_HEADS, GLA_DV)
    out = o.reshape(B, L, GLA_V).astype(h.dtype) @ w_out
    return out, S.astype(h.dtype)

def trunk(x, start, st_dn, st_conv, c_k, c_v, st_gla,
          norm_mix, norm_mlp, norm_final,
          even_w_in, dn_conv_w, dn_a_log, dn_dt_bias, dn_norm, sw_sinks, even_w_out,
          gla_w_in, gla_w_gate_up, gla_b_gate, gla_norm, gla_w_out,
          mlp_w_up, mlp_w_down):
    n_dn, n_conv, n_k, n_v, n_gla = [], [], [], [], []
    for layer in range(DEPTH):
        h = rmsnorm(x, norm_mix[layer])
        if layer % 2 == 0:
            e = layer // 2
            mix, S, buf, nk, nv = even_mixer(h, start, st_dn[e], st_conv[e], c_k[e], c_v[e],
                                             even_w_in[e], dn_conv_w[e], dn_a_log[e], dn_dt_bias[e],
                                             dn_norm[e], sw_sinks[e], even_w_out[e])
            n_dn.append(S); n_conv.append(buf); n_k.append(nk); n_v.append(nv)
        else:
            o_i = layer // 2
            mix, S = odd_mixer(h, st_gla[o_i], gla_w_in[o_i], gla_w_gate_up[o_i], gla_b_gate[o_i],
                               gla_norm[o_i], gla_w_out[o_i])
            n_gla.append(S)
        x = x + mix
        h = rmsnorm(x, norm_mlp[layer])
        x = x + jnp.square(jax.nn.relu(h @ mlp_w_up[layer])) @ mlp_w_down[layer]
    y = rmsnorm(x, norm_final)
    return y, jnp.stack(n_dn), jnp.stack(n_conv), jnp.stack(n_k), jnp.stack(n_v), jnp.stack(n_gla)

def setup_inputs(seed: int = 0) -> dict:
    key = jax.random.key(seed)
    ks = iter(jax.random.split(key, 32))
    nrm = lambda shape, s: jax.random.normal(next(ks), shape, jnp.float32) * s
    return {
        "x_prompt": nrm((BATCH, SEQ, D_MODEL), 1.0),
        "x_sample": nrm((DEC_BATCH, DEC_SEQ, D_MODEL), 1.0),
        "state_dn": nrm((N_EVEN, DEC_BATCH, DN_HEADS, DN_DK, DN_DV), 0.1),
        "state_dn_conv": nrm((N_EVEN, DEC_BATCH, DN_CONV - 1, DN_CONV_CH), 1.0),
        "cache_swa_k": nrm((N_EVEN, DEC_BATCH, WINDOW, SW_KV_HEADS, SW_HD), 1.0),
        "cache_swa_v": nrm((N_EVEN, DEC_BATCH, WINDOW, SW_KV_HEADS, SW_HD), 1.0),
        "state_gla": nrm((N_ODD, DEC_BATCH, GLA_HEADS, GLA_DK, GLA_DV), 0.3),
        "norm_mix": 1.0 + nrm((DEPTH, D_MODEL), 0.02),
        "norm_mlp": 1.0 + nrm((DEPTH, D_MODEL), 0.02),
        "norm_final": 1.0 + nrm((D_MODEL,), 0.02),
        "even_w_in": nrm((N_EVEN, D_MODEL, EVEN_IN), D_MODEL ** -0.5),
        "dn_conv_w": nrm((N_EVEN, DN_CONV, DN_CONV_CH), DN_CONV ** -0.5),
        "dn_a_log": jnp.log(jax.random.uniform(next(ks), (N_EVEN, DN_HEADS), jnp.float32, 1.0, 16.0)),
        "dn_dt_bias": nrm((N_EVEN, DN_HEADS), 0.1),
        "dn_norm": 1.0 + nrm((N_EVEN, DN_DV), 0.02),
        "sw_sinks": nrm((N_EVEN, SW_HEADS), 0.5),
        "even_w_out": nrm((N_EVEN, EVEN_MIX, D_MODEL), EVEN_MIX ** -0.5),
        "gla_w_in": nrm((N_ODD, D_MODEL, ODD_IN), D_MODEL ** -0.5),
        "gla_w_gate_up": nrm((N_ODD, GLA_RANK, GLA_QK), GLA_RANK ** -0.5),
        "gla_b_gate": nrm((N_ODD, GLA_QK), 0.1),
        "gla_norm": 1.0 + nrm((N_ODD, GLA_DV), 0.02),
        "gla_w_out": nrm((N_ODD, GLA_V, D_MODEL), GLA_V ** -0.5),
        "mlp_w_up": nrm((DEPTH, D_MODEL, D_FF), D_MODEL ** -0.5),
        "mlp_w_down": nrm((DEPTH, D_FF, D_MODEL), D_FF ** -0.5),
    }

def reference(x_prompt, x_sample, state_dn, state_dn_conv, cache_swa_k, cache_swa_v, state_gla,
              norm_mix, norm_mlp, norm_final,
              even_w_in, dn_conv_w, dn_a_log, dn_dt_bias, dn_norm, sw_sinks, even_w_out,
              gla_w_in, gla_w_gate_up, gla_b_gate, gla_norm, gla_w_out,
              mlp_w_up, mlp_w_down):
    dt = x_prompt.dtype
    weights = (norm_mix, norm_mlp, norm_final,
               even_w_in, dn_conv_w, dn_a_log, dn_dt_bias, dn_norm, sw_sinks, even_w_out,
               gla_w_in, gla_w_gate_up, gla_b_gate, gla_norm, gla_w_out,
               mlp_w_up, mlp_w_down)
    z_dn = jnp.zeros((N_EVEN, BATCH, DN_HEADS, DN_DK, DN_DV), dt)
    z_conv = jnp.zeros((N_EVEN, BATCH, DN_CONV - 1, DN_CONV_CH), dt)
    z_kv = jnp.zeros((N_EVEN, BATCH, WINDOW, SW_KV_HEADS, SW_HD), dt)
    z_gla = jnp.zeros((N_ODD, BATCH, GLA_HEADS, GLA_DK, GLA_DV), dt)
    y_prompt, p_dn, p_conv, p_k, p_v, p_gla = trunk(x_prompt, 0, z_dn, z_conv, z_kv, z_kv, z_gla, *weights)
    y_sample, s_dn, s_conv, s_k, s_v, s_gla = trunk(x_sample, PAST_LEN, state_dn, state_dn_conv,
                                                    cache_swa_k, cache_swa_v, state_gla, *weights)
    return (y_prompt, y_sample, p_dn, p_conv, p_k, p_v, p_gla, s_dn, s_conv, s_k, s_v, s_gla)


_drawn_inputs = setup_inputs


def setup_inputs(seed=0):
    import zlib

    import numpy as np

    out = dict(_drawn_inputs(seed))
    spreads = {}
    factors = {'norm_final': 8.147,
     'dn_norm': 5.963,
     'sw_sinks': 5.642,
     'gla_norm': 26.822,
     'norm_mlp': 2.699}
    for name, (base, spread) in spreads.items():
        noise = np.random.default_rng([zlib.crc32(name.encode()), seed]).standard_normal(out[name].shape)
        drawn = base * np.exp(spread * noise) if base else spread * noise
        out[name] = __import__('jax').numpy.asarray(drawn.astype(out[name].dtype))
    for name, factor in factors.items():
        out[name] = (out[name] * factor).astype(out[name].dtype)
    return out
```

```python
import concourse.bass as bass
from concourse import mybir
from contextlib import ExitStack

F32 = mybir.dt.float32
F32R = mybir.dt.float32r
ALU = mybir.AluOpType
ACT = mybir.ActivationFunctionType
AX = mybir.AxisListType

P = 128
D = 1024
KT = D // P
SEQ = 1024
DEC = 8
TOK = SEQ + DEC
NCH = 3
CW = TOK // NCH
NB = SEQ // P
EPS = 1e-6
HEADS = 4
CHUNK = 64
DFF = 4 * D
CONV = 4
HD = 64
SWH, KVH = 8, 2
RANK = 16
TAU = 16.0
GDV = 256
E_Z = 3 * 512
E_A = E_Z + 512
E_B = E_A + HEADS
E_Q = E_B + HEADS
E_K = E_Q + SWH * HD
E_V = E_K + KVH * HD
T_Q, T_K, T_V, T_Z, T_SQ, T_SK, T_SV, T_AB = 0, 4, 8, 12, 16, 20, 21, 22
EVEN_TILES = 23
G_Q, G_K, G_V, G_R, G_D = 0, 4, 8, 16, 24
ODD_TILES = 25
O_DOWN = 2 * 512 + 2 * 1024
V_MIX, V_MLP, V_FIN, V_CONV, V_GB, V_DN, V_GN = 0, 16, 32, 40, 88, 92, 93
V_ROWS = 95

TB = TOK * 4
BASE = 16512
PROJ_AT = BASE
ACT_AT = PROJ_AT + 25 * TB
ACT_LO_AT = ACT_AT + 8 * TB
WORK_AT = ACT_AT + 16 * TB
END = 229344


class Ctx:
    pass


def make(nc, es, ins, outs):
    c = Ctx()
    c.nc, c.es = nc, es
    c.ins, c.outs = ins, outs
    c.sems = {}
    c.tiles_before = 0
    c.norms_before = 0

    def at(name, shape, offset, dt=F32):
        return nc.alloc_sbuf_tensor_at(name, shape, dt, offset=offset)

    def sem(name):
        if name not in c.sems:
            c.sems[name] = nc.alloc_semaphore(name=name)
        return c.sems[name]
    c.at, c.sem = at, sem

    top = END
    def const(name, shape, dt=F32):
        nonlocal top
        n = 4
        for s in shape[1:]:
            n *= s
        top -= (n + 31) // 32 * 32
        return at(name, shape, top, dt)
    c.ident = const("ident", [P, P])
    c.ones = const("ones", [P, P])
    c.vcols = const("vcols", [P, V_ROWS + 1])
    c.eps = const("eps", [P, 1])
    c.const = const
    c.bufT = const("buf_cols", [P, 12, DEC * (CONV - 1)])
    c.tail = const("conv_tail", [P, 12, CONV - 1 + DEC])
    c.proj = at("proj", [P, 25, TOK], PROJ_AT)
    c.act_hi = at("act_hi", [P, KT, TOK], ACT_AT, F32R)
    c.act_lo = at("act_lo", [P, KT, TOK], ACT_LO_AT, F32R)
    w = WORK_AT
    c.w_raw = at("w_raw", [P, 2, KT, P], w); w += 2 * KT * P * 4
    c.w_hi = at("w_hi", [P, 2, KT, P], w, F32R); w += 2 * KT * P * 4
    c.w_lo = at("w_lo", [P, 2, KT, P], w, F32R); w += 2 * KT * P * 4
    c.scr_at = w
    c.tmp = at("tmp", [P, 2, TOK], w); w += 2 * TB
    c.rb = at("rb", [P, TOK], w); w += TB
    c.free_at = w
    c.const_at = top
    c.ps = es.enter_context(nc.psum_tensor("ps", [P, 8, 512], F32))
    c.x_save = nc.dram_tensor("x_save", [P, KT, TOK], F32).ap()

    c.passed = {e.engine: sem(f"passed_{n}") for n, e in enumerate((nc.scalar, nc.vector, nc.gpsimd, nc.tensor))}
    c.raw_in = [sem("raw_in0"), sem("raw_in1")]
    c.hi_done, c.lo_done, c.tiles_done, c.evac_done = map(sem, ("hi_done", "lo_done", "tiles_done", "evac_done"))
    return c


def reach(c, eng, sem, value):
    eng.wait_ge(sem, value)
    if not isinstance(value, int):
        eng.sem_inc(c.passed[eng.engine], 1)



def load_tile(c, sp, slot, g, src):
    sp.wait_ge(c.lo_done, g + 1)
    sp.dma_start(c.w_raw[:, slot, :, 0:src.shape[2]], src).then_inc(c.raw_in[slot], 16)


def split_hi(c, act, slot, g):
    act.wait_ge(c.raw_in[slot], g * 8 + (16 - 8 * slot))
    act.wait_ge(c.tiles_done, g + 1)
    c.nc.scalar.activation(c.w_hi[:, slot], c.w_raw[:, slot], ACT.Copy).then_inc(c.hi_done, 1)


def split_lo(c, dve, slot, g):
    dve.wait_ge(c.hi_done, g + 1)
    c.nc.vector.tensor_tensor(c.w_lo[:, slot], c.w_raw[:, slot], c.w_hi[:, slot].bitcast(F32),
                              ALU.subtract).then_inc(c.lo_done, 1)


def multiply_tile(c, pe, slot, g, hi, lo, ready=None):
    pe.wait_ge(c.lo_done, g + 3)
    pe.wait_ge(c.evac_done, g + 1)
    last = None
    for ch in range(NCH):
        cols = slice(ch * CW, (ch + 1) * CW)
        out = c.ps[:, 3 * slot + ch, 0:CW]
        for k in range(KT):
            if ready and ch == 0:
                ready(k)
            for n, (w, x) in enumerate(((c.w_hi, hi), (c.w_hi, lo), (c.w_lo, hi))):
                last = c.nc.tensor.matmul(out, w[:, slot, k, :], x[:, k, cols],
                                          start=(k == 0 and n == 0), stop=(k == KT - 1 and n == 2))
    last.then_inc(c.tiles_done, 1)


def tile_psum(c, slot):
    return c.ps[:, 3 * slot:3 * slot + 3, 0:CW]


def chunked(ap):
    return ap.rearrange("p (c n) -> p c n", c=NCH)


def in_pairs(eng, n, body):
    if n // 2 == 1:
        body(0, 0)
        body(1, 1)
    elif n // 2:
        with eng.Fori(0, n // 2, 1) as pair:
            i = pair * 2
            body(i, 0)
            body(i + 1, 1)
    if n % 2:
        body(n - 1, 0)


def lead_pairs(eng, n, ahead, first, second=None, last_phase=False):
    def turn(t, odd, leads=True):
        first(t, odd)
        if leads:
            ahead(t + 2, odd)
        if second:
            second(t, odd)
    looped = (n - 2 * last_phase) // 2 * 2
    if looped:
        with eng.Fori(0, looped // 2, 1) as pair:
            i = pair * 2
            turn(i, 0)
            turn(i + 1, 1)
    for t in range(looped, n):
        turn(t, t % 2, not last_phase or t + 2 < n)


def cols_view(w, first, count=P):
    return w.rearrange("(k p) n -> p k n", p=P)[:, :, first:first + count]



def setup_phase(c, first_tiles):
    nc, ins = c.nc, c.ins
    loads, consts, small = c.sem("setup_loads"), c.sem("setup_consts"), c.sem("setup_small")
    turned_small, turned, placed = c.sem("small_turned"), c.sem("rows_turned"), c.sem("rows_placed")
    rows = c.at("x_rows", [P, 2, D], ACT_AT)
    srows = c.at("sample_rows", [DEC, D], ACT_AT + 8192)
    vrows = c.at("v_rows", [V_ROWS, P], ACT_AT + 12288)
    brows = c.at("buf_rows", [DEC * 3, 12, P], ACT_AT + 16384)
    rows_in = [c.sem("rows_in0"), c.sem("rows_in1")]
    prompt = ins["x_prompt"].rearrange("a (b p) d -> (a b) p d", p=P)
    with nc.Block() as block:
        @block.sync
        def _(sp):
            sp.dma_start(srows[:], ins["x_sample"].rearrange("b s d -> (b s) d")).then_inc(loads, 16)
            for name, row, n in (("norm_mix", V_MIX, 16), ("norm_mlp", V_MLP, 16), ("norm_final", V_FIN, 8),
                                 ("dn_conv_w", V_CONV, 48), ("gla_b_gate", V_GB, 4), ("dn_norm", V_DN, 1),
                                 ("gla_norm", V_GN, 2)):
                a = ins[name]
                if len(a.shape) == 3:
                    a = a.rearrange("e i c -> (e i c)")
                elif len(a.shape) == 2:
                    a = a.rearrange("e c -> (e c)")
                sp.dma_start(vrows[row:row + n, :], a.rearrange("(k p) -> k p", p=P)).then_inc(loads, 16)
            sp.dma_start(brows[:], ins["state_dn_conv"].rearrange("e b i (t p) -> (e b i) t p", p=P)).then_inc(loads, 16)
            for b in range(2):
                sp.dma_start(rows[:, b], prompt[b]).then_inc(rows_in[b], 16)
            with sp.Fori(1, NB // 2, 1) as pair:
                b = pair * 2
                for slot in range(2):
                    sp.wait_ge(turned, 2 * b + (2 * slot - 2))
                    sp.dma_start(rows[:, slot], prompt[bass.ds(b + slot, 1)].rearrange("a p d -> p (a d)")
                                 ).then_inc(rows_in[slot], 16)
            for t, parts in enumerate(first_tiles):
                load_tile(c, sp, t, t, parts)

        @block.gpsimd
        def _(pool):
            g = nc.gpsimd
            g.memset(c.ident[:], 0.0).then_inc(consts, 1)
            g.memset(c.ones[:], 1.0).then_inc(consts, 1)
            g.memset(c.eps[:], EPS).then_inc(consts, 1)
            pool.wait_ge(consts, 3)
            g.affine_select(out=c.ident[:], in_=c.ident[:], compare_op=ALU.not_equal, fill=1.0, base=0,
                            pattern=[[-1, P]], channel_multiplier=1).then_inc(consts, 1)

        @block.scalar
        def _(act):
            for t in range(2):
                split_hi(c, act, t, t)

        @block.tensor
        def _(pe):
            pe.sem_inc(c.tiles_done, 2)
            pe.wait_ge(loads, 16 * 9)
            pe.wait_ge(consts, 4)
            nc.tensor.transpose(c.ps[:, 0, 0:V_ROWS], vrows[:], c.ident[0:V_ROWS, 0:V_ROWS]).then_inc(turned_small, 1)
            for g3 in range(3):
                for t in range(4):
                    last = nc.tensor.transpose(c.ps[:, 1 + g3, t * 24:(t + 1) * 24], brows[:, 4 * g3 + t, :],
                                               c.ident[0:24, 0:24])
                if g3 < 2:
                    last.then_inc(turned_small, 1)
            for t in range(KT):
                last = nc.tensor.transpose(c.ps[:, 3, 256 + t * DEC:256 + (t + 1) * DEC],
                                           srows[:, t * P:(t + 1) * P], c.ident[0:DEC, 0:DEC])
            last.then_inc(turned_small, 1)
            with pe.Fori(0, NB // 2, 1) as pair:
                b = pair * 2
                for slot in range(2):
                    pe.wait_ge(rows_in[slot], b * 8 + 16)
                    for half in range(2):
                        pe.wait_ge(placed, 2 * b + (2 * slot + half + 1))
                        for t in range(4):
                            k = 4 * half + t
                            last = nc.tensor.transpose(c.ps[:, 4 + 2 * slot + half, t * P:(t + 1) * P],
                                                       rows[:, slot, k * P:(k + 1) * P], c.ident[:])
                        last.then_inc(turned, 1)

        @block.vector
        def _(dve):
            v = nc.vector
            dve.sem_inc(c.lo_done, 2)
            dve.sem_inc(c.evac_done, 2)
            dve.sem_inc(placed, 4)
            dve.wait_ge(turned_small, 1)
            v.tensor_copy(c.vcols[:, 0:V_ROWS], c.ps[:, 0, 0:V_ROWS]).then_inc(small, 1)
            for g3 in range(3):
                dve.wait_ge(turned_small, 2 + g3)
                v.tensor_copy(c.bufT[:, 4 * g3:4 * g3 + 4, :], c.ps[:, 1 + g3, 0:96].rearrange("p (t n) -> p t n", t=4)
                              ).then_inc(small, 1)
            v.tensor_copy(c.proj[:, 0:KT, SEQ:TOK], c.ps[:, 3, 256:256 + KT * DEC].rearrange("p (t n) -> p t n", t=KT)
                          ).then_inc(small, 1)
            with dve.Fori(0, NB // 2, 1) as pair:
                b = pair * 2
                for slot in range(2):
                    for half in range(2):
                        reach(c, dve, turned, 2 * b + (2 * slot + half + 1))
                        v.tensor_copy(c.proj[:, 4 * half:4 * half + 4, bass.ds((b + slot) * P, P)],
                                      c.ps[:, 4 + 2 * slot + half, :].rearrange("p (t n) -> p t n", t=4)
                                      ).then_inc(placed, 1)
            for t in range(2):
                split_lo(c, dve, t, t)



def norm_phase(c, vcol, save=False):
    nc = c.nc
    n0 = c.norms_before
    c.norms_before += 1
    squares, summed, scale = c.sem("norm_squares"), c.sem("norm_summed"), c.sem("norm_scale")
    normed, upper, lower = c.sem("norm_normed"), c.sem("norm_upper"), c.sem("norm_lower")
    x = c.proj
    saved = c.sem("x_saved")
    sq = ht = c.tmp
    with nc.Block() as block:
        if save:
            @block.sync
            def _(sp):
                sp.dma_start(c.x_save, x[:, 0:KT, :]).then_inc(saved, 16)

        @block.scalar
        def _(act):
            for k in range(KT):
                if k >= 2:
                    act.wait_ge(summed, KT * n0 + k - 1)
                nc.scalar.activation(sq[:, k % 2], x[:, k, :], ACT.Square).then_inc(squares, 1)
            act.wait_ge(summed, KT * n0 + KT)
            nc.scalar.activation(chunked(c.rb[:]), c.ps[:, 0:3, 0:CW], ACT.Ln, bias=c.eps[:], scale=1.0 / D
                                 ).then_inc(scale, 1)
            act.wait_ge(scale, 2 * n0 + 1)
            nc.scalar.activation(c.rb[:], c.rb[:], ACT.Exp, scale=-0.5).then_inc(scale, 1)
            for k in range(KT):
                act.wait_ge(normed, KT * n0 + k + 1)
                nc.scalar.activation(c.act_hi[:, k, :], ht[:, k % 2], ACT.Copy).then_inc(upper, 1)

        @block.tensor
        def _(pe):
            for k in range(KT):
                pe.wait_ge(squares, KT * n0 + k + 1)
                for ch in range(NCH):
                    last = nc.tensor.matmul(c.ps[:, ch, 0:CW], c.ones[:], sq[:, k % 2, ch * CW:(ch + 1) * CW],
                                            start=k == 0, stop=k == KT - 1)
                last.then_inc(summed, 1)

        @block.vector
        def _(dve):
            dve.wait_ge(scale, 2 * n0 + 2)

            def lower_part(k):
                dve.wait_ge(upper, KT * n0 + k + 1)
                nc.vector.tensor_tensor(c.act_lo[:, k, :], ht[:, k % 2], c.act_hi[:, k, :].bitcast(F32), ALU.subtract
                                        ).then_inc(lower, 1)
            for k in range(KT):
                if k >= 2:
                    lower_part(k - 2)
                    dve.wait_ge(lower, KT * n0 + k - 1)
                nc.vector.scalar_tensor_tensor(out=ht[:, k % 2], in0=x[:, k, :], scalar=c.vcols[:, vcol + k:vcol + k + 1],
                                               in1=c.rb[:], op0=ALU.mult, op1=ALU.mult).then_inc(normed, 1)
            lower_part(KT - 2)
            lower_part(KT - 1)



def conv_projection_phase(c, next_tiles):
    nc = c.nc
    base, n = c.tiles_before, 12
    c.tiles_before += n
    w_in = c.ins["even_w_in"].rearrange("e d n -> (e d) n")
    conved, silued, saved, tails = c.sem("conved"), c.sem("silued"), c.sem("x_saved"), c.sem("tails_kept")
    conv = c.tmp
    with nc.Block() as block:
        @block.sync
        def _(sp):
            with sp.Fori(1, n // 2, 1) as pair:
                t = pair * 2
                for odd in range(2):
                    load_tile(c, sp, odd, t + (base + odd), w_in.rearrange("(k p) n -> p k n", p=P)[
                        :, :, bass.ds((t + odd) * P, P)])
            for t, parts in enumerate(next_tiles):
                load_tile(c, sp, (base + n + t) % 2, base + n + t, parts)

        @block.tensor
        def _(pe):
            in_pairs(pe, n, lambda t, odd: multiply_tile(c, pe, odd, t + base, c.act_hi, c.act_lo))

        @block.scalar
        def _(act):
            act.sem_inc(silued, 2)
            act.wait_ge(saved, 16)

            def evacuate(t, odd):
                reach(c, act, c.tiles_done, t + (base + 3))
                nc.scalar.activation(chunked(c.proj[:, t, :]), tile_psum(c, odd), ACT.Copy).then_inc(c.evac_done, 1)

            def silu(t, odd):
                reach(c, act, conved, t * CONV_STEPS + CONV_STEPS)
                nc.scalar.activation(c.proj[:, t, :], conv[:, odd], ACT.Silu).then_inc(silued, 1)
            lead_pairs(act, n, lambda t, odd: split_hi(c, act, odd, t + base), evacuate, silu)

        @block.vector
        def _(dve):
            v = nc.vector

            def conv_tile(t, odd):
                u = c.proj[:, t, :]
                o = conv[:, odd]

                def w(i):
                    return c.vcols[:, bass.ds(t + (V_CONV + 12 * i), 1)]
                reach(c, dve, c.evac_done, t + (base + 3))
                reach(c, dve, silued, t + 1)
                s = t * CONV_STEPS
                v.tensor_scalar(o, u, w(CONV - 1), None, ALU.mult).then_inc(conved, 1)
                v.tensor_copy(c.tail[:, t, :], u[:, SEQ - CONV + 1:TOK]).then_inc(tails, 1)
                for i in range(CONV - 1):
                    back = CONV - 1 - i
                    reach(c, dve, conved, s + 1 + 2 * i)
                    v.scalar_tensor_tensor(out=o[:, back:SEQ], in0=u[:, 0:SEQ - back], scalar=w(i),
                                           in1=o[:, back:SEQ], op0=ALU.mult, op1=ALU.add).then_inc(conved, 1)
                    v.scalar_tensor_tensor(out=o[:, SEQ:TOK],
                                           in0=c.bufT[:, t, :].rearrange("p (b i) -> p i b", i=CONV - 1)[:, i, :],
                                           scalar=w(i), in1=o[:, SEQ:TOK], op0=ALU.mult, op1=ALU.add
                                           ).then_inc(conved, 1)
            lead_pairs(dve, n, lambda t, odd: split_lo(c, dve, odd, t + base), lambda t, odd: None, conv_tile)


CONV_STEPS = 1 + 2 * (CONV - 1)



def projection_phase(c, tiles, next_tiles, first, saves=1):
    nc = c.nc
    base, n = c.tiles_before, len(tiles)
    c.tiles_before += n
    parity = base % 2
    with nc.Block() as block:
        @block.sync
        def _(sp):
            for t, parts in list(enumerate(tiles + next_tiles))[2:]:
                load_tile(c, sp, (base + t) % 2, base + t, parts)

        @block.tensor
        def _(pe):
            in_pairs(pe, n, lambda t, odd: multiply_tile(c, pe, (odd + parity) % 2, t + base, c.act_hi, c.act_lo))

        @block.scalar
        def _(act):
            act.wait_ge(c.sem("x_saved"), 16 * saves)

            def evacuate(t, odd):
                reach(c, act, c.tiles_done, t + (base + 3))
                nc.scalar.activation(chunked(c.proj[:, t + first, :]), tile_psum(c, (odd + parity) % 2), ACT.Copy
                                     ).then_inc(c.evac_done, 1)
            lead_pairs(act, n, lambda t, odd: split_hi(c, act, (odd + parity) % 2, t + base), evacuate)

        @block.vector
        def _(dve):
            lead_pairs(dve, n, lambda t, odd: split_lo(c, dve, (odd + parity) % 2, t + base), lambda t, odd: None)



def output_projection_phase(c, tiles, next_tiles, reloads):
    nc = c.nc
    base, n = c.tiles_before, KT
    c.tiles_before += n
    parity = base % 2
    reloaded = c.sem("x_reloaded")
    with nc.Block() as block:
        @block.sync
        def _(sp):
            sp.dma_start(c.proj[:, 0:KT, :], c.x_save).then_inc(reloaded, 16)
            for t, parts in list(enumerate(tiles + next_tiles))[2:]:
                load_tile(c, sp, (base + t) % 2, base + t, parts)

        @block.tensor
        def _(pe):
            in_pairs(pe, n, lambda t, odd: multiply_tile(c, pe, (odd + parity) % 2, t + base, c.act_hi, c.act_lo))

        @block.scalar
        def _(act):
            lead_pairs(act, n, lambda t, odd: split_hi(c, act, (odd + parity) % 2, t + base), lambda t, odd: None)

        @block.vector
        def _(dve):
            dve.wait_ge(reloaded, 16 * reloads)

            def add(t, odd):
                add_to_residual(c, dve, t, (odd + parity) % 2, t + base)
            lead_pairs(dve, n, lambda t, odd: split_lo(c, dve, (odd + parity) % 2, t + base), add)


def add_to_residual(c, dve, k, slot, g):
    dve.wait_ge(c.tiles_done, g + 3)
    x = chunked(c.proj[:, k, :])
    c.nc.vector.tensor_tensor(x, x, tile_psum(c, slot), ALU.add).then_inc(c.evac_done, 1)



def mlp_phase(c, layer, next_tiles):
    nc = c.nc
    nf = DFF // D
    base, n = c.tiles_before, 2 * KT * nf
    c.tiles_before += n
    parity = base % 2
    h0 = layer * KT * nf
    last_phase = not next_tiles
    up = c.ins["mlp_w_up"][layer].rearrange("(k p) n -> p k n", p=P)
    down = c.ins["mlp_w_down"][layer].rearrange("(f k p) n -> p f k n", p=P, k=KT)
    relued, squared = c.sem("hidden_relued"), c.sem("hidden_squared")
    upper, lower = c.sem("hidden_upper"), c.sem("hidden_lower")
    hid_hi = c.at(f"hidden_hi{layer}", [P, KT, TOK], PROJ_AT + KT * TB, F32R)
    hid_lo = c.at(f"hidden_lo{layer}", [P, KT, TOK], PROJ_AT + 2 * KT * TB, F32R)
    h = c.tmp

    def sections(eng, do_up, do_down, leads):
        def part(f, leads_on):
            for section, do in enumerate((do_up, do_down)):
                looped = KT if leads_on or section == 0 else KT - 2
                with eng.Fori(0, looped // 2, 1) as pair:
                    t = pair * 2
                    for odd in range(2):
                        do(f * (2 * KT) + (t + (base + section * KT + odd)), t + odd, f, odd, True)
                for t in range(looped, KT):
                    do(f * (2 * KT) + (t + base + section * KT), t, f, t % 2, False)
        if leads and last_phase:
            with eng.Fori(0, nf - 1, 1) as f:
                part(f, True)
            part(nf - 1, False)
        else:
            with eng.Fori(0, nf, 1) as f:
                part(f, True)

    with nc.Block() as block:
        @block.sync
        def _(sp):
            def load_up(t, f, odd, g):
                load_tile(c, sp, (odd + parity) % 2, g, up[:, :, bass.ds(f * D + t * P, P)])

            def load_down(t, f, odd, g):
                load_tile(c, sp, (odd + parity) % 2, g, down[:, bass.ds(f, 1), :, bass.ds(t * P, P)]
                          .rearrange("p f k n -> p (f k) n"))

            def both(f, skip):
                with sp.Fori(skip // 2, KT // 2, 1) as pair:
                    t = pair * 2
                    for odd in range(2):
                        load_up(t + odd, f, odd, f * (2 * KT) + (t + (base + odd)))
                with sp.Fori(0, KT // 2, 1) as pair:
                    t = pair * 2
                    for odd in range(2):
                        load_down(t + odd, f, odd, f * (2 * KT) + (t + (base + KT + odd)))
            both(0, 2)
            with sp.Fori(1, nf, 1) as f:
                both(f, 0)
            for t, parts in enumerate(next_tiles):
                load_tile(c, sp, (base + n + t) % 2, base + n + t, parts)

        @block.tensor
        def _(pe):
            def do_up(g, t, f, odd, _):
                multiply_tile(c, pe, (odd + parity) % 2, g, c.act_hi, c.act_lo)

            def do_down(g, t, f, odd, _):
                def ready(k):
                    if k == 0 or k == KT - 1:
                        pe.wait_ge(lower, f * KT + (h0 + 2 + (KT - 1 if k == 0 else KT)))
                multiply_tile(c, pe, (odd + parity) % 2, g, hid_hi, hid_lo, ready)
            sections(pe, do_up, do_down, False)

        @block.scalar
        def _(act):
            def do_up(g, t, f, odd, leads):
                slot = (odd + parity) % 2
                n_hid = f * KT + t + h0
                act.wait_ge(c.tiles_done, g + 3)
                act.wait_ge(lower, n_hid + 1)
                nc.scalar.activation(chunked(h[:, odd]), tile_psum(c, slot), ACT.Relu).then_inc(c.evac_done, 1)
                split_hi(c, act, slot, g + 2)
                reach(c, act, squared, n_hid + 1)
                nc.scalar.activation(hid_hi[:, t, :], h[:, odd], ACT.Copy).then_inc(upper, 1)

            def do_down(g, t, f, odd, leads):
                if leads:
                    split_hi(c, act, (odd + parity) % 2, g + 2)
            sections(act, do_up, do_down, True)

        @block.vector
        def _(dve):
            if layer == 0:
                dve.sem_inc(lower, 2)
            def do_up(g, t, f, odd, leads):
                n_hid = f * KT + t + h0
                split_lo(c, dve, (odd + parity) % 2, g + 2)
                dve.wait_ge(c.evac_done, g + 3)
                nc.vector.tensor_tensor(h[:, odd], h[:, odd], h[:, odd], ALU.mult).then_inc(squared, 1)
                reach(c, dve, upper, n_hid + 1)
                nc.vector.tensor_tensor(hid_lo[:, t, :], h[:, odd], hid_hi[:, t, :].bitcast(F32), ALU.subtract
                                        ).then_inc(lower, 1)

            def do_down(g, t, f, odd, leads):
                add_to_residual(c, dve, t, (odd + parity) % 2, g)
                if leads:
                    split_lo(c, dve, (odd + parity) % 2, g + 2)
            sections(dve, do_up, do_down, True)



def final_phase(c):
    nc = c.nc
    n0 = c.norms_before
    c.norms_before += 1
    squares, summed, scale = c.sem("norm_squares"), c.sem("norm_summed"), c.sem("norm_scale")
    scaled, turned, rowed = c.sem("y_scaled"), c.sem("y_turned"), c.sem("y_rowed")
    stored = [c.sem("y_stored0"), c.sem("y_stored1")]
    x, sq = c.proj, c.tmp
    y = c.at("y_cols", [P, 2, KT, P], ACT_AT)
    rows = c.at("y_rows", [P, 2, D], ACT_AT + 2 * KT * P * 4)
    y_out = c.outs["y_prompt"].rearrange("a (b p) d -> (a b) p d", p=P)
    last_store = {0: NB // 2 + 1, 1: NB // 2}
    with nc.Block() as block:
        @block.scalar
        def _(act):
            for k in range(KT):
                if k >= 2:
                    act.wait_ge(summed, KT * n0 + k - 1)
                nc.scalar.activation(sq[:, k % 2], x[:, k, :], ACT.Square).then_inc(squares, 1)
            act.wait_ge(summed, KT * n0 + KT)
            nc.scalar.activation(chunked(c.rb[:]), c.ps[:, 0:3, 0:CW], ACT.Ln, bias=c.eps[:], scale=1.0 / D
                                 ).then_inc(scale, 1)
            act.wait_ge(scale, 2 * n0 + 1)
            nc.scalar.activation(c.rb[:], c.rb[:], ACT.Exp, scale=-0.5).then_inc(scale, 1)
            act.sem_inc(rowed, 4)

            def to_rows(b, slot, n):
                act.wait_ge(stored[slot], b * 8 + (16 - 8 * slot))
                for half in range(2):
                    act.wait_ge(turned, 2 * b + (half + 5))
                    nc.scalar.activation(rows[0:n, slot, half * 512:half * 512 + 512], c.ps[0:n, 4 + 2 * slot + half, :],
                                         ACT.Copy).then_inc(rowed, 1)
            with act.Fori(0, NB // 2, 1) as pair:
                b = pair * 2
                to_rows(b, 0, P)
                to_rows(b + 1, 1, P)
            to_rows(NB, 0, DEC)

        @block.tensor
        def _(pe):
            for k in range(KT):
                pe.wait_ge(squares, KT * n0 + k + 1)
                for ch in range(NCH):
                    last = nc.tensor.matmul(c.ps[:, ch, 0:CW], c.ones[:], sq[:, k % 2, ch * CW:(ch + 1) * CW],
                                            start=k == 0, stop=k == KT - 1)
                last.then_inc(summed, 1)

            pe.sem_inc(turned, 4)

            def turn(b, slot, n):
                pe.wait_ge(scaled, 2 * b + 4)
                for half in range(2):
                    pe.wait_ge(rowed, 2 * b + (half + 1))
                    for t in range(4):
                        last = nc.tensor.transpose(c.ps[0:n, 4 + 2 * slot + half, t * P:(t + 1) * P],
                                                   y[:, slot, 4 * half + t, 0:n], c.ident[:])
                    last.then_inc(turned, 1)
            with pe.Fori(0, NB // 2, 1) as pair:
                b = pair * 2
                turn(b, 0, P)
                turn(b + 1, 1, P)
            turn(NB, 0, DEC)

        @block.vector
        def _(dve):
            dve.wait_ge(scale, 2 * n0 + 2)
            dve.sem_inc(scaled, 2)

            def scale_block(b, slot, n):
                dve.wait_ge(turned, 2 * b + 2)
                cols = bass.ds(b * P, n)
                reach(c, dve, scaled, 2 * b + 2)
                nc.vector.tensor_tensor(y[:, slot, :, 0:n], x[:, 0:KT, cols],
                                        c.rb[:, cols].unsqueeze(1).to_broadcast([P, KT, n]), ALU.mult).then_inc(scaled, 1)
                dve.wait_ge(scaled, 2 * b + 3)
                nc.vector.tensor_tensor(y[:, slot, :, 0:n], y[:, slot, :, 0:n],
                                        c.vcols[:, V_FIN:V_FIN + KT].unsqueeze(2).to_broadcast([P, KT, n]), ALU.mult
                                        ).then_inc(scaled, 1)
            with dve.Fori(0, NB // 2, 1) as pair:
                b = pair * 2
                scale_block(b, 0, P)
                scale_block(b + 1, 1, P)
            scale_block(NB, 0, DEC)

        @block.sync
        def _(sp):
            for s in stored:
                sp.sem_inc(s, 16)
            with sp.Fori(0, NB // 2, 1) as pair:
                b = pair * 2
                for slot in range(2):
                    sp.wait_ge(rowed, 2 * b + (2 * slot + 6))
                    sp.dma_start(y_out[bass.ds(b + slot, 1)].rearrange("a p d -> p (a d)"), rows[:, slot]
                                 ).then_inc(stored[slot], 16)
            sp.wait_ge(rowed, 2 * NB + 6)
            sp.dma_start(c.outs["y_sample"].rearrange("b s d -> (b s) d"), rows[0:DEC, 0]).then_inc(stored[0], 16)
            for slot in range(2):
                sp.wait_ge(stored[slot], 16 + 16 * last_store[slot])


class Area:

    def __init__(self, c, name, places):
        self.c, self.name, self.places = c, name, [list(p) for p in places]

    def __call__(self, name, shape, dt=F32):
        n = 4
        for s in shape[1:]:
            n *= s
        n = (n + 31) // 32 * 32
        for place in self.places:
            if place[0] + n <= place[1]:
                place[0] += n
                return self.c.at(f"{self.name}_{name}", shape, place[0] - n, dt)
        raise ValueError(f"no room for {name}: {self.places}")

    def passing(self, name):
        return Area(self.c, name, self.places)


def mixer_area(c, name):
    return Area(c, name, [(ACT_AT, WORK_AT), (c.scr_at, c.const_at)])



def delta_prepare_phase(c, area):
    nc = c.nc
    a0 = c.ins
    rows = c.delta_rows = area("rows", [36, TOK])
    brief = area.passing("delta_prepare")
    y, t1 = brief("gate_in", [8, TOK]), brief("gate_tmp", [8, TOK])
    mask = brief("chunk_mask", [8, TOK])
    gs = brief("gate_consts", [8, 4])
    loads, ready, step, actd = c.sem("gate_loads"), c.sem("gate_consts"), c.sem("gate_steps"), c.sem("gate_logs")
    squared, summed, logged = c.sem("unit_squares"), c.sem("unit_summed"), c.sem("unit_logged")
    factored, scaled = c.sem("unit_factored"), c.sem("unit_scaled")
    sq, r = brief("unit_squares", [P, 2, TOK]), brief("unit_factor", [P, 2, TOK])
    with nc.Block() as block:
        @block.sync
        def _(sp):
            sp.wait_ge(ready, 6)
            sp.dma_start(gs[0:4, 1:2], a0["dn_dt_bias"].rearrange("e h -> h e")).then_inc(loads, 16)
            sp.dma_start(gs[0:4, 2:3], a0["dn_a_log"].rearrange("e h -> h e")).then_inc(loads, 16)

        @block.gpsimd
        def _(pool):
            g = nc.gpsimd
            g.memset(gs[:], -1.0).then_inc(ready, 1)
            g.memset(mask[:], 0.0).then_inc(ready, 1)
            g.memset(rows[:], 0.0).then_inc(ready, 1)
            pool.wait_ge(ready, 3)
            g.memset(gs[0:4, 0:1], 1.0).then_inc(ready, 1)
            g.memset(gs[:, 1:2], 0.0).then_inc(ready, 1)
            g.memset(mask[0:4, 0:SEQ].rearrange("p (c n) -> p c n", n=CHUNK)[:, :, 1:CHUNK], 1.0).then_inc(ready, 1)

        @block.scalar
        def _(act):
            act.wait_ge(loads, 32)
            nc.scalar.activation(gs[0:4, 2:3], gs[0:4, 2:3], ACT.Exp).then_inc(actd, 1)
            act.wait_ge(step, 3)
            nc.scalar.activation(t1[:], t1[:], ACT.Exp).then_inc(actd, 1)
            act.wait_ge(actd, 2)
            nc.scalar.activation(t1[:], t1[:], ACT.Ln, bias=c.ones[0:8, 0:1]).then_inc(actd, 1)
            act.sem_inc(factored, 2)

            def factor(t, odd):
                act.wait_ge(summed, t + 3)
                act.wait_ge(scaled, t + 1)
                nc.scalar.activation(chunked(r[:, odd]), tile_psum(c, odd), ACT.Ln, bias=c.eps[:]).then_inc(logged, 1)
                act.wait_ge(logged, t + 3)
                nc.scalar.activation(r[:, odd], r[:, odd], ACT.Exp, scale=-0.5).then_inc(factored, 1)
            in_pairs(act, 8, factor)

        @block.tensor
        def _(pe):
            def add_up(t, odd):
                pe.wait_ge(squared, t + 1)
                pe.wait_ge(logged, t + 1)
                for ch in range(NCH):
                    last = nc.tensor.matmul(c.ps[:, 3 * odd + ch, 0:CW], c.ones[:], sq[:, odd, ch * CW:(ch + 1) * CW],
                                            start=True, stop=True)
                last.then_inc(summed, 1)
            in_pairs(pe, 8, add_up)

        @block.vector
        def _(dve):
            v = nc.vector
            dve.wait_ge(actd, 1)
            dve.wait_ge(ready, 6)
            v.tensor_scalar(gs[0:4, 2:3], gs[0:4, 2:3], -1.0, None, ALU.mult).then_inc(step, 1)
            v.tensor_scalar(y[:], c.proj[0:8, T_AB, :], gs[:, 0:1], gs[:, 1:2], ALU.mult, ALU.add).then_inc(step, 1)
            dve.wait_ge(step, 2)
            v.scalar_tensor_tensor(out=t1[:], in0=y[:], scalar=-1.0, in1=y[:], op0=ALU.mult, op1=ALU.min
                                   ).then_inc(step, 1)
            dve.wait_ge(actd, 3)
            v.scalar_tensor_tensor(out=y[:], in0=y[:], scalar=0.0, in1=t1[:], op0=ALU.max, op1=ALU.add
                                   ).then_inc(step, 1)
            dve.wait_ge(step, 4)
            v.tensor_scalar(y[:], y[:], gs[:, 2:3], None, ALU.mult).then_inc(step, 1)
            dve.wait_ge(step, 5)
            v.tensor_tensor_scan(rows[0:8, :], mask[:], y[:], 0.0, ALU.mult, ALU.add).then_inc(step, 1)
            dve.wait_ge(step, 6)
            g4 = rows[0:4, 0:SEQ].rearrange("p (c n) -> p c n", n=CHUNK)
            v.tensor_tensor(rows[32:36, 0:SEQ].rearrange("p (c n) -> p c n", n=CHUNK),
                            g4[:, :, CHUNK - 1:CHUNK].to_broadcast([4, SEQ // CHUNK, CHUNK]), g4, ALU.subtract
                            ).then_inc(step, 1)
            dve.sem_inc(scaled, 2)
            dve.sem_inc(logged, 2)
            dve.sem_inc(summed, 2)
            for first, factor in ((T_Q, P ** -0.5), (T_K, 1.0)):
                def square(t, odd):
                    dve.wait_ge(summed, t + (first + 1))
                    nc.vector.tensor_tensor(sq[:, odd], c.proj[:, t + first, :], c.proj[:, t + first, :], ALU.mult
                                            ).then_inc(squared, 1)

                def scale(t, odd):
                    reach(c, dve, factored, t + (first + 3))
                    nc.vector.scalar_tensor_tensor(out=c.proj[:, t + first, :], in0=c.proj[:, t + first, :],
                                                   scalar=factor, in1=r[:, odd], op0=ALU.mult, op1=ALU.mult
                                                   ).then_inc(scaled, 1)
                with dve.Fori(0, 2, 1) as pair:
                    t = pair * 2
                    square(t, 0)
                    square(t + 1, 1)
                    scale(t, 0)
                    scale(t + 1, 1)



LEVELS = 6
BIG = -1e30


def build_level_masks(c, area):
    nc = c.nc
    made = c.sem(f"{area.name}_masks_made")
    m = c.delta_masks = area("level_masks", [P, LEVELS, P])
    m0 = c.delta_mask0 = area("level0_mask", [P, P])
    neg = c.delta_neg = area("causal", [P, P])
    sel = c.select = area("select", [8, 8, P])
    n = [0]
    with nc.Block() as block:
        @block.gpsimd
        def _(pool):
            g = nc.gpsimd

            def do(ins):
                ins.then_inc(made, 1)
                n[0] += 1
                pool.wait_ge(made, n[0])

            do(g.memset(m[:], 0.0))
            do(g.memset(m0[:], 0.0))
            do(g.memset(neg[:], 0.0))
            do(g.memset(sel[:], 0.0))
            do(g.affine_select(out=m[:, 0].rearrange("p (b s) -> p b s", s=2)[:, :, 1],
                               in_=m[:, 0].rearrange("p (b s) -> p b s", s=2)[:, :, 1],
                               compare_op=ALU.not_equal, fill=-1.0, base=0, pattern=[[-2, P // 2]], channel_multiplier=1))
            do(g.affine_select(out=m0[:].rearrange("p (b s) -> p b s", s=2)[:, :, 0],
                               in_=m0[:].rearrange("p (b s) -> p b s", s=2)[:, :, 0],
                               compare_op=ALU.not_equal, fill=-1.0, base=-1, pattern=[[-2, P // 2]], channel_multiplier=1))
            for level in range(1, LEVELS):
                s = 2 ** level
                late = m[:, level].rearrange("p (b s) -> p b s", s=2 * s)[:, :, s:2 * s]
                do(g.memset(late, 1.0))
                do(g.affine_select(out=late, in_=late, compare_op=ALU.is_ge, fill=0.0, base=0,
                                   pattern=[[-2 * s, P // (2 * s)], [0, s]], channel_multiplier=1))
                do(g.affine_select(out=late, in_=late, compare_op=ALU.is_ge, fill=0.0, base=s - 1,
                                   pattern=[[2 * s, P // (2 * s)], [0, s]], channel_multiplier=-1))
            do(g.affine_select(out=neg[:], in_=neg[:], compare_op=ALU.is_ge, fill=BIG, base=0, pattern=[[1, P]],
                               channel_multiplier=-1))
            do(g.affine_select(out=neg[:, CHUNK:P], in_=neg[:, CHUNK:P], compare_op=ALU.is_ge, fill=BIG, base=-CHUNK,
                               pattern=[[0, CHUNK]], channel_multiplier=1))
            do(g.affine_select(out=sel[:], in_=sel[:], compare_op=ALU.not_equal, fill=1.0, base=0,
                               pattern=[[-1, 8], [0, P]], channel_multiplier=1))


def heads(ap):
    return ap.rearrange("p (h n) -> p h n", h=HEADS)


def delta_phase(c, area):
    nc = c.nc
    H = HEADS
    rows, neg, sel = c.delta_rows, c.delta_neg, c.select

    def buf(name):
        return area(name, [P, H, P])
    kts, vts, dec, kbt, mt, tn, tt, xs, tmp = (buf(n) for n in (
        "k_cols", "v_cols", "decay", "kb_cols", "m_t", "inv", "inv_t", "x", "inv_tmp"))
    egb, bb, qeg, att, kbe, kdc, vb, nw, vnw = (buf(n) for n in (
        "decay_cols", "beta_cols", "q_decayed", "attention", "k_beta_decay", "k_left", "v_beta", "minus_w", "v_new"))
    ms = area("m_level", [P, 2, H, P])
    state = c.delta_state = buf("state")
    rs = area("rows_block", [36, P])
    cols, ecols, beg = area("cols", [P, 36]), area("exp_cols", [P, 36]), area("beta_decay", [P, 4])
    s = lambda n: c.sem("delta_" + n)
    names = ("k_staged v_staged rows_staged spread kn vn kk qk mn xm ym wt vm om dm cols egb bb dec x_copied nw o_out "
             "beg diff kbt qeg k_used vb mt att inv state v_copied ms").split()
    (k_staged, v_staged, rows_staged, spread, kn, vn, kk, qk, mn, xm, ym, wt, vm, om, dm, colsd, egbd, bbd, decd,
     x_copied, nwd, o_out, begd, diff, kbtd, qegd, k_used, vbd, mtd, attd, inv, stated, v_copied, msd) = map(s, names)
    stored, tmpd = c.sem("delta_stored"), c.sem("delta_inv_tmp")
    B = [heads(c.ps[:, n, :]) for n in range(8)]
    L = LEVELS - 1
    INV = 1 + 2 * (L + 1)
    eye = c.ident[:].unsqueeze(1).to_broadcast([P, H, P])

    def mask(ap):
        return ap.unsqueeze(1).to_broadcast([P, H, P])

    def col(ap):
        return ap.unsqueeze(2).to_broadcast([P, H, P])

    def block_start(eng, b):
        eng.wait_ge(stated, b * 8 + 1)
        eng.wait_ge(o_out, b * 2 + 1)

    with nc.Block() as block:
        @block.gpsimd
        def _(pool):
            g = nc.gpsimd
            with pool.Fori(0, NB, 1) as b:
                tok = bass.ds(b * P, P)
                block_start(pool, b)
                pool.sem_inc(c.passed[pool.engine], 1)
                g.tensor_copy(kts[:], c.proj[:, T_K:T_K + H, tok]).then_inc(k_staged, 1)
                g.tensor_copy(vts[:], c.proj[:, T_V:T_V + H, tok]).then_inc(v_staged, 1)
                pool.wait_ge(mtd, b + 1)
                for level in range(1, LEVELS):
                    if level > 2:
                        pool.wait_ge(xm, b * L + (level - 2))
                    g.tensor_tensor(ms[:, level % 2], mt[:], mask(c.delta_masks[:, level]), ALU.mult).then_inc(msd, 1)

        @block.tensor
        def _(pe):
            t = nc.tensor
            with pe.Fori(0, NB, 1) as b:
                tok = bass.ds(b * P, P)
                block_start(pe, b)
                reach(c, pe, rows_staged, b + 1)
                t.transpose(c.ps[:, 0, 0:36], rs[:], c.ident[0:36, 0:36]).then_inc(spread, 1)
                for first, bank in ((0, 1), (H, 2)):
                    for h in range(H):
                        last = t.matmul(B[bank][:, h], sel[:, first + h], rows[0:8, tok], start=True, stop=True)
                    last.then_inc(spread, 1)
                pe.wait_ge(k_staged, b + 1)
                for h in range(H):
                    last = t.transpose(B[5][:, h], kts[:, h], c.ident[:])
                last.then_inc(kn, 1)
                pe.wait_ge(v_staged, b + 1)
                for h in range(H):
                    last = t.transpose(B[6][:, h], vts[:, h], c.ident[:])
                last.then_inc(vn, 1)
                for h in range(H):
                    last = t.matmul(B[4][:, h], kts[:, h], c.proj[:, T_Q + h, tok], start=True, stop=True)
                last.then_inc(qk, 1)
                pe.wait_ge(kbtd, b + 1)
                for h in range(H):
                    last = t.matmul(B[3][:, h], kts[:, h], kbt[:, h], start=True, stop=True)
                last.then_inc(kk, 1)
                pe.wait_ge(mtd, b + 1)
                pe.wait_ge(k_used, b * 2 + 2)
                for h in range(H):
                    last = t.transpose(B[5][:, h], mt[:, h], c.ident[:])
                last.then_inc(mn, 1)
                for level in range(1, LEVELS):
                    pe.wait_ge(msd, b * L + level)
                    pe.wait_ge(inv, b * INV + (1 + 2 * level))
                    for h in range(H):
                        last = t.matmul(B[5][:, h], ms[:, level % 2, h], tn[:, h], start=True, stop=True)
                    last.then_inc(xm, 1)
                    pe.wait_ge(x_copied, b * L + level)
                    if level == 1:
                        pe.wait_ge(vbd, b + 1)
                    for h in range(H):
                        t.matmul(B[6][:, h], tt[:, h], xs[:, h], start=True, stop=True)
                    for h in range(H):
                        last = t.matmul(B[7][:, h], xs[:, h], tt[:, h], start=True, stop=True)
                    last.then_inc(ym, 1)
                pe.wait_ge(inv, b * INV + INV)
                for h in range(H):
                    last = t.matmul(B[7][:, h], kbe[:, h], tt[:, h], start=True, stop=True)
                last.then_inc(wt, 1)
                for a in range(2):
                    part = slice(a * CHUNK, (a + 1) * CHUNK)
                    if a:
                        reach(c, pe, stated, b * 8 + 5)
                    else:
                        reach(c, pe, nwd, b + 1)
                    for h in range(H):
                        t.matmul(B[6][part, h], tt[part, h, part], vb[part, h], start=True, stop=False)
                        last = t.matmul(B[6][part, h], nw[:, h, part], state[:, h], start=False, stop=True)
                    last.then_inc(vm, 1)
                    pe.wait_ge(v_copied, b * 2 + (a + 1))
                    if a == 0:
                        pe.wait_ge(attd, b + 1)
                        pe.wait_ge(qegd, b + 1)
                    if a:
                        pe.wait_ge(o_out, b * 2 + 2)
                    for h in range(H):
                        t.matmul(B[7][:, h, 0:CHUNK], state[:, h], qeg[:, h, part], start=True, stop=False)
                        last = t.matmul(B[7][:, h, 0:CHUNK], vnw[part, h], att[part, h, part], start=False, stop=True)
                    last.then_inc(om, 1)
                    for h in range(H):
                        last = t.matmul(B[5][:, h], kdc[part, h], vnw[part, h], start=True, stop=True)
                    last.then_inc(dm, 1)

        @block.scalar
        def _(act):
            def a(*args, **kw):
                return nc.scalar.activation(*args, **kw)
            act.sem_inc(o_out, 1)
            with act.Fori(0, NB, 1) as b:
                block_start(act, b)
                act.wait_ge(spread, b * 3 + 1)
                a(cols[:], c.ps[:, 0, 0:36], ACT.Copy).then_inc(colsd, 1)
                a(ecols[:], c.ps[:, 0, 0:36], ACT.Exp).then_inc(colsd, 1)
                act.wait_ge(spread, b * 3 + 2)
                a(egb[:], B[1], ACT.Exp).then_inc(egbd, 1)
                act.wait_ge(spread, b * 3 + 3)
                a(bb[:], B[2], ACT.Exp).then_inc(bbd, 1)
                act.wait_ge(diff, b * H + H)
                a(dec[:], dec[:], ACT.Exp).then_inc(decd, 1)
                for level in range(1, LEVELS):
                    act.wait_ge(xm, b * L + level)
                    act.wait_ge(ym, b * L + (level - 1)) if level > 1 else None
                    a(xs[:], B[5], ACT.Copy).then_inc(x_copied, 1)
                act.wait_ge(wt, b + 1)
                a(nw[:], B[7], ACT.Copy, scale=-1.0).then_inc(nwd, 1)
                for n in range(2):
                    reach(c, act, om, b * 2 + (n + 1))
                    a(c.proj[:, T_Q:T_Q + H, bass.ds(b * P + n * CHUNK, CHUNK)], B[7][:, :, 0:CHUNK], ACT.Copy
                      ).then_inc(o_out, 1)

        @block.vector
        def _(dve):
            v = nc.vector
            v.memset(state[:], 0.0).then_inc(stated, 1)
            with dve.Fori(0, NB, 1) as b:
                tok = bass.ds(b * P, P)
                block_start(dve, b)
                dve.sem_inc(c.passed[dve.engine], 1)
                v.tensor_copy(rs[:], rows[:, tok]).then_inc(rows_staged, 1)
                dve.wait_ge(colsd, b * 2 + 2)
                v.tensor_tensor(beg[:], ecols[:, 0:H], ecols[:, H:2 * H], ALU.mult).then_inc(begd, 1)
                dve.wait_ge(egbd, b + 1)
                for h in range(H):
                    v.scalar_tensor_tensor(out=dec[:, h], in0=B[1][:, h], scalar=cols[:, h:h + 1], in1=neg[:],
                                           op0=ALU.subtract, op1=ALU.add).then_inc(diff, 1)
                dve.wait_ge(bbd, b + 1)
                dve.wait_ge(k_staged, b + 1)
                v.tensor_tensor(kbt[:], kts[:], bb[:], ALU.mult).then_inc(kbtd, 1)
                v.tensor_tensor(qeg[:], c.proj[:, T_Q:T_Q + H, tok], egb[:], ALU.mult).then_inc(qegd, 1)
                dve.wait_ge(kn, b + 1)
                dve.wait_ge(begd, b + 1)
                v.tensor_tensor(kbe[:], B[5], col(beg[:]), ALU.mult).then_inc(k_used, 1)
                v.tensor_tensor(kdc[:], B[5], col(ecols[:, 32:36]), ALU.mult).then_inc(k_used, 1)
                dve.wait_ge(vn, b + 1)
                v.tensor_tensor(vb[:], B[6], col(ecols[:, H:2 * H]), ALU.mult).then_inc(vbd, 1)
                dve.wait_ge(decd, b + 1)
                dve.wait_ge(kk, b + 1)
                v.tensor_tensor(mt[:], B[3], dec[:], ALU.mult).then_inc(mtd, 1)
                dve.wait_ge(qk, b + 1)
                v.tensor_tensor(att[:], B[4], dec[:], ALU.mult).then_inc(attd, 1)
                dve.wait_ge(mn, b + 1)
                v.tensor_tensor(tmp[:], B[5], mask(c.delta_mask0[:]), ALU.mult).then_inc(inv, 1)
                dve.wait_ge(inv, b * INV + 1)
                v.tensor_tensor(tn[:], tmp[:], eye, ALU.add).then_inc(inv, 1)
                dve.wait_ge(mtd, b + 1)
                dve.wait_ge(inv, b * INV + 2)
                v.tensor_tensor(tmp[:], mt[:], mask(c.delta_masks[:, 0]), ALU.mult).then_inc(tmpd, 1)
                dve.wait_ge(tmpd, b + 1)
                v.tensor_tensor(tt[:], tmp[:], eye, ALU.add).then_inc(inv, 1)
                for level in range(1, LEVELS):
                    dve.wait_ge(ym, b * L + level)
                    v.tensor_tensor(tn[:], tn[:], B[6], ALU.subtract).then_inc(inv, 1)
                    v.tensor_tensor(tt[:], tt[:], B[7], ALU.subtract).then_inc(inv, 1)
                for n in range(2):
                    part = slice(n * CHUNK, (n + 1) * CHUNK)
                    dve.wait_ge(vm, b * 2 + (n + 1))
                    v.tensor_copy(vnw[part], B[6][part]).then_inc(v_copied, 1)
                    dve.wait_ge(dm, b * 2 + (n + 1))
                    for h in range(H):
                        v.scalar_tensor_tensor(out=state[:, h], in0=state[:, h],
                                               scalar=egb[:, h, n * CHUNK + CHUNK - 1:n * CHUNK + CHUNK], in1=B[5][:, h],
                                               op0=ALU.mult, op1=ALU.add).then_inc(stated, 1)

        @block.sync
        def _(sp):
            sp.wait_ge(stated, 1 + 8 * NB)
            sp.dma_start(c.outs["p_state_dn"].rearrange("e b h k v -> k (e b h) v"), state[:]).then_inc(stored, 16)
            sp.wait_ge(stored, 16)


class Steps:

    def __init__(self, sem):
        self.sem, self.n = sem, 0

    def __call__(self, ins):
        ins.then_inc(self.sem, 1)
        self.n += 1
        return self.n



def delta_sample_phase(c, area):
    nc = c.nc
    H, U = HEADS, DEC * HEADS
    states = area("sample_states", [P, U, P])
    ee, dots = area("sample_gates", [P, 8, DEC]), area("qk_dots", [P, H, DEC])
    both = area("state_products", [P, DEC, H, 2])
    prod, tmp, vnew = area("qk_products", [P, H, DEC]), area("sample_tmp", [P, H, DEC]), area("sample_v_new", [P, H, DEC])
    diag = area("v_diagonals", [P, 2, H, P])
    s = lambda n: c.sem("ds_" + n)
    loaded, spread, expd, prodd, dotted, mult, taken = map(s, "loaded spread exp prod dotted multiplied taken".split())
    made, decayed, diagd, wide, new = map(s, "v_made decayed diag wide new".split())
    stored, tails_in, tail_rows, tail_out = c.sem("ds_stored"), c.sem("tails_kept"), c.sem("tail_rows"), c.sem("tail_stored")
    tailr = area("tail_rows", [CONV - 1 + DEC, 12, P])
    q = c.proj[:, T_Q:T_Q + H, SEQ:TOK]
    k = c.proj[:, T_K:T_K + H, SEQ:TOK]
    vv = c.proj[:, T_V:T_V + H, SEQ:TOK]
    eg, beta = ee[:, 0:H], ee[:, H:2 * H]
    by_head = both[:].rearrange("p b h n -> p n h b")
    with nc.Block() as block:
        @block.sync
        def _(sp):
            sp.dma_start(states[:], c.ins["state_dn"].rearrange("e b h k v -> k (e b h) v")).then_inc(loaded, 16)
            old = c.ins["state_dn_conv"].rearrange("e b i c -> (e b) i c")
            conv_out = c.outs["s_state_dn_conv"].rearrange("e b i c -> (e b) i c")
            sp.dma_start(conv_out[:, 0:CONV - 2, :], old[:, 1:CONV - 1, :]).then_inc(tail_out, 16)
            sp.wait_ge(tail_rows, 3 + 3)
            sp.dma_start(c.outs["p_state_dn_conv"].rearrange("e b i c -> (e b i) c"),
                         tailr[0:CONV - 1].rearrange("p t n -> p (t n)")).then_inc(tail_out, 16)
            sp.dma_start(conv_out[:, CONV - 2, :], tailr[CONV - 1:].rearrange("p t n -> p (t n)")
                         ).then_inc(tail_out, 16)
            with sp.Fori(0, DEC, 1) as b:
                sp.wait_ge(new, b * H + H)
                sp.dma_start(c.outs["s_state_dn"].rearrange("e b h k v -> k (e b) h v")[:, bass.ds(b, 1)]
                             .rearrange("k b h v -> k (b h) v"), states[:, bass.ds(b * H, H), :]).then_inc(stored, 16)
            sp.wait_ge(stored, 16 * DEC)
            sp.wait_ge(tail_out, 48)

        @block.tensor
        def _(pe):
            t = nc.tensor
            for r in range(8):
                last = t.matmul(c.ps[:, 0, r * DEC:(r + 1) * DEC], c.select[:, r], c.delta_rows[0:8, SEQ:TOK],
                                start=True, stop=True)
            last.then_inc(spread, 1)
            pe.wait_ge(prodd, 1)
            t.matmul(c.ps[:, 1, 0:U], c.ones[:], prod[:], start=True, stop=True).then_inc(dotted, 1)
            for g3 in range(3):
                for n in range(4):
                    last = t.transpose(c.ps[0:CONV - 1 + DEC, 2 + g3, n * P:(n + 1) * P], c.tail[:, 4 * g3 + n, :],
                                       c.ident[:])
                last.then_inc(tail_rows, 1)
            pe.wait_ge(loaded, 16)
            for b in range(DEC):
                for h in range(H):
                    u = b * H + h
                    last = t.matmul(c.ps[:, 5, 2 * u:2 * u + 2], states[:, u],
                                    c.proj[:, T_Q + h:T_K + h + 1:T_K - T_Q, SEQ + b], start=True, stop=True)
            last.then_inc(mult, 1)
            for b in range(DEC):
                pe.wait_ge(diagd, b + 1)
                if b >= 2:
                    pe.wait_ge(new, H * (b - 1))
                t.matmul(c.ps[:, 6 + b % 2, :], c.ones[:], diag[:, b % 2], start=True, stop=True).then_inc(wide, 1)

        @block.scalar
        def _(act):
            act.wait_ge(spread, 1)
            nc.scalar.activation(ee[:], c.ps[:, 0, 0:64], ACT.Exp).then_inc(expd, 1)
            act.wait_ge(tail_rows, 3)
            for g3 in range(3):
                nc.scalar.activation(tailr[:, 4 * g3:4 * g3 + 4], c.ps[0:CONV - 1 + DEC, 2 + g3, :], ACT.Copy
                                     ).then_inc(tail_rows, 1)
            act.wait_ge(expd, 1)
            act.wait_ge(mult, 1)
            for b in range(DEC):
                for h in range(H):
                    u = b * H + h
                    nc.scalar.activation(states[:, u], states[:, u], ACT.Copy, scale=eg[:, h, b:b + 1]
                                         ).then_inc(decayed, 1)

        @block.vector
        def _(dve):
            v = nc.vector
            own = Steps(c.sem("ds_steps"))
            v.tensor_tensor(prod[:], q, k, ALU.mult).then_inc(prodd, 1)
            dve.wait_ge(dotted, 1)
            own(v.tensor_copy(dots[:], c.ps[:, 1, 0:U]))
            dve.wait_ge(mult, 1)
            n = own(v.tensor_copy(both[:], c.ps[:, 5, 0:2 * U]))
            dve.wait_ge(expd, 1)
            dve.wait_ge(own.sem, n)
            n = own(v.tensor_tensor(tmp[:], by_head[:, 1], eg, ALU.mult))
            dve.wait_ge(own.sem, n)
            n = own(v.tensor_tensor(vnew[:], vv, tmp[:], ALU.subtract))
            dve.wait_ge(own.sem, n)
            n = own(v.tensor_tensor(vnew[:], vnew[:], beta, ALU.mult))
            m = own(v.tensor_tensor(tmp[:], by_head[:, 0], eg, ALU.mult))
            dve.wait_ge(own.sem, m)
            n = own(v.tensor_tensor(prod[:], vnew[:], dots[:], ALU.mult))
            dve.wait_ge(own.sem, n)
            own(v.tensor_tensor(q, tmp[:], prod[:], ALU.add))

            def update(b):
                dve.wait_ge(wide, b + 1)
                dve.wait_ge(decayed, (b + 1) * H)
                for h in range(H):
                    v.scalar_tensor_tensor(out=states[:, b * H + h], in0=c.ps[:, 6 + b % 2, h * P:(h + 1) * P],
                                           scalar=k[:, h, b:b + 1], in1=states[:, b * H + h], op0=ALU.mult,
                                           op1=ALU.add).then_inc(new, 1)
            for b in range(DEC):
                if b >= 2:
                    dve.wait_ge(wide, b - 1)
                v.tensor_tensor(diag[:, b % 2], c.ident[:].unsqueeze(1).to_broadcast([P, H, P]),
                                vnew[:, :, b:b + 1].to_broadcast([P, H, P]), ALU.mult).then_inc(diagd, 1)
                if b >= 1:
                    update(b - 1)
            update(DEC - 1)



W2 = 2 * P
BY_HALF = [2 * i + r for r in range(2) for i in range(SWH // 2)]


def window_masks_phase(c, area):
    nc = c.nc
    bias = c.window_bias = area("bias", [P, SWH, W2])
    ksw = c.k_swapped = area("k_swapped", [P, TOK])
    sinks = c.sinks = area("sinks", [P, SWH])
    rel, forbid = area.passing("window_masks")("distance", [P, W2]), None
    brief = area.passing("window_masks2")
    brief("pad", [P, W2])
    forbid = brief("forbidden", [P, W2])
    sinks_in = brief("sinks_in", [P, SWH])
    made, biased, swapped, loaded = c.sem("wm_made"), c.sem("wm_biased"), c.sem("k_swapped"), c.sem("sinks_in")
    with nc.Block() as block:
        @block.sync
        def _(sp):
            sp.dma_start(sinks_in[:], c.ins["sw_sinks"].rearrange("e h -> (e h)").partition_broadcast(P)
                         ).then_inc(loaded, 16)
            sp.wait_ge(loaded, 16)

        @block.gpsimd
        def _(pool):
            g = nc.gpsimd
            g.iota(rel[:], pattern=[[-1, W2]], base=P, channel_multiplier=1, allow_small_or_imprecise_dtypes=True
                   ).then_inc(made, 1)
            g.memset(forbid[:], 0.0).then_inc(made, 1)
            pool.wait_ge(made, 2)
            g.affine_select(out=forbid[:], in_=forbid[:], compare_op=ALU.is_ge, fill=BIG, base=P, pattern=[[-1, W2]],
                            channel_multiplier=1).then_inc(made, 1)
            pool.wait_ge(made, 3)
            g.affine_select(out=forbid[:], in_=forbid[:], compare_op=ALU.is_gt, fill=BIG, base=0, pattern=[[1, W2]],
                            channel_multiplier=-1).then_inc(made, 1)

        @block.vector
        def _(dve):
            dve.wait_ge(made, 4)
            for n, h in enumerate(BY_HALF):
                nc.vector.scalar_tensor_tensor(out=bias[:, n], in0=rel[:], scalar=-2.0 ** -(h + 1), in1=forbid[:],
                                               op0=ALU.mult, op1=ALU.add).then_inc(biased, 1)
            dve.wait_ge(loaded, 16)
            nc.vector.tensor_copy(sinks[:].rearrange("p (r i) -> p r i", r=2),
                                  sinks_in[:].rearrange("p (i r) -> p r i", r=2)).then_inc(biased, 1)

        @block.scalar
        def _(act):
            for a in range(2):
                nc.scalar.activation(ksw[a * HD:(a + 1) * HD, :], c.proj[(1 - a) * HD:(2 - a) * HD, T_SK, :], ACT.Copy
                                     ).then_inc(swapped, 1)


def window_phase(c, area):
    nc = c.nc
    bias, ksw, sinks = c.window_bias, c.k_swapped, c.sinks
    qs, ks = area("q_block", [P, 4, P]), area("k_block", [P, 2, W2])
    vs, vn = area("v_block", [P, P]), area("v_rows", [P, 2, P])
    sc, pt = area("scores", [P, SWH, W2]), area("probs_cols", [P, SWH, 2, P])
    mx, nm, sums, es, rd = (area(n, [P, SWH]) for n in ("max", "minus_max", "sums", "sink_exp", "rden"))
    kr = area("k_rows", [P, P])
    s = lambda n: c.sem("w_" + n)
    staged, vt, scored, biased, stat, expd, turned, ptd, od, odone, vrow = map(s, (
        "staged v_turned scored biased stats exp turned probs_out o o_out v_row").split())
    stored = s("stored")
    k_turned, k_out = s("k_turned"), s("k_out")
    PB, ST = 2, 6
    base_key = {False: 0, True: P}

    with nc.Block() as block:
        def each(eng, body):
            body(0, True)
            with eng.Fori(1, NB, 1) as b:
                body(b, False)

        @block.gpsimd
        def _(pool):
            g = nc.gpsimd

            def body(b, first):
                n = P if first else W2
                lo = W2 - n
                keys = slice(0, P) if first else bass.ds((b - 1) * P, W2)
                tok = slice(0, P) if first else bass.ds(b * P, P)
                if not first:
                    reach(c, pool, odone, b * 1)
                    reach(c, pool, scored, b * 4)
                g.tensor_copy(qs[:], c.proj[:, T_SQ:T_SQ + 4, tok]).then_inc(staged, 1)
                g.tensor_copy(ks[:, 0, lo:], c.proj[:, T_SK, keys]).then_inc(staged, 1)
                g.tensor_copy(ks[:, 1, lo:], ksw[:, keys]).then_inc(staged, 1)
                g.tensor_copy(vs[:], c.proj[:, T_SV, tok]).then_inc(staged, 1)
            each(pool, body)

        @block.tensor
        def _(pe):
            t = nc.tensor

            def body(b, first):
                n = P if first else W2
                lo = W2 - n
                pe.wait_ge(staged, b * 4 + 4)
                if not first:
                    pe.wait_ge(biased, b * 4)
                    pe.wait_ge(vrow, b * 1)
                    pe.wait_ge(odone, b * 1)
                for i, h in enumerate(BY_HALF):
                    p0, kv = HD * (h % 2), h // 4
                    rows = slice(p0, p0 + HD)
                    last = t.matmul(c.ps[:, i // 2, (i % 2) * W2 + lo:(i % 2) * W2 + W2], qs[rows, h // 2],
                                    ks[rows, int(kv != h % 2), lo:], start=True, stop=True)
                    if i % 2:
                        last.then_inc(scored, 1)
                t.transpose(c.ps[:, 4, 0:P], vs[:], c.ident[:]).then_inc(vt, 1)
                for h in range(SWH):
                    if h % 2 == 0:
                        pe.wait_ge(stat, b * ST + ST)
                        if h >= 4:
                            pe.wait_ge(ptd, b * 4 + (h // 2 - 1))
                        elif not first:
                            pe.wait_ge(ptd, b * 4)
                    for a in range(1 if first else 0, 2):
                        last = t.transpose(c.ps[:, 5 + (h // 2) % 2, (2 * (h % 2) + a) * P:(2 * (h % 2) + a + 1) * P],
                                           sc[:, h, a * P:(a + 1) * P], c.ident[:])
                    if h % 2:
                        last.then_inc(turned, 1)
                pe.wait_ge(ptd, b * 4 + 4)
                pe.wait_ge(vrow, b * 1 + 1)
                for i, h in enumerate(BY_HALF):
                    p0, kv = HD * (h % 2), h // 4
                    for a in range(1 if first else 0, 2):
                        last = t.matmul(c.ps[p0:p0 + HD, 7, (h // 2) * P:(h // 2 + 1) * P],
                                        vn[:, a, kv * HD:(kv + 1) * HD], pt[:, i, a],
                                        start=first or a == 0, stop=a == 1)
                last.then_inc(od, 1)
            each(pe, body)
            t.transpose(c.ps[:, 4, P:2 * P], ks[:, 0, P:W2], c.ident[:]).then_inc(k_turned, 1)

        @block.scalar
        def _(act):
            def body(b, first):
                n = P if first else W2
                lo = W2 - n
                act.wait_ge(stat, b * ST + 3)
                for h in range(SWH):
                    nc.scalar.activation(sc[:, h, lo:], sc[:, h, lo:], ACT.Exp, bias=nm[:, h:h + 1],
                                         accum_out=sums[:, h:h + 1]).then_inc(expd, 1)
                nc.scalar.activation(es[:], es[:], ACT.Exp).then_inc(expd, 1)
                for j in range(4):
                    act.wait_ge(turned, b * 4 + (j + 1))
                    a = 1 if first else 0
                    nc.scalar.activation(pt[:, 2 * j:2 * j + 2, a:],
                                         c.ps[:, 5 + j % 2, :].rearrange("p (h a n) -> p h a n", h=2, a=2)[:, :, a:],
                                         ACT.Copy).then_inc(ptd, 1)
                reach(c, act, od, b * 1 + 1)
                nc.scalar.activation(c.proj[:, T_SQ:T_SQ + 4, slice(0, P) if first else bass.ds(b * P, P)],
                                     c.ps[:, 7, :].rearrange("p (t n) -> p t n", t=4), ACT.Copy).then_inc(odone, 1)
            each(act, body)

        @block.vector
        def _(dve):
            v = nc.vector
            v.memset(vn[:], 0.0).then_inc(c.sem("w_init"), 1)
            dve.wait_ge(c.sem("w_init"), 1)

            def body(b, first):
                n = P if first else W2
                lo = W2 - n
                if not first:
                    dve.wait_ge(odone, b * 1)
                    v.tensor_copy(vn[:, 0], vn[:, 1]).then_inc(vshift, 1)
                for j in range(4):
                    dve.wait_ge(scored, b * 4 + (j + 1))
                    v.scalar_tensor_tensor(out=sc[:, 2 * j:2 * j + 2, lo:],
                                           in0=c.ps[:, j, :].rearrange("p (h n) -> p h n", h=2)[:, :, lo:],
                                           scalar=HD ** -0.5, in1=bias[:, 2 * j:2 * j + 2, lo:], op0=ALU.mult,
                                           op1=ALU.add).then_inc(biased, 1)
                dve.wait_ge(vt, b * 1 + 1)
                if not first:
                    dve.wait_ge(vshift, b * 1)
                v.tensor_copy(vn[:, 1], c.ps[:, 4, 0:P]).then_inc(vrow, 1)
                dve.wait_ge(biased, b * 4 + 4)
                v.tensor_reduce(mx[:], sc[:, :, lo:], AX.X, ALU.max).then_inc(stat, 1)
                dve.wait_ge(stat, b * ST + 1)
                v.tensor_tensor(mx[:], mx[:], sinks[:], ALU.max).then_inc(stat, 1)
                dve.wait_ge(stat, b * ST + 2)
                v.tensor_scalar(nm[:], mx[:], -1.0, None, ALU.mult).then_inc(nmd, 1)
                v.tensor_tensor(es[:], sinks[:], mx[:], ALU.subtract).then_inc(stat, 1)
                dve.wait_ge(expd, b * 9 + 9)
                v.tensor_tensor(sums[:], sums[:], es[:], ALU.add).then_inc(stat, 1)
                dve.wait_ge(stat, b * ST + 4)
                v.reciprocal(rd[:], sums[:]).then_inc(stat, 1)
                dve.wait_ge(stat, b * ST + 5)
                v.tensor_tensor(sc[:, :, lo:], sc[:, :, lo:], rd[:].unsqueeze(2).to_broadcast([P, SWH, n]), ALU.mult
                                ).then_inc(stat, 1)
            vshift, nmd = c.sem("w_v_shift"), c.sem("w_minus_max")
            each(dve, body)
            dve.wait_ge(k_turned, 1)
            v.tensor_copy(kr[:], c.ps[:, 4, P:2 * P]).then_inc(k_out, 1)

        @block.sync
        def _(sp):
            sp.wait_ge(vrow, NB)
            sp.dma_start(c.outs["p_cache_swa_v"].rearrange("e b w g d -> (e b w) (g d)"), vn[:, 1]).then_inc(stored, 16)
            sp.wait_ge(k_out, 1)
            sp.dma_start(c.outs["p_cache_swa_k"].rearrange("e b w g d -> (e b w) (g d)"), kr[:]).then_inc(stored, 16)
            sp.wait_ge(stored, 32)



def window_sample_phase(c, area):
    nc = c.nc
    G, J, U = KVH, SWH // KVH, DEC * KVH
    kc, vc = area("k_cache", [P, DEC, P]), area("v_cache", [P, DEC, P])
    kt = area("k_cache_cols", [P, DEC, P])
    news = area("new_rows", [DEC, 2, P])
    qg = area("q_groups", [P, J, DEC])
    sc, rel = area("sample_scores", [J, U, P]), area("sample_distance", [J, P])
    slope, sk = area("slopes", [J, G]), area("sample_sinks", [J, G])
    bias = area("sample_bias", [J, G, P])
    mx, es, sums = area("sample_max", [J, U]), area("sample_sink_exp", [J, U]), area("sample_sums", [J, U])
    pt = area("sample_probs", [P, U, J])
    s = lambda n: c.sem("ws_" + n)
    loaded, made, new_t, new_out, placed, kturn, kcopied, qd = map(s, (
        "loaded made new_turned new_out placed k_turned k_copied q_grouped").split())
    scored, actd, pturn, ptd, od, stored = map(s, "scored exp p_turned p_out o stored".split())
    steps, biasd = s("steps"), s("bias")
    LAST = 10
    by_unit = lambda ap: ap.rearrange("p (g b) -> p g b", g=G)
    with nc.Block() as block:
        @block.sync
        def _(sp):
            by_group = c.ins["sw_sinks"].rearrange("e (g j a) -> (e g) j a", g=G, a=1)
            for grp in range(G):
                sp.dma_start(sk[:, grp:grp + 1], by_group[grp]).then_inc(loaded, 16)
            for cache, name in ((kc, "cache_swa_k"), (vc, "cache_swa_v")):
                sp.dma_start(cache[0:P - 1], c.ins[name].rearrange("e b w g d -> w (e b) (g d)")[1:P]
                             ).then_inc(loaded, 16)
            sp.wait_ge(new_out, 1)
            for n, cache in enumerate((kc, vc)):
                for b in range(DEC):
                    sp.dma_start(cache[P - 1:P, b, :], news[b:b + 1, n, :]).then_inc(placed, 16)
            sp.wait_ge(placed, 16 * 2 * DEC)
            sp.wait_ge(loaded, 64)
            for cache, name in ((kc, "s_cache_swa_k"), (vc, "s_cache_swa_v")):
                sp.dma_start(c.outs[name].rearrange("e b w g d -> w (e b) (g d)"), cache[:]).then_inc(stored, 16)
            sp.wait_ge(stored, 32)

        @block.gpsimd
        def _(pool):
            g = nc.gpsimd
            g.iota(rel[:], pattern=[[-1, P]], base=P - 1, channel_multiplier=0, allow_small_or_imprecise_dtypes=True
                   ).then_inc(made, 1)
            g.memset(slope[:], 0.0).then_inc(made, 1)
            n = 2
            for j in range(J):
                for grp in range(G):
                    pool.wait_ge(made, n)
                    g.affine_select(out=slope[:, grp:grp + 1], in_=slope[:, grp:grp + 1], compare_op=ALU.not_equal,
                                    fill=-2.0 ** -(J * grp + j + 1), base=-j, pattern=[[0, 1]], channel_multiplier=1
                                    ).then_inc(made, 1)
                    n += 1

        @block.tensor
        def _(pe):
            t = nc.tensor
            for n in range(2):
                last = t.transpose(c.ps[0:DEC, 0, n * P:(n + 1) * P], c.proj[:, T_SK + n, SEQ:TOK], c.ident[:])
            last.then_inc(new_t, 1)
            pe.wait_ge(placed, 16 * 2 * DEC)
            pe.wait_ge(loaded, 64)
            for b in range(DEC):
                last = t.transpose(c.ps[:, 1 + b // 4, (b % 4) * P:(b % 4 + 1) * P], kc[:, b], c.ident[:])
                if b % 4 == 3:
                    last.then_inc(kturn, 1)
            pe.wait_ge(kcopied, 2)
            pe.wait_ge(qd, 4)
            for grp in range(G):
                for b in range(DEC):
                    u = grp * DEC + b
                    rows = slice(grp * HD, (grp + 1) * HD)
                    last = t.matmul(c.ps[0:J, 3 + u // 4, (u % 4) * P:(u % 4 + 1) * P], qg[rows, :, b], kt[rows, b],
                                    start=True, stop=True)
            last.then_inc(scored, 1)
            pe.wait_ge(steps, LAST)
            for u in range(U):
                last = t.transpose(c.ps[:, 1, u * J:(u + 1) * J], sc[:, u], c.ident[0:J, 0:J])
            last.then_inc(pturn, 1)
            pe.wait_ge(ptd, 1)
            for b in range(DEC):
                for grp in range(G):
                    rows = slice(grp * HD, (grp + 1) * HD)
                    last = t.matmul(c.ps[rows, 2, b * J:(b + 1) * J], vc[:, b, rows], pt[:, grp * DEC + b], start=True,
                                    stop=True)
            last.then_inc(od, 1)

        @block.scalar
        def _(act):
            act.wait_ge(new_t, 1)
            nc.scalar.activation(news[:], c.ps[0:DEC, 0, 0:2 * P], ACT.Copy).then_inc(new_out, 1)
            for n in range(2):
                act.wait_ge(kturn, n + 1)
                nc.scalar.activation(kt[:, 4 * n:4 * n + 4], c.ps[:, 1 + n, :], ACT.Copy).then_inc(kcopied, 1)
            act.wait_ge(steps, 6)
            nc.scalar.activation(sc[:], sc[:], ACT.Exp).then_inc(actd, 1)
            nc.scalar.activation(es[:], es[:], ACT.Exp).then_inc(actd, 1)
            act.wait_ge(pturn, 1)
            nc.scalar.activation(pt[:], c.ps[:, 1, 0:U * J], ACT.Copy).then_inc(ptd, 1)

        @block.vector
        def _(dve):
            v = nc.vector
            own = Steps(steps)
            for grp in range(G):
                for r in range(2):
                    v.tensor_copy(qg[grp * HD:(grp + 1) * HD, r:J:2, :],
                                  c.proj[r * HD:(r + 1) * HD, T_SQ + 2 * grp:T_SQ + 2 * grp + 2, SEQ:TOK]
                                  ).then_inc(qd, 1)
            dve.wait_ge(made, 2 + J * G)
            for grp in range(G):
                v.tensor_scalar(bias[:, grp], rel[:], slope[:, grp:grp + 1], None, ALU.mult).then_inc(biasd, 1)
            dve.wait_ge(biasd, 2)
            dve.wait_ge(scored, 1)
            for grp in range(G):
                n = own(v.scalar_tensor_tensor(out=sc[:, grp * DEC:(grp + 1) * DEC, :],
                                               in0=c.ps[0:J, 3 + 2 * grp:5 + 2 * grp, :]
                                               .rearrange("p c (b n) -> p (c b) n", n=P),
                                               scalar=HD ** -0.5, in1=bias[:, grp].unsqueeze(1)
                                               .to_broadcast([J, DEC, P]), op0=ALU.mult, op1=ALU.add))
            dve.wait_ge(own.sem, n)
            n = own(v.tensor_reduce(mx[:], sc[:], AX.X, ALU.max))
            dve.wait_ge(own.sem, n)
            dve.wait_ge(loaded, 64)
            n = own(v.tensor_tensor(by_unit(mx[:]), by_unit(mx[:]), sk[:].unsqueeze(2).to_broadcast([J, G, DEC]),
                                    ALU.max))
            dve.wait_ge(own.sem, n)
            own(v.tensor_tensor(by_unit(es[:]), sk[:].unsqueeze(2).to_broadcast([J, G, DEC]), by_unit(mx[:]),
                                ALU.subtract))
            own(v.tensor_tensor(sc[:], sc[:], mx[:].unsqueeze(2).to_broadcast([J, U, P]), ALU.subtract))
            dve.wait_ge(actd, 2)
            n = own(v.tensor_reduce(sums[:], sc[:], AX.X, ALU.add))
            dve.wait_ge(own.sem, n)
            n = own(v.tensor_tensor(sums[:], sums[:], es[:], ALU.add))
            dve.wait_ge(own.sem, n)
            n = own(v.reciprocal(sums[:], sums[:]))
            dve.wait_ge(own.sem, n)
            n = own(v.tensor_tensor(sc[:], sc[:], sums[:].unsqueeze(2).to_broadcast([J, U, P]), ALU.mult))
            assert n == LAST
            dve.wait_ge(od, 1)
            for grp in range(G):
                for r in range(2):
                    own(v.tensor_copy(c.proj[r * HD:(r + 1) * HD, T_SQ + 2 * grp:T_SQ + 2 * grp + 2, SEQ:TOK],
                                      c.ps[grp * HD:(grp + 1) * HD, 2, 0:DEC * J]
                                      .rearrange("p (b j) -> p j b", j=J)[:, r:J:2, :]))





def finish_phase(c, name, o_first, z_first, halves, vcol, sq_first, factor_first, plain):
    nc = c.nc
    n = HEADS * halves
    s = lambda x: c.sem(f"{name}_{x}")
    silud, sqd, summed, logged, fact, normed, gated, upper, lower = map(s, (
        "silu squares summed logged factor normed gated upper lower").split())

    def square(h, j):
        return c.proj[:, sq_first + h, :] if j == 0 else c.tmp[:, h % 2]
    with nc.Block() as block:
        @block.scalar
        def _(act):
            for t in range(n):
                z = c.proj[:, z_first + t, :]
                nc.scalar.activation(z, z, ACT.Silu).then_inc(silud, 1)

            def split(t):
                act.wait_ge(gated, t + 1)
                nc.scalar.activation(c.act_hi[:, t, :], c.proj[:, o_first + t, :], ACT.Copy).then_inc(upper, 1)
            for h in range(HEADS):
                r = c.proj[:, factor_first + h, :]
                act.wait_ge(summed, h + 1)
                nc.scalar.activation(chunked(r), tile_psum(c, h % 2), ACT.Ln, bias=c.eps[:], scale=1.0 / (halves * P)
                                     ).then_inc(logged, 1)
                act.wait_ge(logged, h + 1)
                nc.scalar.activation(r, r, ACT.Exp, scale=-0.5).then_inc(fact, 1)
                if h:
                    for j in range(halves):
                        split((h - 1) * halves + j)
            for j in range(halves):
                split((HEADS - 1) * halves + j)
            for i, t in enumerate(plain):
                nc.scalar.activation(c.act_hi[:, n + i, :], c.proj[:, t, :], ACT.Copy).then_inc(upper, 1)

        @block.tensor
        def _(pe):
            for h in range(HEADS):
                pe.wait_ge(sqd, (h + 1) * halves)
                if h >= 2:
                    pe.wait_ge(logged, h - 1)
                for ch in range(NCH):
                    for j in range(halves):
                        last = nc.tensor.matmul(c.ps[:, 3 * (h % 2) + ch, 0:CW], c.ones[:],
                                                square(h, j)[:, ch * CW:(ch + 1) * CW], start=j == 0,
                                                stop=j == halves - 1)
                last.then_inc(summed, 1)

        @block.vector
        def _(dve):
            v = nc.vector

            def squares(h):
                for j in range(halves):
                    if j and h >= 2:
                        dve.wait_ge(summed, h - 1)
                    o = c.proj[:, o_first + h * halves + j, :]
                    v.tensor_tensor(square(h, j), o, o, ALU.mult).then_inc(sqd, 1)

            def low(t, src):
                dve.wait_ge(upper, t + 1)
                v.tensor_tensor(c.act_lo[:, t, :], c.proj[:, src, :], c.act_hi[:, t, :].bitcast(F32), ALU.subtract
                                ).then_inc(lower, 1)
            squares(0)
            squares(1)
            for h in range(HEADS):
                for j in range(halves):
                    t = h * halves + j
                    o = c.proj[:, o_first + t, :]
                    dve.wait_ge(fact, h + 1)
                    v.scalar_tensor_tensor(out=o, in0=o, scalar=c.vcols[:, vcol + j:vcol + j + 1],
                                           in1=c.proj[:, factor_first + h, :], op0=ALU.mult, op1=ALU.mult
                                           ).then_inc(normed, 1)
                    dve.wait_ge(silud, t + 1)
                    dve.wait_ge(normed, t + 1)
                    v.tensor_tensor(o, o, c.proj[:, z_first + t, :], ALU.mult).then_inc(gated, 1)
                if h + 2 < HEADS:
                    squares(h + 2)
                if h:
                    for j in range(halves):
                        low((h - 1) * halves + j, o_first + (h - 1) * halves + j)
            for j in range(halves):
                low((HEADS - 1) * halves + j, o_first + (HEADS - 1) * halves + j)
            for i, t in enumerate(plain):
                low(n + i, t)



def gla_prepare_phase(c, area):
    nc = c.nc
    H = HEADS
    logs = c.gla_logs = area("log_decay", [P, H, TOK])
    brief = area.passing("gla_prepare")
    wg = brief("gate_up", [RANK, H, P])
    y, t1 = brief("gate", [P, 2, TOK]), brief("gate_exp", [P, 2, TOK])
    mask = brief("chunk_mask", [P, TOK])
    s = lambda n: c.sem("gp_" + n)
    loaded, masked, proj, gated, low, expd, logd, summed, done = map(s, (
        "loaded masked projected gated low exp log summed done").split())
    with nc.Block() as block:
        @block.sync
        def _(sp):
            sp.dma_start(wg[:], c.ins["gla_w_gate_up"].rearrange("e r (h n) -> (e r) h n", h=H)).then_inc(loaded, 16)

        @block.gpsimd
        def _(pool):
            nc.gpsimd.memset(mask[:], 0.0).then_inc(masked, 1)
            pool.wait_ge(masked, 1)
            nc.gpsimd.memset(mask[:, 0:SEQ].rearrange("p (c n) -> p c n", n=CHUNK)[:, :, 1:CHUNK], 1.0
                             ).then_inc(masked, 1)

        @block.tensor
        def _(pe):
            pe.wait_ge(loaded, 16)
            for h in range(H):
                if h >= 2:
                    pe.wait_ge(gated, h - 1)
                for ch in range(NCH):
                    last = nc.tensor.matmul(c.ps[:, 3 * (h % 2) + ch, 0:CW], wg[:, h],
                                            c.proj[0:RANK, G_D, ch * CW:(ch + 1) * CW], start=True, stop=True)
                last.then_inc(proj, 1)

        @block.scalar
        def _(act):
            for h in range(H):
                e = t1[:, h % 2]
                act.wait_ge(low, h + 1)
                nc.scalar.activation(e, e, ACT.Exp).then_inc(expd, 1)
                act.wait_ge(expd, h + 1)
                nc.scalar.activation(e, e, ACT.Ln, bias=c.ones[:, 0:1]).then_inc(logd, 1)

        @block.vector
        def _(dve):
            v = nc.vector

            def start(h):
                yy, e = y[:, h % 2], t1[:, h % 2]
                dve.wait_ge(proj, h + 1)
                if h >= 2:
                    dve.wait_ge(done, h - 1)
                v.tensor_scalar(chunked(yy), tile_psum(c, h % 2), c.vcols[:, V_GB + h:V_GB + h + 1], None, ALU.add
                                ).then_inc(gated, 1)
                dve.wait_ge(gated, h + 1)
                v.scalar_tensor_tensor(out=e, in0=yy, scalar=-1.0, in1=yy, op0=ALU.mult, op1=ALU.min).then_inc(low, 1)
            start(0)
            dve.wait_ge(masked, 2)
            for h in range(H):
                yy, e = y[:, h % 2], t1[:, h % 2]
                if h + 1 < H:
                    start(h + 1)
                dve.wait_ge(logd, h + 1)
                v.scalar_tensor_tensor(out=yy, in0=yy, scalar=0.0, in1=e, op0=ALU.min, op1=ALU.subtract
                                       ).then_inc(summed, 1)
                dve.wait_ge(summed, h + 1)
                v.tensor_tensor_scan(logs[:, h], mask[:], yy, 0.0, ALU.mult, ALU.add).then_inc(done, 1)



def gla_phase(c, area):
    nc = c.nc
    H = HEADS
    logs, masks = c.gla_logs, c.delta_masks
    state = c.gla_state = area("state", [P, H, GDV])

    def buf(name):
        return area(name, [P, H, P])
    qs, ks, qeg, kd, kdn, att, eg = (buf(n) for n in ("q_cols", "k_cols", "q_decayed", "k_left", "k_left_rows",
                                                      "attention", "decay"))
    d, w = area("exponents", [P, 2, H, P]), area("level_factors", [P, 2, H, P])
    vs, vn = area("v_cols", [P, 2 * H, P]), area("v_rows", [P, 2 * H, P])
    s = lambda n: c.sem("gla_" + n)
    (staged, diffd, expd, factd, prodd, tailed, egd, kdd, kturn, vturn, kout, vout, attd, qegd, od, oout, dsd, stated
     ) = map(s, ("staged diff exp factors product left decay k_left k_turned v_turned k_out v_out attention "
                 "q_decayed o o_out ds state").split())
    stored = s("stored")
    SCALE = P ** -0.5
    NX = LEVELS + 1
    B = [c.ps[:, n, :] for n in range(8)]

    def block_start(eng, b):
        eng.wait_ge(stated, b * 8 + 1)
        eng.wait_ge(oout, b * 2 + 1)

    def halves(ap, level):
        v = ap.rearrange("p h (b s) -> p h b s", s=2 * 2 ** level)
        half = 2 ** level
        return v[:, :, :, 0:half], v[:, :, :, half:]

    with nc.Block() as block:
        @block.gpsimd
        def _(pool):
            g = nc.gpsimd
            with pool.Fori(0, NB, 1) as b:
                tok = bass.ds(b * P, P)
                block_start(pool, b)
                pool.sem_inc(c.passed[pool.engine], 1)
                g.tensor_copy(ks[:], c.proj[:, G_K:G_K + H, tok]).then_inc(staged, 1)
                g.tensor_copy(vs[:], c.proj[:, G_V:G_V + 2 * H, tok]).then_inc(staged, 1)
                lg = logs[:, :, tok]
                for level in range(LEVELS):
                    if level >= 2:
                        reach(c, pool, factd, b * 2 * LEVELS + 2 * (level - 1))
                    early, late = halves(lg, level)
                    to_e, to_l = halves(d[:, level % 2], level)
                    n = 2 ** level
                    meet = early[:, :, :, n - 1:n].to_broadcast([P, H, P // (2 * n), n])
                    g.tensor_tensor(to_e, meet, early, ALU.subtract).then_inc(diffd, 1)
                    g.tensor_tensor(to_l, late, meet, ALU.subtract).then_inc(diffd, 1)
                reach(c, pool, factd, b * 2 * LEVELS + 2 * (LEVELS - 1))
                by_chunk = lg.rearrange("p h (a n) -> p h a n", n=CHUNK)
                g.tensor_tensor(d[:, LEVELS % 2].rearrange("p h (a n) -> p h a n", n=CHUNK),
                                by_chunk[:, :, :, CHUNK - 1:CHUNK].to_broadcast([P, H, 2, CHUNK]), by_chunk,
                                ALU.subtract).then_inc(diffd, 1)

        @block.scalar
        def _(act):
            a = nc.scalar.activation
            act.sem_inc(oout, 1)
            with act.Fori(0, NB, 1) as b:
                tok = bass.ds(b * P, P)
                block_start(act, b)
                act.sem_inc(c.passed[act.engine], 1)
                a(eg[:], logs[:, :, tok], ACT.Exp, scale=1.0 / TAU).then_inc(egd, 1)
                for x in range(NX):
                    act.wait_ge(diffd, b * (2 * LEVELS + 1) + min(2 * x + 2, 2 * LEVELS + 1))
                    a(d[:, x % 2], d[:, x % 2], ACT.Exp, scale=1.0 / TAU).then_inc(expd, 1)
                    if x == 1:
                        for n in range(2):
                            act.wait_ge(vturn, b * 2 + (n + 1))
                            a(vn[:, 4 * n:4 * n + 4], B[4 + n], ACT.Copy).then_inc(vout, 1)
                act.wait_ge(kturn, b + 1)
                a(kdn[:], B[6], ACT.Copy).then_inc(kout, 1)
                for n in range(2):
                    reach(c, act, od, b * 2 + (n + 1))
                    a(c.proj[:, G_V:G_V + 2 * H, bass.ds(b * P + n * CHUNK, CHUNK)],
                      B[7].rearrange("p (t n) -> p t n", t=2 * H), ACT.Copy).then_inc(oout, 1)

        @block.tensor
        def _(pe):
            t = nc.tensor
            with pe.Fori(0, NB, 1) as b:
                block_start(pe, b)
                pe.wait_ge(staged, b * 2 + 2)
                for n in range(2):
                    for i in range(4):
                        last = t.transpose(B[4 + n][:, i * P:(i + 1) * P], vs[:, 4 * n + i], c.ident[:])
                    last.then_inc(vturn, 1)
                pe.wait_ge(qegd, b * 2 + 1)
                for h in range(H):
                    last = t.matmul(B[0][:, h * P:(h + 1) * P], ks[:, h], qs[:, h], start=True, stop=True)
                last.then_inc(prodd, 1)
                for level in range(LEVELS):
                    pe.wait_ge(factd, b * 2 * LEVELS + 2 * level + 2)
                    if level >= 1:
                        pe.wait_ge(attd, b * (LEVELS + 1) + level)
                    for h in range(H):
                        last = t.matmul(B[(level + 1) % 2][:, h * P:(h + 1) * P], w[:, level % 2, h],
                                        w[:, level % 2, h], start=True, stop=True)
                    last.then_inc(prodd, 1)
                pe.wait_ge(kdd, b + 1)
                for h in range(H):
                    last = t.transpose(B[6][:, h * P:(h + 1) * P], kd[:, h], c.ident[:])
                last.then_inc(kturn, 1)
                pe.wait_ge(vout, b * 2 + 2)
                for a in range(2):
                    part = slice(a * CHUNK, (a + 1) * CHUNK)
                    if a == 0:
                        pe.wait_ge(qegd, b * 2 + 2)
                        pe.wait_ge(attd, b * (LEVELS + 1) + (LEVELS + 1))
                        pe.wait_ge(kout, b + 1)
                    else:
                        pe.wait_ge(stated, b * 8 + 5)
                        pe.wait_ge(oout, b * 2 + 2)
                    for h in range(H):
                        for half in range(2):
                            i = 2 * h + half
                            o = B[7][:, i * CHUNK:(i + 1) * CHUNK]
                            t.matmul(o, state[:, h, half * P:(half + 1) * P], qeg[:, h, part], start=True, stop=False)
                            last = t.matmul(o, vn[part, i], att[part, h, part], start=False, stop=True)
                    last.then_inc(od, 1)
                    for h in range(H):
                        last = t.matmul(B[2 + h // 2][:, (h % 2) * GDV:(h % 2 + 1) * GDV], kdn[part, h],
                                        vn[part, 2 * h:2 * h + 2], start=True, stop=True)
                    last.then_inc(dsd, 1)

        @block.vector
        def _(dve):
            v = nc.vector
            v.memset(state[:], 0.0).then_inc(stated, 1)
            with dve.Fori(0, NB, 1) as b:
                tok = bass.ds(b * P, P)
                block_start(dve, b)
                dve.sem_inc(c.passed[dve.engine], 1)
                v.tensor_scalar(qs[:], c.proj[:, G_Q:G_Q + H, tok], SCALE, None, ALU.mult).then_inc(qegd, 1)
                dve.wait_ge(egd, b + 1)
                dve.wait_ge(qegd, b * 2 + 1)
                v.tensor_tensor(qeg[:], qs[:], eg[:], ALU.mult).then_inc(qegd, 1)
                dve.wait_ge(staged, b * 2 + 1)
                reach(c, dve, prodd, b * NX + 1)
                v.tensor_tensor(att[:], B[0].rearrange("p (h n) -> p h n", h=H),
                                c.ident[:].unsqueeze(1).to_broadcast([P, H, P]), ALU.mult).then_inc(attd, 1)

                def select(level):
                    dve.wait_ge(attd, b * NX + (level + 1))
                    reach(c, dve, prodd, b * NX + (level + 2))
                    v.copy_predicated(att[:], masks[:, level].bitcast(mybir.dt.uint32).unsqueeze(1)
                                      .to_broadcast([P, H, P]),
                                      B[(level + 1) % 2].rearrange("p (h n) -> p h n", h=H)).then_inc(attd, 1)
                for level in range(LEVELS):
                    dve.wait_ge(expd, b * NX + (level + 1))
                    if level >= 2:
                        dve.wait_ge(prodd, b * NX + level)
                    w_e, w_l = halves(w[:, level % 2], level)
                    e_e, e_l = halves(d[:, level % 2], level)
                    k_e, _ = halves(ks[:], level)
                    _, q_l = halves(qs[:], level)
                    v.tensor_tensor(w_e, k_e, e_e, ALU.mult).then_inc(factd, 1)
                    v.tensor_tensor(w_l, q_l, e_l, ALU.mult).then_inc(factd, 1)
                    if level >= 1:
                        select(level - 1)
                dve.wait_ge(expd, b * NX + NX)
                v.tensor_tensor(kd[:], ks[:], d[:, LEVELS % 2], ALU.mult).then_inc(kdd, 1)
                select(LEVELS - 1)
                for n in range(2):
                    dve.wait_ge(dsd, b * 2 + (n + 1))
                    for h in range(H):
                        last = n * CHUNK + CHUNK - 1
                        v.scalar_tensor_tensor(out=state[:, h], in0=state[:, h], scalar=eg[:, h, last:last + 1],
                                               in1=B[2 + h // 2][:, (h % 2) * GDV:(h % 2 + 1) * GDV],
                                               op0=ALU.mult, op1=ALU.add).then_inc(stated, 1)

        @block.sync
        def _(sp):
            sp.wait_ge(stated, 1 + 8 * NB)
            sp.dma_start(c.outs["p_state_gla"].rearrange("o b h k v -> k (o b h) v"), state[:]).then_inc(stored, 16)
            sp.wait_ge(stored, 16)



def gla_sample_phase(c, area):
    nc = c.nc
    H, U = HEADS, DEC * HEADS
    states = area("sample_states", [P, U, GDV])
    eg, qe, prod = area("decay", [P, H, DEC]), area("q_decayed", [P, H, DEC]), area("qk", [P, H, DEC])
    dots, tmp = area("dots", [P, H, DEC]), area("dots_v", [P, H, 2, DEC])
    diag = area("v_diagonals", [P, 2, 2 * H, P])
    s = lambda n: c.sem("gs_" + n)
    loaded, egd, dotted, mult, decayed, diagd, wide, new, steps, stored = map(s, (
        "loaded decay dotted multiplied decayed diag wide new steps stored").split())
    q, k = c.proj[:, G_Q:G_Q + H, SEQ:TOK], c.proj[:, G_K:G_K + H, SEQ:TOK]
    vv = c.proj[:, G_V:G_V + 2 * H, SEQ:TOK]
    vcopy = area("v", [P, 2 * H, DEC])
    with nc.Block() as block:
        @block.sync
        def _(sp):
            sp.dma_start(states[:], c.ins["state_gla"].rearrange("o b h k v -> k (o b h) v")).then_inc(loaded, 16)
            with sp.Fori(0, DEC, 1) as b:
                sp.wait_ge(new, b * H + H)
                sp.dma_start(c.outs["s_state_gla"].rearrange("o b h k v -> k (o b) h v")[:, bass.ds(b, 1)]
                             .rearrange("k b h v -> k (b h) v"), states[:, bass.ds(b * H, H), :]).then_inc(stored, 16)
            sp.wait_ge(stored, 16 * DEC)

        @block.scalar
        def _(act):
            nc.scalar.activation(eg[:], c.gla_logs[:, :, SEQ:TOK], ACT.Exp, scale=1.0 / TAU).then_inc(egd, 1)
            act.wait_ge(egd, 1)
            act.wait_ge(mult, 1)
            for b in range(DEC):
                for h in range(H):
                    u = b * H + h
                    nc.scalar.activation(states[:, u], states[:, u], ACT.Copy, scale=eg[:, h, b:b + 1]
                                         ).then_inc(decayed, 1)

        @block.tensor
        def _(pe):
            t = nc.tensor
            pe.wait_ge(steps, 2)
            t.matmul(c.ps[:, 0, 0:U], c.ones[:], prod[:], start=True, stop=True).then_inc(dotted, 1)
            pe.wait_ge(loaded, 16)
            pe.wait_ge(steps, 3)
            for h in range(H):
                for half in range(2):
                    for b in range(DEC):
                        col = (2 * h + half) * DEC + b
                        last = t.matmul(c.ps[:, 1, col:col + 1], states[:, b * H + h, half * P:(half + 1) * P],
                                        qe[:, h, b:b + 1], start=True, stop=True)
            last.then_inc(mult, 1)
            for b in range(DEC):
                pe.wait_ge(diagd, b + 1)
                if b >= 2:
                    pe.wait_ge(new, H * (b - 1))
                for n in range(2):
                    last = t.matmul(c.ps[:, 2 + 2 * (b % 2) + n, :], c.ones[:], diag[:, b % 2, 4 * n:4 * n + 4],
                                    start=True, stop=True)
                last.then_inc(wide, 1)

        @block.vector
        def _(dve):
            v = nc.vector
            own = Steps(steps)
            SCALE = P ** -0.5
            own(v.tensor_copy(vcopy[:], vv))
            own(v.scalar_tensor_tensor(out=prod[:], in0=q, scalar=SCALE, in1=k, op0=ALU.mult, op1=ALU.mult))
            dve.wait_ge(egd, 1)
            own(v.scalar_tensor_tensor(out=qe[:], in0=q, scalar=SCALE, in1=eg[:], op0=ALU.mult, op1=ALU.mult))
            dve.wait_ge(dotted, 1)
            n = own(v.tensor_copy(dots[:], c.ps[:, 0, 0:U]))
            dve.wait_ge(own.sem, n)
            n = own(v.tensor_tensor(tmp[:], vcopy[:].rearrange("p (h a) b -> p h a b", a=2),
                                    dots[:].unsqueeze(2).to_broadcast([P, H, 2, DEC]), ALU.mult))
            dve.wait_ge(own.sem, n)
            dve.wait_ge(mult, 1)
            own(v.tensor_tensor(vv, tmp[:].rearrange("p h a b -> p (h a) b"),
                                c.ps[:, 1, 0:2 * H * DEC].rearrange("p (t b) -> p t b", b=DEC), ALU.add))

            def update(b):
                dve.wait_ge(wide, b + 1)
                dve.wait_ge(decayed, (b + 1) * H)
                for h in range(H):
                    v.scalar_tensor_tensor(out=states[:, b * H + h],
                                           in0=c.ps[:, 2 + 2 * (b % 2) + h // 2, (h % 2) * GDV:(h % 2 + 1) * GDV],
                                           scalar=k[:, h, b:b + 1], in1=states[:, b * H + h], op0=ALU.mult,
                                           op1=ALU.add).then_inc(new, 1)
            for b in range(DEC):
                if b >= 2:
                    dve.wait_ge(wide, b - 1)
                v.tensor_tensor(diag[:, b % 2], c.ident[:].unsqueeze(1).to_broadcast([P, 2 * H, P]),
                                vcopy[:, :, b:b + 1].to_broadcast([P, 2 * H, P]), ALU.mult).then_inc(diagd, 1)
                if b >= 1:
                    update(b - 1)
            update(DEC - 1)



def give_back(c, before):
    mine = [name for name in c.sems if name not in before]
    c.nc.clear_and_free_semaphores([c.sems.pop(name) for name in mine])
    c.nc.all_engine_barrier()


def even_mixer_phases(c):
    area = mixer_area(c, "delta")
    delta_prepare_phase(c, area)
    build_level_masks(c, area)
    delta_phase(c, area.passing("delta_main"))
    delta_sample_phase(c, area.passing("delta_sample"))
    area = mixer_area(c, "window")
    window_masks_phase(c, area)
    window_phase(c, area)
    window_sample_phase(c, mixer_area(c, "window_sample"))
    finish_phase(c, "even_finish", T_Q, T_Z, 1, V_DN, T_K, T_V, range(T_SQ, T_SQ + 4))


def odd_mixer_phases(c):
    area = mixer_area(c, "gla")
    gla_prepare_phase(c, area)
    build_level_masks(c, area)
    gla_phase(c, area.passing("gla_main"))
    gla_sample_phase(c, area.passing("gla_sample"))
    finish_phase(c, "odd_finish", G_V, G_R, 2, V_GN, G_K, G_Q, [])


def program(nc, ins, outs):
    with ExitStack() as es:
        c = make(nc, es, ins, outs)
        even_w = ins["even_w_in"][0]
        even_in = ([cols_view(even_w, t * P) for t in range(12)] + [cols_view(even_w, E_Z + t * P) for t in range(4)]
                   + [cols_view(even_w, E_Q + t * P) for t in range(4)] + [cols_view(even_w, E_K), cols_view(even_w, E_V)]
                   + [cols_view(even_w, E_A, 2 * HEADS)])
        even_out = [cols_view(ins["even_w_out"][0], t * P) for t in range(KT)]
        odd_in = ([cols_view(ins["gla_w_in"][0], t * P) for t in range(ODD_TILES - 1)]
                  + [cols_view(ins["gla_w_in"][0], O_DOWN, RANK)])
        odd_out = [cols_view(ins["gla_w_out"][0], t * P) for t in range(KT)]
        mlp_first = [[cols_view(ins["mlp_w_up"][layer], t * P) for t in range(2)] for layer in range(2)]

        setup_phase(c, even_in[:2])
        norm_phase(c, V_MIX, save=True)
        conv_projection_phase(c, even_in[12:14])
        projection_phase(c, even_in[12:], even_out[:2], 12)
        kept = set(c.sems)
        even_mixer_phases(c)
        give_back(c, kept)
        output_projection_phase(c, even_out, mlp_first[0], 1)
        norm_phase(c, V_MLP)
        mlp_phase(c, 0, odd_in[:2])
        norm_phase(c, V_MIX + KT, save=True)
        projection_phase(c, odd_in, odd_out[:2], 0, saves=2)
        odd_mixer_phases(c)
        output_projection_phase(c, odd_out, mlp_first[1], 2)
        norm_phase(c, V_MLP + KT)
        mlp_phase(c, 1, [])
        final_phase(c)


OUTPUTS = [("y_prompt", (1, SEQ, D)), ("y_sample", (DEC, 1, D)), ("p_state_dn", (1, 1, HEADS, P, P)),
           ("p_state_dn_conv", (1, 1, CONV - 1, 3 * HEADS * P)), ("p_cache_swa_k", (1, 1, P, KVH, HD)),
           ("p_cache_swa_v", (1, 1, P, KVH, HD)), ("p_state_gla", (1, 1, HEADS, P, GDV)),
           ("s_state_dn", (1, DEC, HEADS, P, P)), ("s_state_dn_conv", (1, DEC, CONV - 1, 3 * HEADS * P)),
           ("s_cache_swa_k", (1, DEC, P, KVH, HD)), ("s_cache_swa_v", (1, DEC, P, KVH, HD)),
           ("s_state_gla", (1, DEC, HEADS, P, GDV))]


def kernel(**inputs):
    import numpy as np
    import concourse.bacc as bacc
    from concourse.bass_utils import run_bass_kernel_spmd
    nc = bacc.Bacc("TRN2", target_bir_lowering=False, num_devices=1)
    arrays = {name: np.ascontiguousarray(a) for name, a in inputs.items()}
    ins = {name: nc.dram_tensor(name, a.shape, mybir.dt.from_np(a.dtype), kind="ExternalInput").ap()
           for name, a in arrays.items()}
    outs = {name: nc.dram_tensor("o_" + name, shape, F32, kind="ExternalOutput").ap() for name, shape in OUTPUTS}
    program(nc, ins, outs)
    result = run_bass_kernel_spmd(nc, [arrays], core_ids=[0]).results[0]
    return tuple(result["o_" + name] for name, _ in OUTPUTS)
```

```python
import concourse.bass as bass
from concourse import mybir
from contextlib import ExitStack

F32 = mybir.dt.float32
F32R = mybir.dt.float32r
ALU = mybir.AluOpType
ACT = mybir.ActivationFunctionType
AX = mybir.AxisListType

P = 128
D = 1024
KT = D // P
SEQ = 1024
DEC = 8
TOK = SEQ + DEC
NCH = 3
CW = TOK // NCH
NB = SEQ // P
EPS = 1e-6
HEADS = 4
CHUNK = 64
DFF = 4 * D
CONV = 4
HD = 64
SWH, KVH = 8, 2
RANK = 16
TAU = 16.0
GDV = 256
E_Z = 3 * 512
E_A = E_Z + 512
E_B = E_A + HEADS
E_Q = E_B + HEADS
E_K = E_Q + SWH * HD
E_V = E_K + KVH * HD
T_Q, T_K, T_V, T_Z, T_SQ, T_SK, T_SV, T_AB = 0, 4, 8, 12, 16, 20, 21, 22
EVEN_TILES = 23
G_Q, G_K, G_V, G_R, G_D = 0, 4, 8, 16, 24
ODD_TILES = 25
O_DOWN = 2 * 512 + 2 * 1024
V_MIX, V_MLP, V_FIN, V_CONV, V_GB, V_DN, V_GN = 0, 16, 32, 40, 88, 92, 93
V_ROWS = 95

TB = TOK * 4
BASE = 16512
PROJ_AT = BASE
ACT_AT = PROJ_AT + 25 * TB
ACT_LO_AT = ACT_AT + 8 * TB
WORK_AT = ACT_AT + 16 * TB
END = 229344


class Ctx:
    pass


def make(nc, es, ins, outs):
    c = Ctx()
    c.nc, c.es = nc, es
    c.ins, c.outs = ins, outs
    c.sems = {}
    c.tiles_before = 0
    c.norms_before = 0

    def at(name, shape, offset, dt=F32):
        return nc.alloc_sbuf_tensor_at(name, shape, dt, offset=offset)

    def sem(name):
        if name not in c.sems:
            c.sems[name] = nc.alloc_semaphore(name=name)
        return c.sems[name]
    c.at, c.sem = at, sem

    top = END
    def const(name, shape, dt=F32):
        nonlocal top
        n = 4
        for s in shape[1:]:
            n *= s
        top -= (n + 31) // 32 * 32
        return at(name, shape, top, dt)
    c.ident = const("ident", [P, P])
    c.ones = const("ones", [P, P])
    c.vcols = const("vcols", [P, V_ROWS + 1])
    c.eps = const("eps", [P, 1])
    c.const = const
    c.bufT = const("buf_cols", [P, 12, DEC * (CONV - 1)])
    c.tail = const("conv_tail", [P, 12, CONV - 1 + DEC])
    c.proj = at("proj", [P, 25, TOK], PROJ_AT)
    c.act_hi = at("act_hi", [P, KT, TOK], ACT_AT, F32R)
    c.act_lo = at("act_lo", [P, KT, TOK], ACT_LO_AT, F32R)
    w = WORK_AT
    c.w_raw = at("w_raw", [P, 2, KT, P], w); w += 2 * KT * P * 4
    c.w_hi = at("w_hi", [P, 2, KT, P], w, F32R); w += 2 * KT * P * 4
    c.w_lo = at("w_lo", [P, 2, KT, P], w, F32R); w += 2 * KT * P * 4
    c.scr_at = w
    c.tmp = at("tmp", [P, 2, TOK], w); w += 2 * TB
    c.rb = at("rb", [P, TOK], w); w += TB
    c.const_at = top
    c.ps = es.enter_context(nc.psum_tensor("ps", [P, 8, 512], F32))
    c.x_save = nc.dram_tensor("x_save", [P, KT, TOK], F32).ap()

    c.passed = {e.engine: sem(f"passed_{n}") for n, e in enumerate((nc.scalar, nc.vector, nc.gpsimd, nc.tensor))}
    c.raw_in = [sem("raw_in0"), sem("raw_in1")]
    c.hi_done, c.lo_done, c.tiles_done, c.evac_done = map(sem, ("hi_done", "lo_done", "tiles_done", "evac_done"))
    return c


def reach(c, eng, sem, value):
    eng.wait_ge(sem, value)
    if not isinstance(value, int):
        eng.sem_inc(c.passed[eng.engine], 1)



def load_tile(c, sp, slot, g, src):
    sp.wait_ge(c.lo_done, g + 1)
    sp.dma_start(c.w_raw[:, slot, :, 0:src.shape[2]], src).then_inc(c.raw_in[slot], 16)


def split_hi(c, act, slot, g):
    act.wait_ge(c.raw_in[slot], g * 8 + (16 - 8 * slot))
    act.wait_ge(c.tiles_done, g + 1)
    c.nc.scalar.activation(c.w_hi[:, slot], c.w_raw[:, slot], ACT.Copy).then_inc(c.hi_done, 1)


def split_lo(c, dve, slot, g):
    dve.wait_ge(c.hi_done, g + 1)
    c.nc.vector.tensor_tensor(c.w_lo[:, slot], c.w_raw[:, slot], c.w_hi[:, slot].bitcast(F32),
                              ALU.subtract).then_inc(c.lo_done, 1)


def multiply_tile(c, pe, slot, g, hi, lo, ready=None):
    pe.wait_ge(c.lo_done, g + 3)
    pe.wait_ge(c.evac_done, g + 1)
    last = None
    for ch in range(NCH):
        cols = slice(ch * CW, (ch + 1) * CW)
        out = c.ps[:, 3 * slot + ch, 0:CW]
        for k in range(KT):
            if ready and (ch == 0 or (ch == 1 and k == 0)):
                ready(k if ch == 0 else KT)
            for n, (w, x) in enumerate(((c.w_hi, hi), (c.w_hi, lo), (c.w_lo, hi))):
                last = c.nc.tensor.matmul(out, w[:, slot, k, :], x[:, k, cols],
                                          start=(k == 0 and n == 0), stop=(k == KT - 1 and n == 2))
    last.then_inc(c.tiles_done, 1)


def tile_psum(c, slot):
    return c.ps[:, 3 * slot:3 * slot + 3, 0:CW]


def chunked(ap):
    return ap.rearrange("p (c n) -> p c n", c=NCH)


def in_pairs(eng, n, body, first=None):
    if first:
        first()
        with eng.Fori(1, n // 2, 1) as pair:
            i = pair * 2
            body(i, 0)
            body(i + 1, 1)
    elif n // 2 == 1:
        body(0, 0)
        body(1, 1)
    elif n // 2:
        with eng.Fori(0, n // 2, 1) as pair:
            i = pair * 2
            body(i, 0)
            body(i + 1, 1)
    if n % 2:
        body(n - 1, 0)


def lead_pairs(eng, n, ahead, first, second=None):
    def turn(t, odd):
        first(t, odd)
        ahead(t + 2, odd)
        if second:
            second(t, odd)
    looped = n // 2 * 2
    if looped:
        with eng.Fori(0, looped // 2, 1) as pair:
            i = pair * 2
            turn(i, 0)
            turn(i + 1, 1)
    for t in range(looped, n):
        turn(t, t % 2)


def cols_view(w, first, count=P):
    return w.rearrange("(k p) n -> p k n", p=P)[:, :, first:first + count]



def setup_phase(c, first_tiles):
    nc, ins = c.nc, c.ins
    loads, consts, small = c.sem("setup_loads"), c.sem("setup_consts"), c.sem("setup_small")
    turned_small, turned, placed = c.sem("small_turned"), c.sem("rows_turned"), c.sem("rows_placed")
    rows = c.at("x_rows", [P, 2, D], ACT_AT)
    srows = c.at("sample_rows", [DEC, D], ACT_AT + 8192)
    vrows = c.at("v_rows", [V_ROWS, P], ACT_AT + 12288)
    brows = c.at("buf_rows", [DEC * 3, 12, P], ACT_AT + 16384)
    rows_in = [c.sem("rows_in0"), c.sem("rows_in1")]
    prompt = ins["x_prompt"].rearrange("a (b p) d -> (a b) p d", p=P)
    with nc.Block() as block:
        @block.sync
        def _(sp):
            sp.dma_start(srows[:], ins["x_sample"].rearrange("b s d -> (b s) d")).then_inc(loads, 16)
            for name, row, n in (("norm_mix", V_MIX, 16), ("norm_mlp", V_MLP, 16), ("norm_final", V_FIN, 8),
                                 ("dn_conv_w", V_CONV, 48), ("gla_b_gate", V_GB, 4), ("dn_norm", V_DN, 1),
                                 ("gla_norm", V_GN, 2)):
                a = ins[name]
                if len(a.shape) == 3:
                    a = a.rearrange("e i c -> (e i c)")
                elif len(a.shape) == 2:
                    a = a.rearrange("e c -> (e c)")
                sp.dma_start(vrows[row:row + n, :], a.rearrange("(k p) -> k p", p=P)).then_inc(loads, 16)
            sp.dma_start(brows[:], ins["state_dn_conv"].rearrange("e b i (t p) -> (e b i) t p", p=P)).then_inc(loads, 16)
            for b in range(2):
                sp.dma_start(rows[:, b], prompt[b]).then_inc(rows_in[b], 16)
            with sp.Fori(1, NB // 2, 1) as pair:
                b = pair * 2
                for slot in range(2):
                    sp.wait_ge(turned, 2 * b + (2 * slot - 2))
                    sp.dma_start(rows[:, slot], prompt[bass.ds(b + slot, 1)].rearrange("a p d -> p (a d)")
                                 ).then_inc(rows_in[slot], 16)
            for t, parts in enumerate(first_tiles):
                load_tile(c, sp, t, t, parts)

        @block.gpsimd
        def _(pool):
            g = nc.gpsimd
            g.memset(c.ident[:], 0.0).then_inc(consts, 1)
            g.memset(c.ones[:], 1.0).then_inc(consts, 1)
            g.memset(c.eps[:], EPS).then_inc(consts, 1)
            pool.wait_ge(consts, 3)
            g.affine_select(out=c.ident[:], in_=c.ident[:], compare_op=ALU.not_equal, fill=1.0, base=0,
                            pattern=[[-1, P]], channel_multiplier=1).then_inc(consts, 1)

        @block.scalar
        def _(act):
            for t in range(2):
                split_hi(c, act, t, t)

        @block.tensor
        def _(pe):
            pe.sem_inc(c.tiles_done, 2)
            pe.wait_ge(loads, 16 * 9)
            pe.wait_ge(consts, 4)
            nc.tensor.transpose(c.ps[:, 0, 0:V_ROWS], vrows[:], c.ident[0:V_ROWS, 0:V_ROWS]).then_inc(turned_small, 1)
            for g3 in range(3):
                for t in range(4):
                    last = nc.tensor.transpose(c.ps[:, 1 + g3, t * 24:(t + 1) * 24], brows[:, 4 * g3 + t, :],
                                               c.ident[0:24, 0:24])
                if g3 < 2:
                    last.then_inc(turned_small, 1)
            for t in range(KT):
                last = nc.tensor.transpose(c.ps[:, 3, 256 + t * DEC:256 + (t + 1) * DEC],
                                           srows[:, t * P:(t + 1) * P], c.ident[0:DEC, 0:DEC])
            last.then_inc(turned_small, 1)
            with pe.Fori(0, NB // 2, 1) as pair:
                b = pair * 2
                for slot in range(2):
                    pe.wait_ge(rows_in[slot], b * 8 + 16)
                    for half in range(2):
                        pe.wait_ge(placed, 2 * b + (2 * slot + half + 1))
                        for t in range(4):
                            k = 4 * half + t
                            last = nc.tensor.transpose(c.ps[:, 4 + 2 * slot + half, t * P:(t + 1) * P],
                                                       rows[:, slot, k * P:(k + 1) * P], c.ident[:])
                        last.then_inc(turned, 1)

        @block.vector
        def _(dve):
            v = nc.vector
            dve.sem_inc(c.lo_done, 2)
            dve.sem_inc(c.evac_done, 2)
            dve.sem_inc(placed, 4)
            dve.wait_ge(turned_small, 1)
            v.tensor_copy(c.vcols[:, 0:V_ROWS], c.ps[:, 0, 0:V_ROWS]).then_inc(small, 1)
            for g3 in range(3):
                dve.wait_ge(turned_small, 2 + g3)
                v.tensor_copy(c.bufT[:, 4 * g3:4 * g3 + 4, :], c.ps[:, 1 + g3, 0:96].rearrange("p (t n) -> p t n", t=4)
                              ).then_inc(small, 1)
            v.tensor_copy(c.proj[:, 0:KT, SEQ:TOK], c.ps[:, 3, 256:256 + KT * DEC].rearrange("p (t n) -> p t n", t=KT)
                          ).then_inc(small, 1)
            with dve.Fori(0, NB // 2, 1) as pair:
                b = pair * 2
                for slot in range(2):
                    for half in range(2):
                        reach(c, dve, turned, 2 * b + (2 * slot + half + 1))
                        v.tensor_copy(c.proj[:, 4 * half:4 * half + 4, bass.ds((b + slot) * P, P)],
                                      c.ps[:, 4 + 2 * slot + half, :].rearrange("p (t n) -> p t n", t=4)
                                      ).then_inc(placed, 1)
            for t in range(2):
                split_lo(c, dve, t, t)



class Norm:

    def __init__(self, c, vcol, save=False):
        self.c, self.vcol, self.keeps_residual = c, vcol, save
        self.n0, self.base = c.norms_before, c.tiles_before
        c.norms_before += 1
        (self.squares, self.squares_v, self.paired, self.summed, self.scale, self.upper, self.lower) = map(c.sem, (
            "norm_squares", "norm_squares_v", "norm_paired", "norm_summed", "norm_scale", "norm_upper", "norm_lower"))
        self.x = c.proj
        self.pairs = KT // 2 * self.n0
        self.slot = self.base % 2

    def weight(self, k):
        return self.c.vcols[:, self.vcol + k:self.vcol + k + 1]

    def square(self, k):
        return self.c.proj[:, KT + k, :]

    def on_sync(self, sp):
        if self.keeps_residual:
            sp.dma_start(self.c.x_save, self.x[:, 0:KT, :]).then_inc(self.c.sem("x_saved"), 16)

    def on_scalar(self, act):
        c, nc = self.c, self.c.nc
        for k in range(KT):
            if k % 2 == 0:
                nc.scalar.activation(self.square(k), self.x[:, k, :], ACT.Square).then_inc(self.squares, 1)
            nc.scalar.activation(c.act_hi[:, k, :], self.x[:, k, :], ACT.Copy, scale=self.weight(k)
                                 ).then_inc(self.upper, 1)
        act.wait_ge(self.summed, self.pairs + KT // 2)
        nc.scalar.activation(chunked(c.rb[:]), tile_psum(c, 1 - self.slot), ACT.Ln, bias=c.eps[:], scale=1.0 / D
                             ).then_inc(self.scale, 1)
        act.wait_ge(self.scale, 2 * self.n0 + 1)
        nc.scalar.activation(c.rb[:], c.rb[:], ACT.Exp, scale=-0.5).then_inc(self.scale, 1)

    def on_gpsimd(self, pool):
        for j in range(KT // 2):
            pool.wait_ge(self.squares, self.pairs + j + 1)
            pool.wait_ge(self.squares_v, self.pairs + j + 1)
            even = self.square(2 * j)
            self.c.nc.gpsimd.tensor_tensor(even, even, self.square(2 * j + 1), ALU.add).then_inc(self.paired, 1)

    def on_vector(self, dve):
        c, v = self.c, self.c.nc.vector
        for k in range(KT):
            if k % 2 == 0:
                v.tensor_tensor(self.square(k + 1), self.x[:, k + 1, :], self.x[:, k + 1, :], ALU.mult
                                ).then_inc(self.squares_v, 1)
            dve.wait_ge(self.upper, KT * self.n0 + k + 1)
            v.scalar_tensor_tensor(out=c.act_lo[:, k, :], in0=self.x[:, k, :], scalar=self.weight(k),
                                   in1=c.act_hi[:, k, :].bitcast(F32), op0=ALU.mult, op1=ALU.subtract
                                   ).then_inc(self.lower, 1)
        dve.wait_ge(self.scale, 2 * self.n0 + 2)

    def on_tensor(self, pe):
        c = self.c

        def ready(k):
            if k and k % 2 == 0:
                j = k // 2 - 1
                pe.wait_ge(self.paired, self.pairs + j + 1)
                for ch in range(NCH):
                    last = c.nc.tensor.matmul(c.ps[:, 3 * (1 - self.slot) + ch, 0:CW], c.ones[:],
                                              self.square(2 * j)[:, ch * CW:(ch + 1) * CW], start=j == 0, stop=j == KT // 2 - 1)
                last.then_inc(self.summed, 1)
            if k < KT:
                pe.wait_ge(self.lower, KT * self.n0 + k + 1)
        multiply_tile(c, pe, self.slot, self.base, c.act_hi, c.act_lo, ready)
        pe.wait_ge(self.scale, 2 * self.n0 + 1)
        multiply_tile(c, pe, 1 - self.slot, self.base + 1, c.act_hi, c.act_lo)



def even_projection_phase(c, vcol, tiles, next_tiles):
    nc = c.nc
    norm = Norm(c, vcol, save=True)
    base, n = c.tiles_before, 12
    base2, n2 = base + n, len(tiles) - n
    c.tiles_before += n + n2
    w_in = c.ins["even_w_in"].rearrange("e d n -> (e d) n")
    conved, silued, saved, tails = c.sem("conved"), c.sem("silued"), c.sem("x_saved"), c.sem("tails_kept")
    conv = c.tmp
    with nc.Block() as block:
        @block.sync
        def _(sp):
            norm.on_sync(sp)
            with sp.Fori(1, n // 2, 1) as pair:
                t = pair * 2
                for odd in range(2):
                    load_tile(c, sp, odd, t + (base + odd), w_in.rearrange("(k p) n -> p k n", p=P)[
                        :, :, bass.ds((t + odd) * P, P)])
            for t, parts in enumerate(tiles[n:] + next_tiles):
                load_tile(c, sp, t % 2, base2 + t, parts)

        @block.gpsimd
        def _(pool):
            norm.on_gpsimd(pool)

        @block.tensor
        def _(pe):
            in_pairs(pe, n, lambda t, odd: multiply_tile(c, pe, odd, t + base, c.act_hi, c.act_lo),
                     lambda: norm.on_tensor(pe))
            in_pairs(pe, n2, lambda t, odd: multiply_tile(c, pe, odd, t + base2, c.act_hi, c.act_lo))

        @block.scalar
        def _(act):
            norm.on_scalar(act)
            act.sem_inc(silued, 2)

            def silu(t, odd):
                reach(c, act, conved, t * CONV_STEPS + CONV_STEPS)
                nc.scalar.activation(c.proj[:, t, :], conv[:, odd], ACT.Silu).then_inc(silued, 1)
            lead_pairs(act, n, lambda t, odd: split_hi(c, act, odd, t + base), lambda t, odd: None, silu)
            lead_pairs(act, n2, lambda t, odd: split_hi(c, act, odd, t + base2), lambda t, odd: None)

        @block.vector
        def _(dve):
            norm.on_vector(dve)
            v = nc.vector

            def conv_tile(t, odd):
                u = c.proj[:, t, :]
                o = conv[:, odd]

                def w(i):
                    return c.vcols[:, bass.ds(t + (V_CONV + 12 * i), 1)]
                evacuate(c, dve, c.proj[:, t, :], odd, t + base)
                reach(c, dve, c.evac_done, t + (base + 3))
                reach(c, dve, silued, t + 1)
                s = t * CONV_STEPS
                v.tensor_scalar(o, u, w(CONV - 1), None, ALU.mult).then_inc(conved, 1)
                v.tensor_copy(c.tail[:, t, :], u[:, SEQ - CONV + 1:TOK]).then_inc(tails, 1)
                for i in range(CONV - 1):
                    back = CONV - 1 - i
                    reach(c, dve, conved, s + 1 + 2 * i)
                    v.scalar_tensor_tensor(out=o[:, back:SEQ], in0=u[:, 0:SEQ - back], scalar=w(i),
                                           in1=o[:, back:SEQ], op0=ALU.mult, op1=ALU.add).then_inc(conved, 1)
                    v.scalar_tensor_tensor(out=o[:, SEQ:TOK],
                                           in0=c.bufT[:, t, :].rearrange("p (b i) -> p i b", i=CONV - 1)[:, i, :],
                                           scalar=w(i), in1=o[:, SEQ:TOK], op0=ALU.mult, op1=ALU.add
                                           ).then_inc(conved, 1)
            dve.wait_ge(saved, 16)
            lead_pairs(dve, n, lambda t, odd: split_lo(c, dve, odd, t + base), lambda t, odd: None, conv_tile)
            lead_pairs(dve, n2, lambda t, odd: split_lo(c, dve, odd, t + base2),
                       lambda t, odd: evacuate(c, dve, c.proj[:, t + n, :], odd, t + base2))


CONV_STEPS = 1 + 2 * (CONV - 1)



def projection_phase(c, vcol, tiles, next_tiles, saves):
    norm = Norm(c, vcol, save=True)
    nc = c.nc
    base, n = c.tiles_before, len(tiles)
    c.tiles_before += n
    parity = base % 2
    with nc.Block() as block:
        @block.sync
        def _(sp):
            norm.on_sync(sp)
            for t, parts in list(enumerate(tiles + next_tiles))[2:]:
                load_tile(c, sp, (base + t) % 2, base + t, parts)

        @block.gpsimd
        def _(pool):
            norm.on_gpsimd(pool)

        @block.tensor
        def _(pe):
            in_pairs(pe, n, lambda t, odd: multiply_tile(c, pe, (odd + parity) % 2, t + base, c.act_hi, c.act_lo),
                     lambda: norm.on_tensor(pe))

        @block.scalar
        def _(act):
            norm.on_scalar(act)
            lead_pairs(act, n, lambda t, odd: split_hi(c, act, (odd + parity) % 2, t + base), lambda t, odd: None)

        @block.vector
        def _(dve):
            norm.on_vector(dve)
            dve.wait_ge(c.sem("x_saved"), 16 * saves)

            def take(t, odd):
                evacuate(c, dve, c.proj[:, t, :], (odd + parity) % 2, t + base)
            lead_pairs(dve, n, lambda t, odd: split_lo(c, dve, (odd + parity) % 2, t + base), take)


def evacuate(c, dve, out, slot, g):
    reach(c, dve, c.tiles_done, g + 3)
    c.nc.vector.tensor_tensor(chunked(out), tile_psum(c, slot), chunked(c.rb[:]), ALU.mult).then_inc(c.evac_done, 1)



def output_projection_phase(c, tiles, next_tiles, reloads):
    nc = c.nc
    base, n = c.tiles_before, KT
    c.tiles_before += n
    parity = base % 2
    reloaded = c.sem("x_reloaded")
    with nc.Block() as block:
        @block.sync
        def _(sp):
            sp.dma_start(c.proj[:, 0:KT, :], c.x_save).then_inc(reloaded, 16)
            for t, parts in list(enumerate(tiles + next_tiles))[2:]:
                load_tile(c, sp, (base + t) % 2, base + t, parts)

        @block.tensor
        def _(pe):
            in_pairs(pe, n, lambda t, odd: multiply_tile(c, pe, (odd + parity) % 2, t + base, c.act_hi, c.act_lo))

        @block.scalar
        def _(act):
            lead_pairs(act, n, lambda t, odd: split_hi(c, act, (odd + parity) % 2, t + base), lambda t, odd: None)

        @block.vector
        def _(dve):
            dve.wait_ge(reloaded, 16 * reloads)

            def add(t, odd):
                add_to_residual(c, dve, t, (odd + parity) % 2, t + base)
            lead_pairs(dve, n, lambda t, odd: split_lo(c, dve, (odd + parity) % 2, t + base), add)


def add_to_residual(c, dve, k, slot, g):
    dve.wait_ge(c.tiles_done, g + 3)
    x = chunked(c.proj[:, k, :])
    c.nc.vector.tensor_tensor(x, x, tile_psum(c, slot), ALU.add).then_inc(c.evac_done, 1)



def mlp_phase(c, vcol, layer, next_tiles):
    nc = c.nc
    norm = Norm(c, vcol)
    nf = DFF // D
    base, n = c.tiles_before, 2 * KT * nf
    c.tiles_before += n
    parity = base % 2
    h0 = layer * KT * nf
    last_phase = not next_tiles
    up = c.ins["mlp_w_up"][layer].rearrange("(k p) n -> p k n", p=P)
    down = c.ins["mlp_w_down"][layer].rearrange("(f k p) n -> p f k n", p=P, k=KT)
    relued, squared = c.sem("hidden_relued"), c.sem("hidden_squared")
    upper, lower = c.sem("hidden_upper"), c.sem("hidden_lower")
    hid_hi = c.at(f"hidden_hi{layer}", [P, KT, TOK], PROJ_AT + KT * TB, F32R)
    hid_lo = c.at(f"hidden_lo{layer}", [P, KT, TOK], PROJ_AT + 2 * KT * TB, F32R)
    h = c.tmp

    def sections(eng, do_up, do_down, leads, first=None):
        def part(f, leads_on, first=None):
            for section, do in enumerate((do_up, do_down)):
                looped = KT if leads_on or section == 0 else KT - 2
                peeled = int(first is not None and section == 0)
                if peeled:
                    first()
                with eng.Fori(peeled, looped // 2, 1) as pair:
                    t = pair * 2
                    for odd in range(2):
                        do(f * (2 * KT) + (t + (base + section * KT + odd)), t + odd, f, odd, True)
                for t in range(looped, KT):
                    do(f * (2 * KT) + (t + base + section * KT), t, f, t % 2, False)
        if leads and last_phase:
            with eng.Fori(0, nf - 1, 1) as f:
                part(f, True)
            part(nf - 1, False)
        elif first:
            part(0, True, first)
            with eng.Fori(1, nf, 1) as f:
                part(f, True)
        else:
            with eng.Fori(0, nf, 1) as f:
                part(f, True)

    with nc.Block() as block:
        @block.sync
        def _(sp):
            def load_up(t, f, odd, g):
                load_tile(c, sp, (odd + parity) % 2, g, up[:, :, bass.ds(f * D + t * P, P)])

            def load_down(t, f, odd, g):
                load_tile(c, sp, (odd + parity) % 2, g, down[:, bass.ds(f, 1), :, bass.ds(t * P, P)]
                          .rearrange("p f k n -> p (f k) n"))

            def both(f, skip):
                with sp.Fori(skip // 2, KT // 2, 1) as pair:
                    t = pair * 2
                    for odd in range(2):
                        load_up(t + odd, f, odd, f * (2 * KT) + (t + (base + odd)))
                with sp.Fori(0, KT // 2, 1) as pair:
                    t = pair * 2
                    for odd in range(2):
                        load_down(t + odd, f, odd, f * (2 * KT) + (t + (base + KT + odd)))
            both(0, 2)
            with sp.Fori(1, nf, 1) as f:
                both(f, 0)
            for t, parts in enumerate(next_tiles):
                load_tile(c, sp, (base + n + t) % 2, base + n + t, parts)

        @block.gpsimd
        def _(pool):
            norm.on_gpsimd(pool)

        @block.tensor
        def _(pe):
            def do_up(g, t, f, odd, _):
                multiply_tile(c, pe, (odd + parity) % 2, g, c.act_hi, c.act_lo)

            def do_down(g, t, f, odd, _):
                def ready(k):
                    if k == 0 or k == KT - 1:
                        pe.wait_ge(lower, f * KT + (h0 + 2 + (KT - 1 if k == 0 else KT)))
                multiply_tile(c, pe, (odd + parity) % 2, g, hid_hi, hid_lo, ready)
            sections(pe, do_up, do_down, False, lambda: norm.on_tensor(pe))

        @block.scalar
        def _(act):
            norm.on_scalar(act)

            def do_up(g, t, f, odd, leads):
                slot = (odd + parity) % 2
                n_hid = f * KT + t + h0
                act.wait_ge(c.evac_done, g + 3)
                nc.scalar.activation(h[:, odd], h[:, odd], ACT.Square).then_inc(squared, 1)
                split_hi(c, act, slot, g + 2)
                reach(c, act, squared, n_hid + 1)
                nc.scalar.activation(hid_hi[:, t, :], h[:, odd], ACT.Copy).then_inc(upper, 1)

            def do_down(g, t, f, odd, leads):
                if leads:
                    split_hi(c, act, (odd + parity) % 2, g + 2)
            sections(act, do_up, do_down, True)

        @block.vector
        def _(dve):
            norm.on_vector(dve)
            if layer == 0:
                dve.sem_inc(lower, 2)
            def do_up(g, t, f, odd, leads):
                n_hid = f * KT + t + h0
                dve.wait_ge(c.tiles_done, g + 3)
                dve.wait_ge(lower, n_hid + 1)
                nc.vector.scalar_tensor_tensor(out=chunked(h[:, odd]), in0=tile_psum(c, (odd + parity) % 2), scalar=0.0,
                                               in1=chunked(c.rb[:]), op0=ALU.max, op1=ALU.mult).then_inc(c.evac_done, 1)
                split_lo(c, dve, (odd + parity) % 2, g + 2)
                reach(c, dve, upper, n_hid + 1)
                nc.vector.tensor_tensor(hid_lo[:, t, :], h[:, odd], hid_hi[:, t, :].bitcast(F32), ALU.subtract
                                        ).then_inc(lower, 1)

            def do_down(g, t, f, odd, leads):
                add_to_residual(c, dve, t, (odd + parity) % 2, g)
                if leads:
                    split_lo(c, dve, (odd + parity) % 2, g + 2)
            sections(dve, do_up, do_down, True)



def final_phase(c):
    nc = c.nc
    squares, summed, scale = c.sem("y_squares"), c.sem("y_summed"), c.sem("y_scale")
    scaled, turned, rowed = c.sem("y_scaled"), c.sem("y_turned"), c.sem("y_rowed")
    stored = [c.sem("y_stored0"), c.sem("y_stored1")]
    x, sq = c.proj, c.tmp
    y = c.at("y_cols", [P, 2, KT, P], ACT_AT)
    rows = c.at("y_rows", [P, 2, D], ACT_AT + 2 * KT * P * 4)
    y_out = c.outs["y_prompt"].rearrange("a (b p) d -> (a b) p d", p=P)
    last_store = {0: NB // 2 + 1, 1: NB // 2}
    with nc.Block() as block:
        @block.scalar
        def _(act):
            for k in range(KT):
                if k >= 2:
                    act.wait_ge(summed, k - 1)
                nc.scalar.activation(sq[:, k % 2], x[:, k, :], ACT.Square).then_inc(squares, 1)
            act.wait_ge(summed, KT)
            nc.scalar.activation(chunked(c.rb[:]), c.ps[:, 0:3, 0:CW], ACT.Ln, bias=c.eps[:], scale=1.0 / D
                                 ).then_inc(scale, 1)
            act.wait_ge(scale, 1)
            nc.scalar.activation(c.rb[:], c.rb[:], ACT.Exp, scale=-0.5).then_inc(scale, 1)
            act.sem_inc(rowed, 4)

            def to_rows(b, slot, n):
                act.wait_ge(stored[slot], b * 8 + (16 - 8 * slot))
                for half in range(2):
                    act.wait_ge(turned, 2 * b + (half + 5))
                    nc.scalar.activation(rows[0:n, slot, half * 512:half * 512 + 512], c.ps[0:n, 4 + 2 * slot + half, :],
                                         ACT.Copy).then_inc(rowed, 1)
            with act.Fori(0, NB // 2, 1) as pair:
                b = pair * 2
                to_rows(b, 0, P)
                to_rows(b + 1, 1, P)
            to_rows(NB, 0, DEC)

        @block.tensor
        def _(pe):
            for k in range(KT):
                pe.wait_ge(squares, k + 1)
                for ch in range(NCH):
                    last = nc.tensor.matmul(c.ps[:, ch, 0:CW], c.ones[:], sq[:, k % 2, ch * CW:(ch + 1) * CW],
                                            start=k == 0, stop=k == KT - 1)
                last.then_inc(summed, 1)

            pe.sem_inc(turned, 4)

            def turn(b, slot, n):
                pe.wait_ge(scaled, 2 * b + 4)
                for half in range(2):
                    pe.wait_ge(rowed, 2 * b + (half + 1))
                    for t in range(4):
                        last = nc.tensor.transpose(c.ps[0:n, 4 + 2 * slot + half, t * P:(t + 1) * P],
                                                   y[:, slot, 4 * half + t, 0:n], c.ident[:])
                    last.then_inc(turned, 1)
            with pe.Fori(0, NB // 2, 1) as pair:
                b = pair * 2
                turn(b, 0, P)
                turn(b + 1, 1, P)
            turn(NB, 0, DEC)

        @block.vector
        def _(dve):
            dve.wait_ge(scale, 2)
            dve.sem_inc(scaled, 2)

            def scale_block(b, slot, n):
                dve.wait_ge(turned, 2 * b + 2)
                cols = bass.ds(b * P, n)
                reach(c, dve, scaled, 2 * b + 2)
                nc.vector.tensor_tensor(y[:, slot, :, 0:n], x[:, 0:KT, cols],
                                        c.rb[:, cols].unsqueeze(1).to_broadcast([P, KT, n]), ALU.mult).then_inc(scaled, 1)
                dve.wait_ge(scaled, 2 * b + 3)
                nc.vector.tensor_tensor(y[:, slot, :, 0:n], y[:, slot, :, 0:n],
                                        c.vcols[:, V_FIN:V_FIN + KT].unsqueeze(2).to_broadcast([P, KT, n]), ALU.mult
                                        ).then_inc(scaled, 1)
            with dve.Fori(0, NB // 2, 1) as pair:
                b = pair * 2
                scale_block(b, 0, P)
                scale_block(b + 1, 1, P)
            scale_block(NB, 0, DEC)

        @block.sync
        def _(sp):
            for s in stored:
                sp.sem_inc(s, 16)
            with sp.Fori(0, NB // 2, 1) as pair:
                b = pair * 2
                for slot in range(2):
                    sp.wait_ge(rowed, 2 * b + (2 * slot + 6))
                    sp.dma_start(y_out[bass.ds(b + slot, 1)].rearrange("a p d -> p (a d)"), rows[:, slot]
                                 ).then_inc(stored[slot], 16)
            sp.wait_ge(rowed, 2 * NB + 6)
            sp.dma_start(c.outs["y_sample"].rearrange("b s d -> (b s) d"), rows[0:DEC, 0]).then_inc(stored[0], 16)
            for slot in range(2):
                sp.wait_ge(stored[slot], 16 + 16 * last_store[slot])


class Area:

    def __init__(self, c, name, places):
        self.c, self.name, self.places = c, name, [list(p) for p in places]

    def __call__(self, name, shape, dt=F32):
        n = 4
        for s in shape[1:]:
            n *= s
        n = (n + 31) // 32 * 32
        for place in self.places:
            if place[0] + n <= place[1]:
                place[0] += n
                return self.c.at(f"{self.name}_{name}", shape, place[0] - n, dt)
        raise ValueError(f"no room for {name}: {self.places}")

    def passing(self, name):
        return Area(self.c, name, self.places)


def mixer_area(c, name):
    return Area(c, name, [(ACT_AT, WORK_AT), (c.scr_at, c.const_at)])


def is_first(b):
    return isinstance(b, int) and b == 0


def is_last(b):
    return isinstance(b, int) and b == NB


def in_turns(eng, turn):
    turn(0, 0)
    turn(1, 1)
    with eng.Fori(1, NB // 2, 1) as pair:
        b = pair * 2
        turn(b, 0)
        turn(b + 1, 1)
    turn(NB, 0)



def delta_prepare_phase(c, area):
    nc = c.nc
    a0 = c.ins
    rows = c.delta_rows = area("rows", [36, TOK])
    build_masks = level_masks(c, area, delta=True)
    brief = area.passing("delta_prepare")
    y, t1 = brief("gate_in", [8, TOK]), brief("gate_tmp", [8, TOK])
    mask = brief("chunk_mask", [8, TOK])
    gs = brief("gate_consts", [8, 4])
    loads, ready, step, actd = c.sem("gate_loads"), c.sem("gate_consts"), c.sem("gate_steps"), c.sem("gate_logs")
    squared, summed, logged = c.sem("unit_squares"), c.sem("unit_summed"), c.sem("unit_logged")
    factored, scaled = c.sem("unit_factored"), c.sem("unit_scaled")
    n = T_V - T_Q
    r, sq = brief("unit_factor", [P, n, TOK]), brief("unit_squares", [P, 2, TOK])
    with nc.Block() as block:
        @block.sync
        def _(sp):
            sp.wait_ge(ready, 6)
            sp.dma_start(gs[0:4, 1:2], a0["dn_dt_bias"].rearrange("e h -> h e")).then_inc(loads, 16)
            sp.dma_start(gs[0:4, 2:3], a0["dn_a_log"].rearrange("e h -> h e")).then_inc(loads, 16)

        @block.gpsimd
        def _(pool):
            g = nc.gpsimd
            g.memset(gs[:], -1.0).then_inc(ready, 1)
            g.memset(mask[:], 0.0).then_inc(ready, 1)
            g.memset(rows[:], 0.0).then_inc(ready, 1)
            pool.wait_ge(ready, 3)
            g.memset(gs[0:4, 0:1], 1.0).then_inc(ready, 1)
            g.memset(gs[:, 1:2], 0.0).then_inc(ready, 1)
            g.memset(mask[0:4, 0:SEQ].rearrange("p (c n) -> p c n", n=CHUNK)[:, :, 1:CHUNK], 1.0).then_inc(ready, 1)
            build_masks(pool)

        @block.scalar
        def _(act):
            act.wait_ge(loads, 32)
            nc.scalar.activation(gs[0:4, 2:3], gs[0:4, 2:3], ACT.Exp).then_inc(actd, 1)
            act.wait_ge(step, 3)
            nc.scalar.activation(t1[:], t1[:], ACT.Exp).then_inc(actd, 1)
            act.wait_ge(actd, 2)
            nc.scalar.activation(t1[:], t1[:], ACT.Ln, bias=c.ones[0:8, 0:1]).then_inc(actd, 1)
            for t in range(n):
                act.wait_ge(summed, t + 1)
                nc.scalar.activation(chunked(r[:, t]), tile_psum(c, t % 2), ACT.Ln, bias=c.eps[:]).then_inc(logged, 1)
            for t in range(n):
                act.wait_ge(logged, t + 1)
                nc.scalar.activation(r[:, t], r[:, t], ACT.Exp, scale=-0.5).then_inc(factored, 1)

        @block.tensor
        def _(pe):
            for t in range(n):
                pe.wait_ge(squared, t + 1)
                if t >= 2:
                    pe.wait_ge(logged, t - 1)
                for ch in range(NCH):
                    last = nc.tensor.matmul(c.ps[:, 3 * (t % 2) + ch, 0:CW], c.ones[:],
                                            sq[:, t % 2, ch * CW:(ch + 1) * CW], start=True, stop=True)
                last.then_inc(summed, 1)

        @block.vector
        def _(dve):
            v = nc.vector
            dve.wait_ge(actd, 1)
            dve.wait_ge(ready, 6)
            v.tensor_scalar(gs[0:4, 2:3], gs[0:4, 2:3], -1.0, None, ALU.mult).then_inc(step, 1)
            v.tensor_scalar(y[:], c.proj[0:8, T_AB, :], gs[:, 0:1], gs[:, 1:2], ALU.mult, ALU.add).then_inc(step, 1)
            dve.wait_ge(step, 2)
            v.scalar_tensor_tensor(out=t1[:], in0=y[:], scalar=-1.0, in1=y[:], op0=ALU.mult, op1=ALU.min
                                   ).then_inc(step, 1)
            dve.wait_ge(actd, 3)
            v.scalar_tensor_tensor(out=y[:], in0=y[:], scalar=0.0, in1=t1[:], op0=ALU.max, op1=ALU.add
                                   ).then_inc(step, 1)
            dve.wait_ge(step, 4)
            v.tensor_scalar(y[:], y[:], gs[:, 2:3], None, ALU.mult).then_inc(step, 1)
            dve.wait_ge(step, 5)
            v.tensor_tensor_scan(rows[0:8, :], mask[:], y[:], 0.0, ALU.mult, ALU.add).then_inc(step, 1)
            dve.wait_ge(step, 6)
            g4 = rows[0:4, 0:SEQ].rearrange("p (c n) -> p c n", n=CHUNK)
            v.tensor_tensor(rows[32:36, 0:SEQ].rearrange("p (c n) -> p c n", n=CHUNK),
                            g4[:, :, CHUNK - 1:CHUNK].to_broadcast([4, SEQ // CHUNK, CHUNK]), g4, ALU.subtract
                            ).then_inc(step, 1)
            for t in range(n):
                if t >= 2:
                    dve.wait_ge(summed, t - 1)
                x = c.proj[:, T_Q + t, :]
                v.tensor_tensor(sq[:, t % 2], x, x, ALU.mult).then_inc(squared, 1)
            for t in range(n):
                x = c.proj[:, T_Q + t, :]
                dve.wait_ge(factored, t + 1)
                v.scalar_tensor_tensor(out=x, in0=x, scalar=P ** -0.5 if t < T_K else 1.0, in1=r[:, t], op0=ALU.mult,
                                       op1=ALU.mult).then_inc(scaled, 1)



LEVELS = 6
BIG = -1e30


def level_masks(c, area, delta):
    nc = c.nc
    made = c.sem(f"{area.name}_masks_made")
    m = c.level_masks = area("level_masks", [P, LEVELS, P])
    if delta:
        m0 = c.level0_mask = area("level0_mask", [P, P])
        neg = c.causal_bias = area("causal", [P, P])
        sel = c.select = area("select", [8, 8, P])
    n = [0]

    def build(pool):
        g = nc.gpsimd

        def do(ins):
            ins.then_inc(made, 1)
            n[0] += 1
            pool.wait_ge(made, n[0])

        do(g.memset(m[:], 0.0))
        do(g.affine_select(out=m[:, 0].rearrange("p (b s) -> p b s", s=2)[:, :, 1],
                           in_=m[:, 0].rearrange("p (b s) -> p b s", s=2)[:, :, 1],
                           compare_op=ALU.not_equal, fill=-1.0, base=0, pattern=[[-2, P // 2]], channel_multiplier=1))
        for level in range(1, LEVELS):
            s = 2 ** level
            late = m[:, level].rearrange("p (b s) -> p b s", s=2 * s)[:, :, s:2 * s]
            do(g.memset(late, 1.0))
            do(g.affine_select(out=late, in_=late, compare_op=ALU.is_ge, fill=0.0, base=0,
                               pattern=[[-2 * s, P // (2 * s)], [0, s]], channel_multiplier=1))
            do(g.affine_select(out=late, in_=late, compare_op=ALU.is_ge, fill=0.0, base=s - 1,
                               pattern=[[2 * s, P // (2 * s)], [0, s]], channel_multiplier=-1))
        if delta:
            do(g.memset(m0[:], 0.0))
            do(g.memset(neg[:], 0.0))
            do(g.memset(sel[:], 0.0))
            do(g.affine_select(out=m0[:].rearrange("p (b s) -> p b s", s=2)[:, :, 0],
                               in_=m0[:].rearrange("p (b s) -> p b s", s=2)[:, :, 0],
                               compare_op=ALU.not_equal, fill=-1.0, base=-1, pattern=[[-2, P // 2]], channel_multiplier=1))
            do(g.affine_select(out=neg[:], in_=neg[:], compare_op=ALU.is_ge, fill=BIG, base=0, pattern=[[1, P]],
                               channel_multiplier=-1))
            do(g.affine_select(out=neg[:, CHUNK:P], in_=neg[:, CHUNK:P], compare_op=ALU.is_ge, fill=BIG, base=-CHUNK,
                               pattern=[[0, CHUNK]], channel_multiplier=1))
            do(g.affine_select(out=sel[:], in_=sel[:], compare_op=ALU.not_equal, fill=1.0, base=0,
                               pattern=[[-1, 8], [0, P]], channel_multiplier=1))
    return build


def heads(ap):
    return ap.rearrange("p (h n) -> p h n", h=HEADS)


def delta_phase(c, area):
    nc = c.nc
    H = HEADS
    rows, neg, sel = c.delta_rows, c.causal_bias, c.select

    def buf(name):
        return area(name, [P, H, P])

    def two(name):
        return area(name, [P, 2, H, P])
    kts, vts, dec, kbt, mt, tn, xs, tmp = (buf(n) for n in (
        "k_cols", "v_cols", "decay", "kb_cols", "m_t", "inv", "x", "inv_tmp"))
    bb, kbe, vnw = (buf(n) for n in ("beta_cols", "k_beta_decay", "v_new"))
    egb, qeg, att, kdc, vb, nw, tt = (two(n) for n in (
        "decay_cols", "q_decayed", "attention", "k_left", "v_beta", "minus_w", "inv_t"))
    ms = two("m_level")
    state = c.delta_state = buf("state")
    rs = area("rows_block", [36, P])
    cols, ecols, beg = area("cols", [P, 36]), area("exp_cols", [P, 36]), area("beta_decay", [P, 4])
    s = lambda n: c.sem("delta_" + n)
    names = ("k_staged v_staged rows_staged spread kn vn kk qk mn xm ym wt vm om dm cols egb bb dec x_copied nw o_out "
             "beg diff kbt qeg k_used vb mt att inv state v_copied ms").split()
    (k_staged, v_staged, rows_staged, spread, kn, vn, kk, qk, mn, xm, ym, wt, vm, om, dm, colsd, egbd, bbd, decd,
     x_copied, nwd, o_out, begd, diff, kbtd, qegd, k_used, vbd, mtd, attd, inv, stated, v_copied, msd) = map(s, names)
    stored, tmpd = c.sem("delta_stored"), c.sem("delta_inv_tmp")
    B = [heads(c.ps[:, n, :]) for n in range(8)]
    VM, OM, DM = B[3], B[4], B[0]
    L = LEVELS - 1
    INV = 3 + 4 * L - 2
    GROUPS = [slice(0, H // 2), slice(H // 2, H)]
    XB = [B[5], B[7]]
    YB = [heads(c.ps[:, 6, :]), heads(c.ps[:, 1, :])]
    eye = c.ident[:].unsqueeze(1).to_broadcast([P, H, P])

    def mask(ap):
        return ap.unsqueeze(1).to_broadcast([P, H, P])

    def col(ap):
        return ap.unsqueeze(2).to_broadcast([P, H, P])

    def chain_over(eng, b):
        if not is_first(b) and not is_first(b - 1):
            eng.wait_ge(stated, b * 8 - 7)
            eng.wait_ge(o_out, b * 2 - 2)

    with nc.Block() as block:
        @block.gpsimd
        def _(pool):
            g = nc.gpsimd

            def turn(b, slot):
                if is_last(b):
                    return
                tok = bass.ds(b * P, P)
                if not is_first(b):
                    reach(c, pool, kk, b * 1)
                g.tensor_copy(rs[:], rows[:, tok]).then_inc(rows_staged, 1)
                g.tensor_copy(kts[:], c.proj[:, T_K:T_K + H, tok]).then_inc(k_staged, 1)
                g.tensor_copy(vts[:], c.proj[:, T_V:T_V + H, tok]).then_inc(v_staged, 1)
                pool.wait_ge(mtd, b + 1)
                for level in range(1, LEVELS):
                    if level > 2:
                        pool.wait_ge(xm, b * 2 * L + (2 * level - 4))
                    elif not is_first(b):
                        pool.wait_ge(xm, b * 2 * L)
                    g.tensor_tensor(ms[:, level % 2], mt[:], mask(c.level_masks[:, level]), ALU.mult).then_inc(msd, 1)
            in_turns(pool, turn)

        @block.tensor
        def _(pe):
            t = nc.tensor

            def v_new(c1, a, slot):
                part = slice(a * CHUNK, (a + 1) * CHUNK)
                if a:
                    reach(c, pe, stated, c1 * 8 + 5)
                else:
                    reach(c, pe, nwd, c1 + 1)
                    reach(c, pe, stated, c1 * 8 + 1)
                for h in range(H):
                    t.matmul(VM[part, h], tt[part, slot, h, part], vb[part, slot, h], start=True, stop=False)
                    last = t.matmul(VM[part, h], nw[:, slot, h, part], state[:, h], start=False, stop=True)
                last.then_inc(vm, 1)

            def out_and_state(c1, a, slot):
                part = slice(a * CHUNK, (a + 1) * CHUNK)
                pe.wait_ge(v_copied, c1 * 2 + (a + 1))
                if a:
                    pe.wait_ge(o_out, c1 * 2 + 1)
                for h in range(H):
                    t.matmul(OM[:, h, 0:CHUNK], state[:, h], qeg[:, slot, h, part], start=True, stop=False)
                    last = t.matmul(OM[:, h, 0:CHUNK], vnw[part, h], att[part, slot, h, part], start=False, stop=True)
                last.then_inc(om, 1)
                for h in range(H):
                    last = t.matmul(DM[:, h], kdc[part, slot, h], vnw[part, h], start=True, stop=True)
                last.then_inc(dm, 1)

            def turn(b, slot):
                chain = not is_first(b)
                if is_last(b):
                    for a in range(2):
                        v_new(b - 1, a, 1 - slot)
                        out_and_state(b - 1, a, 1 - slot)
                    return
                tok = bass.ds(b * P, P)
                chain_over(pe, b)
                if chain:
                    pe.wait_ge(inv, b * INV)
                    pe.wait_ge(x_copied, b * 2 * L)
                reach(c, pe, rows_staged, b + 1)
                t.transpose(c.ps[:, 0, 0:36], rs[:], c.ident[0:36, 0:36]).then_inc(spread, 1)
                for first, bank in ((0, 1), (H, 2)):
                    for h in range(H):
                        last = t.matmul(B[bank][:, h], sel[:, first + h], rows[0:8, tok], start=True, stop=True)
                    last.then_inc(spread, 1)
                pe.wait_ge(k_staged, b + 1)
                for h in range(H):
                    last = t.transpose(B[5][:, h], kts[:, h], c.ident[:])
                last.then_inc(kn, 1)
                pe.wait_ge(v_staged, b + 1)
                for h in range(H):
                    last = t.transpose(B[6][:, h], vts[:, h], c.ident[:])
                last.then_inc(vn, 1)
                for h in range(H):
                    last = t.matmul(B[4][:, h], kts[:, h], c.proj[:, T_Q + h, tok], start=True, stop=True)
                last.then_inc(qk, 1)
                pe.wait_ge(kbtd, b + 1)
                for h in range(H):
                    last = t.matmul(B[3][:, h], kts[:, h], kbt[:, h], start=True, stop=True)
                last.then_inc(kk, 1)
                pe.wait_ge(mtd, b + 1)
                pe.wait_ge(k_used, b * 2 + 2)
                for h in range(H):
                    last = t.transpose(B[5][:, h], mt[:, h], c.ident[:])
                last.then_inc(mn, 1)
                for level in range(1, LEVELS):
                    pe.wait_ge(msd, b * L + level)
                    for n, group in enumerate(GROUPS):
                        pe.wait_ge(inv, b * INV + (3 if level == 1 else 4 * level - 5 + 2 * (n + 1)))
                        if level == 1 and n and chain:
                            pe.wait_ge(nwd, b * 1)
                        for h in range(H)[group]:
                            last = t.matmul(XB[n][:, h], ms[:, level % 2, h], tn[:, h], start=True, stop=True)
                        last.then_inc(xm, 1)
                    if chain and level in (1, 3):
                        if level == 1:
                            pe.wait_ge(attd, b + 1)
                        v_new(b - 1, level // 2, 1 - slot)
                    if chain and level in (2, 4):
                        out_and_state(b - 1, level // 2 - 1, 1 - slot)
                    for n, group in enumerate(GROUPS):
                        pe.wait_ge(x_copied, b * 2 * L + (2 * level - 1 + n))
                        if level == 1:
                            pe.wait_ge(vbd, b + 1)
                        if level < L:
                            for i, h in enumerate(range(H)[group]):
                                t.matmul(YB[n][:, i], tt[:, slot, h], xs[:, h], start=True, stop=True)
                        for i, h in enumerate(range(H)[group]):
                            last = t.matmul(YB[n][:, 2 + i], xs[:, h], tt[:, slot, h], start=True, stop=True)
                        last.then_inc(ym, 1)
                pe.wait_ge(inv, b * INV + INV)
                for h in range(H):
                    last = t.matmul(B[7][:, h], kbe[:, h], tt[:, slot, h], start=True, stop=True)
                last.then_inc(wt, 1)
            in_turns(pe, turn)

        @block.scalar
        def _(act):
            def a(*args, **kw):
                return nc.scalar.activation(*args, **kw)

            def o_rows(c1, n):
                reach(c, act, om, c1 * 2 + (n + 1))
                a(c.proj[:, T_Q:T_Q + H, bass.ds(c1 * P + n * CHUNK, CHUNK)], OM[:, :, 0:CHUNK], ACT.Copy
                  ).then_inc(o_out, 1)

            def turn(b, slot):
                chain = not is_first(b)
                if is_last(b):
                    o_rows(b - 1, 0)
                    o_rows(b - 1, 1)
                    return
                chain_over(act, b)
                act.wait_ge(spread, b * 3 + 1)
                if chain:
                    act.wait_ge(vbd, b * 1)
                a(cols[:], c.ps[:, 0, 0:36], ACT.Copy).then_inc(colsd, 1)
                a(ecols[:], c.ps[:, 0, 0:36], ACT.Exp).then_inc(colsd, 1)
                act.wait_ge(spread, b * 3 + 2)
                a(egb[:, slot], B[1], ACT.Exp).then_inc(egbd, 1)
                act.wait_ge(spread, b * 3 + 3)
                a(bb[:], B[2], ACT.Exp).then_inc(bbd, 1)
                act.wait_ge(diff, b * H + H)
                a(dec[:], dec[:], ACT.Exp).then_inc(decd, 1)
                for level in range(1, LEVELS):
                    for n, group in enumerate(GROUPS):
                        act.wait_ge(xm, b * 2 * L + (2 * level - 1 + n))
                        if level > 1 or chain:
                            act.wait_ge(ym, b * 2 * L + (2 * level - 3 + n))
                        a(xs[:, group], XB[n][:, group], ACT.Copy).then_inc(x_copied, 1)
                    if chain and level in (3, 5):
                        o_rows(b - 1, level // 2 - 1)
                act.wait_ge(wt, b + 1)
                a(nw[:, slot], B[7], ACT.Copy, scale=-1.0).then_inc(nwd, 1)
            in_turns(act, turn)

        @block.vector
        def _(dve):
            v = nc.vector
            v.memset(state[:], 0.0).then_inc(stated, 1)

            def take_v(c1, n):
                part = slice(n * CHUNK, (n + 1) * CHUNK)
                dve.wait_ge(vm, c1 * 2 + (n + 1))
                v.tensor_copy(vnw[part], VM[part]).then_inc(v_copied, 1)

            def new_state(c1, n, slot):
                dve.wait_ge(dm, c1 * 2 + (n + 1))
                for h in range(H):
                    v.scalar_tensor_tensor(out=state[:, h], in0=state[:, h],
                                           scalar=egb[:, slot, h, n * CHUNK + CHUNK - 1:n * CHUNK + CHUNK],
                                           in1=DM[:, h], op0=ALU.mult, op1=ALU.add).then_inc(stated, 1)

            def turn(b, slot):
                chain = not is_first(b)
                if is_last(b):
                    for n in range(2):
                        take_v(b - 1, n)
                        new_state(b - 1, n, 1 - slot)
                    return
                tok = bass.ds(b * P, P)
                dve.wait_ge(colsd, b * 2 + 2)
                v.tensor_tensor(beg[:], ecols[:, 0:H], ecols[:, H:2 * H], ALU.mult).then_inc(begd, 1)
                dve.wait_ge(egbd, b + 1)
                for h in range(H):
                    v.scalar_tensor_tensor(out=dec[:, h], in0=B[1][:, h], scalar=cols[:, h:h + 1], in1=neg[:],
                                           op0=ALU.subtract, op1=ALU.add).then_inc(diff, 1)
                dve.wait_ge(bbd, b + 1)
                dve.wait_ge(k_staged, b + 1)
                v.tensor_tensor(kbt[:], kts[:], bb[:], ALU.mult).then_inc(kbtd, 1)
                dve.sem_inc(c.passed[dve.engine], 1)
                v.tensor_tensor(qeg[:, slot], c.proj[:, T_Q:T_Q + H, tok], egb[:, slot], ALU.mult).then_inc(qegd, 1)
                dve.wait_ge(kn, b + 1)
                dve.wait_ge(begd, b + 1)
                if chain:
                    dve.wait_ge(wt, b * 1)
                v.tensor_tensor(kbe[:], B[5], col(beg[:]), ALU.mult).then_inc(k_used, 1)
                v.tensor_tensor(kdc[:, slot], B[5], col(ecols[:, 32:36]), ALU.mult).then_inc(k_used, 1)
                dve.wait_ge(vn, b + 1)
                v.tensor_tensor(vb[:, slot], B[6], col(ecols[:, H:2 * H]), ALU.mult).then_inc(vbd, 1)
                dve.wait_ge(decd, b + 1)
                dve.wait_ge(kk, b + 1)
                v.tensor_tensor(mt[:], B[3], dec[:], ALU.mult).then_inc(mtd, 1)
                dve.wait_ge(mtd, b + 1)
                v.tensor_tensor(tmp[:], mt[:], mask(c.level_masks[:, 0]), ALU.mult).then_inc(tmpd, 1)
                dve.wait_ge(tmpd, b + 1)
                v.tensor_tensor(tt[:, slot], tmp[:], eye, ALU.add).then_inc(inv, 1)
                dve.wait_ge(mn, b + 1)
                dve.wait_ge(inv, b * INV + 1)
                v.tensor_tensor(tmp[:], B[5], mask(c.level0_mask[:]), ALU.mult).then_inc(inv, 1)
                dve.wait_ge(inv, b * INV + 2)
                v.tensor_tensor(tn[:], tmp[:], eye, ALU.add).then_inc(inv, 1)
                dve.wait_ge(qk, b + 1)
                v.tensor_tensor(att[:, slot], B[4], dec[:], ALU.mult).then_inc(attd, 1)
                for level in range(1, LEVELS):
                    if chain and level in (1, 3):
                        take_v(b - 1, level // 2)
                    for n, group in enumerate(GROUPS):
                        dve.wait_ge(ym, b * 2 * L + (2 * level - 1 + n))
                        if level < L:
                            v.tensor_tensor(tn[:, group], tn[:, group], YB[n][:, 0:2], ALU.subtract).then_inc(inv, 1)
                        v.tensor_tensor(tt[:, slot, group], tt[:, slot, group], YB[n][:, 2:4], ALU.subtract
                                        ).then_inc(inv, 1)
                    if chain and level in (2, 4):
                        new_state(b - 1, level // 2 - 1, 1 - slot)
            in_turns(dve, turn)

        @block.sync
        def _(sp):
            sp.wait_ge(stated, 1 + 8 * NB)
            sp.dma_start(c.outs["p_state_dn"].rearrange("e b h k v -> k (e b h) v"), state[:]).then_inc(stored, 16)
            sp.wait_ge(stored, 16)


class Steps:

    def __init__(self, sem):
        self.sem, self.n = sem, 0

    def __call__(self, ins):
        ins.then_inc(self.sem, 1)
        self.n += 1
        return self.n



def delta_sample_phase(c, area):
    nc = c.nc
    H, U = HEADS, DEC * HEADS
    states = area("sample_states", [P, U, P])
    ee, dots = area("sample_gates", [P, 8, DEC]), area("qk_dots", [P, H, DEC])
    both = area("state_products", [P, DEC, H, 2])
    prod, tmp, vnew = area("qk_products", [P, H, DEC]), area("sample_tmp", [P, H, DEC]), area("sample_v_new", [P, H, DEC])
    diag = area("v_diagonals", [P, 2, H, P])
    s = lambda n: c.sem("ds_" + n)
    loaded, spread, expd, prodd, dotted, mult, taken = map(s, "loaded spread exp prod dotted multiplied taken".split())
    made, decayed, diagd, wide, new = map(s, "v_made decayed diag wide new".split())
    stored, tails_in, tail_rows, tail_out = c.sem("ds_stored"), c.sem("tails_kept"), c.sem("tail_rows"), c.sem("tail_stored")
    tailr = area("tail_rows", [CONV - 1 + DEC, 12, P])
    q = c.proj[:, T_Q:T_Q + H, SEQ:TOK]
    k = c.proj[:, T_K:T_K + H, SEQ:TOK]
    vv = c.proj[:, T_V:T_V + H, SEQ:TOK]
    eg, beta = ee[:, 0:H], ee[:, H:2 * H]
    by_head = both[:].rearrange("p b h n -> p n h b")
    with nc.Block() as block:
        @block.sync
        def _(sp):
            sp.dma_start(states[:], c.ins["state_dn"].rearrange("e b h k v -> k (e b h) v")).then_inc(loaded, 16)
            old = c.ins["state_dn_conv"].rearrange("e b i c -> (e b) i c")
            conv_out = c.outs["s_state_dn_conv"].rearrange("e b i c -> (e b) i c")
            sp.dma_start(conv_out[:, 0:CONV - 2, :], old[:, 1:CONV - 1, :]).then_inc(tail_out, 16)
            sp.wait_ge(tail_rows, 3 + 3)
            sp.dma_start(c.outs["p_state_dn_conv"].rearrange("e b i c -> (e b i) c"),
                         tailr[0:CONV - 1].rearrange("p t n -> p (t n)")).then_inc(tail_out, 16)
            sp.dma_start(conv_out[:, CONV - 2, :], tailr[CONV - 1:].rearrange("p t n -> p (t n)")
                         ).then_inc(tail_out, 16)
            with sp.Fori(0, DEC, 1) as b:
                sp.wait_ge(new, b * H + H)
                sp.dma_start(c.outs["s_state_dn"].rearrange("e b h k v -> k (e b) h v")[:, bass.ds(b, 1)]
                             .rearrange("k b h v -> k (b h) v"), states[:, bass.ds(b * H, H), :]).then_inc(stored, 16)
            sp.wait_ge(stored, 16 * DEC)
            sp.wait_ge(tail_out, 48)

        @block.tensor
        def _(pe):
            t = nc.tensor
            for r in range(8):
                last = t.matmul(c.ps[:, 0, r * DEC:(r + 1) * DEC], c.select[:, r], c.delta_rows[0:8, SEQ:TOK],
                                start=True, stop=True)
            last.then_inc(spread, 1)
            pe.wait_ge(prodd, 1)
            t.matmul(c.ps[:, 1, 0:U], c.ones[:], prod[:], start=True, stop=True).then_inc(dotted, 1)
            for g3 in range(3):
                for n in range(4):
                    last = t.transpose(c.ps[0:CONV - 1 + DEC, 2 + g3, n * P:(n + 1) * P], c.tail[:, 4 * g3 + n, :],
                                       c.ident[:])
                last.then_inc(tail_rows, 1)
            pe.wait_ge(loaded, 16)
            for b in range(DEC):
                for h in range(H):
                    u = b * H + h
                    last = t.matmul(c.ps[:, 5, 2 * u:2 * u + 2], states[:, u],
                                    c.proj[:, T_Q + h:T_K + h + 1:T_K - T_Q, SEQ + b], start=True, stop=True)
            last.then_inc(mult, 1)
            for b in range(DEC):
                pe.wait_ge(diagd, b + 1)
                if b >= 2:
                    pe.wait_ge(new, H * (b - 1))
                t.matmul(c.ps[:, 6 + b % 2, :], c.ones[:], diag[:, b % 2], start=True, stop=True).then_inc(wide, 1)

        @block.scalar
        def _(act):
            act.wait_ge(spread, 1)
            nc.scalar.activation(ee[:], c.ps[:, 0, 0:64], ACT.Exp).then_inc(expd, 1)
            act.wait_ge(tail_rows, 3)
            for g3 in range(3):
                nc.scalar.activation(tailr[:, 4 * g3:4 * g3 + 4], c.ps[0:CONV - 1 + DEC, 2 + g3, :], ACT.Copy
                                     ).then_inc(tail_rows, 1)
            act.wait_ge(expd, 1)
            act.wait_ge(mult, 1)
            for b in range(DEC):
                for h in range(H):
                    u = b * H + h
                    nc.scalar.activation(states[:, u], states[:, u], ACT.Copy, scale=eg[:, h, b:b + 1]
                                         ).then_inc(decayed, 1)

        @block.vector
        def _(dve):
            v = nc.vector
            own = Steps(c.sem("ds_steps"))
            v.tensor_tensor(prod[:], q, k, ALU.mult).then_inc(prodd, 1)
            dve.wait_ge(dotted, 1)
            own(v.tensor_copy(dots[:], c.ps[:, 1, 0:U]))
            dve.wait_ge(mult, 1)
            n = own(v.tensor_copy(both[:], c.ps[:, 5, 0:2 * U]))
            dve.wait_ge(expd, 1)
            dve.wait_ge(own.sem, n)
            n = own(v.tensor_tensor(tmp[:], by_head[:, 1], eg, ALU.mult))
            dve.wait_ge(own.sem, n)
            n = own(v.tensor_tensor(vnew[:], vv, tmp[:], ALU.subtract))
            dve.wait_ge(own.sem, n)
            n = own(v.tensor_tensor(vnew[:], vnew[:], beta, ALU.mult))
            m = own(v.tensor_tensor(tmp[:], by_head[:, 0], eg, ALU.mult))
            dve.wait_ge(own.sem, m)
            n = own(v.tensor_tensor(prod[:], vnew[:], dots[:], ALU.mult))
            dve.wait_ge(own.sem, n)
            own(v.tensor_tensor(q, tmp[:], prod[:], ALU.add))

            def update(b):
                dve.wait_ge(wide, b + 1)
                dve.wait_ge(decayed, (b + 1) * H)
                for h in range(H):
                    v.scalar_tensor_tensor(out=states[:, b * H + h], in0=c.ps[:, 6 + b % 2, h * P:(h + 1) * P],
                                           scalar=k[:, h, b:b + 1], in1=states[:, b * H + h], op0=ALU.mult,
                                           op1=ALU.add).then_inc(new, 1)
            for b in range(DEC):
                if b >= 2:
                    dve.wait_ge(wide, b - 1)
                v.tensor_tensor(diag[:, b % 2], c.ident[:].unsqueeze(1).to_broadcast([P, H, P]),
                                vnew[:, :, b:b + 1].to_broadcast([P, H, P]), ALU.mult).then_inc(diagd, 1)
                if b >= 1:
                    update(b - 1)
            update(DEC - 1)



W2 = 2 * P
BY_HALF = [2 * i + r for r in range(2) for i in range(SWH // 2)]


def window_masks_phase(c, area):
    nc = c.nc
    bias = c.window_bias = area("bias", [P, SWH, W2])
    ksw = c.k_swapped = area("k_swapped", [P, TOK])
    sinks = c.sinks = area("sinks", [P, SWH])
    brief = area.passing("window_masks")
    rel, forbid = brief("distance", [P, W2]), brief("forbidden", [P, W2])
    sinks_in = brief("sinks_in", [P, SWH])
    made, biased, swapped, loaded = c.sem("wm_made"), c.sem("wm_biased"), c.sem("k_swapped"), c.sem("sinks_in")
    with nc.Block() as block:
        @block.sync
        def _(sp):
            sp.dma_start(sinks_in[:], c.ins["sw_sinks"].rearrange("e h -> (e h)").partition_broadcast(P)
                         ).then_inc(loaded, 16)
            sp.wait_ge(loaded, 16)

        @block.gpsimd
        def _(pool):
            g = nc.gpsimd
            g.iota(rel[:], pattern=[[-1, W2]], base=P, channel_multiplier=1, allow_small_or_imprecise_dtypes=True
                   ).then_inc(made, 1)
            g.memset(forbid[:], 0.0).then_inc(made, 1)
            pool.wait_ge(made, 2)
            g.affine_select(out=forbid[:], in_=forbid[:], compare_op=ALU.is_ge, fill=BIG, base=P, pattern=[[-1, W2]],
                            channel_multiplier=1).then_inc(made, 1)
            pool.wait_ge(made, 3)
            g.affine_select(out=forbid[:], in_=forbid[:], compare_op=ALU.is_gt, fill=BIG, base=0, pattern=[[1, W2]],
                            channel_multiplier=-1).then_inc(made, 1)

        @block.vector
        def _(dve):
            dve.wait_ge(made, 4)
            for n, h in enumerate(BY_HALF):
                nc.vector.scalar_tensor_tensor(out=bias[:, n], in0=rel[:], scalar=-2.0 ** -(h + 1), in1=forbid[:],
                                               op0=ALU.mult, op1=ALU.add).then_inc(biased, 1)
            dve.wait_ge(loaded, 16)
            nc.vector.tensor_copy(sinks[:].rearrange("p (r i) -> p r i", r=2),
                                  sinks_in[:].rearrange("p (i r) -> p r i", r=2)).then_inc(biased, 1)

        @block.scalar
        def _(act):
            for a in range(2):
                nc.scalar.activation(ksw[a * HD:(a + 1) * HD, :], c.proj[(1 - a) * HD:(2 - a) * HD, T_SK, :], ACT.Copy
                                     ).then_inc(swapped, 1)


def window_phase(c, area):
    nc = c.nc
    bias, ksw, sinks = c.window_bias, c.k_swapped, c.sinks
    qs, ks = area("q_block", [P, 2, 4, P]), area("k_block", [P, 2, 2, W2])
    vs, vn = area("v_block", [P, 2, P]), area("v_rows", [P, 2, P])
    sc, pt = area("scores", [P, 2, SWH, W2]), area("probs_cols", [P, SWH, 2, P])
    mx, nm, sums, es, rd = (area(n, [P, SWH]) for n in ("max", "minus_max", "sums", "sink_exp", "rden"))
    kr = area("k_rows", [P, P])
    s = lambda n: c.sem("w_" + n)
    staged, vt, scored, biased, stat, expd, turned, ptd, od, odone, vrow = map(s, (
        "staged v_turned scored biased stats exp turned probs_out o o_out v_row").split())
    stored, nmd = s("stored"), s("minus_max")
    k_turned, k_out = s("k_turned"), s("k_out")
    ST = 6

    with nc.Block() as block:
        @block.gpsimd
        def _(pool):
            g = nc.gpsimd

            def turn(b, slot):
                if is_last(b):
                    return
                first = is_first(b)
                lo = P if first else 0
                keys = slice(0, P) if first else bass.ds((b - 1) * P, W2)
                tok = bass.ds(b * P, P)
                if not is_first(b - 1) and not first:
                    reach(c, pool, scored, b * 4 - 4)
                    reach(c, pool, vt, b - 1)
                g.tensor_copy(qs[:, slot], c.proj[:, T_SQ:T_SQ + 4, tok]).then_inc(staged, 1)
                g.tensor_copy(ks[:, slot, 0, lo:], c.proj[:, T_SK, keys]).then_inc(staged, 1)
                g.tensor_copy(ks[:, slot, 1, lo:], ksw[:, keys]).then_inc(staged, 1)
                g.tensor_copy(vs[:, slot], c.proj[:, T_SV, tok]).then_inc(staged, 1)
            in_turns(pool, turn)

        @block.tensor
        def _(pe):
            t = nc.tensor

            def scores(b, slot):
                lo = P if is_first(b) else 0
                pe.wait_ge(staged, b * 4 + 4)
                if not is_first(b):
                    pe.wait_ge(biased, b * 4)
                for i, h in enumerate(BY_HALF):
                    p0, kv = HD * (h % 2), h // 4
                    rows = slice(p0, p0 + HD)
                    last = t.matmul(c.ps[:, i // 2, (i % 2) * W2 + lo:(i % 2) * W2 + W2], qs[rows, slot, h // 2],
                                    ks[rows, slot, int(kv != h % 2), lo:], start=True, stop=True)
                    if i % 2:
                        last.then_inc(scored, 1)

            def values(b, slot):
                first = is_first(b)
                for h in range(SWH):
                    if h % 2 == 0:
                        pe.wait_ge(stat, b * ST + ST)
                        if h >= 4:
                            pe.wait_ge(ptd, b * 4 + (h // 2 - 1))
                        elif not first:
                            pe.wait_ge(ptd, b * 4)
                    for a in range(1 if first else 0, 2):
                        last = t.transpose(c.ps[:, 5 + (h // 2) % 2, (2 * (h % 2) + a) * P:(2 * (h % 2) + a + 1) * P],
                                           sc[:, slot, h, a * P:(a + 1) * P], c.ident[:])
                    if h % 2:
                        last.then_inc(turned, 1)
                pe.wait_ge(ptd, b * 4 + 4)
                pe.wait_ge(vrow, b + 1)
                if not first:
                    pe.wait_ge(odone, b * 1)
                for i, h in enumerate(BY_HALF):
                    p0, kv = HD * (h % 2), h // 4
                    for a in range(1 if first else 0, 2):
                        last = t.matmul(c.ps[p0:p0 + HD, 7, (h // 2) * P:(h // 2 + 1) * P],
                                        vn[:, slot if a else 1 - slot, kv * HD:(kv + 1) * HD], pt[:, i, a],
                                        start=first or a == 0, stop=a == 1)
                last.then_inc(od, 1)

            def turn(b, slot):
                if not is_last(b):
                    scores(b, slot)
                if not is_first(b):
                    values(b - 1, 1 - slot)
                if not is_last(b):
                    if not is_first(b):
                        pe.wait_ge(vrow, b * 1)
                    t.transpose(c.ps[:, 4, 0:P], vs[:, slot], c.ident[:]).then_inc(vt, 1)
            in_turns(pe, turn)
            t.transpose(c.ps[:, 4, P:2 * P], ks[:, (NB - 1) % 2, 0, P:W2], c.ident[:]).then_inc(k_turned, 1)

        @block.scalar
        def _(act):
            def turn(b, slot):
                lo = P if is_first(b) else 0
                if not is_first(b):
                    c1, a = b - 1, int(is_first(b - 1))
                    for j in range(4):
                        act.wait_ge(turned, c1 * 4 + (j + 1))
                        nc.scalar.activation(pt[:, 2 * j:2 * j + 2, a:],
                                             c.ps[:, 5 + j % 2, :].rearrange("p (h a n) -> p h a n", h=2, a=2)[:, :, a:],
                                             ACT.Copy).then_inc(ptd, 1)
                if not is_last(b):
                    act.wait_ge(stat, b * ST + 3)
                    for h in range(SWH):
                        nc.scalar.activation(sc[:, slot, h, lo:], sc[:, slot, h, lo:], ACT.Exp, bias=nm[:, h:h + 1],
                                             accum_out=sums[:, h:h + 1]).then_inc(expd, 1)
                    nc.scalar.activation(es[:], es[:], ACT.Exp).then_inc(expd, 1)
                if not is_first(b):
                    reach(c, act, od, b * 1)
                    nc.scalar.activation(c.proj[:, T_SQ:T_SQ + 4, bass.ds((b - 1) * P, P)],
                                         c.ps[:, 7, :].rearrange("p (t n) -> p t n", t=4), ACT.Copy).then_inc(odone, 1)
            in_turns(act, turn)

        @block.vector
        def _(dve):
            v = nc.vector

            def turn(b, slot):
                if is_last(b):
                    return
                first = is_first(b)
                lo = P if first else 0
                for j in range(4):
                    dve.wait_ge(scored, b * 4 + (j + 1))
                    v.scalar_tensor_tensor(out=sc[:, slot, 2 * j:2 * j + 2, lo:],
                                           in0=c.ps[:, j, :].rearrange("p (h n) -> p h n", h=2)[:, :, lo:],
                                           scalar=HD ** -0.5, in1=bias[:, 2 * j:2 * j + 2, lo:], op0=ALU.mult,
                                           op1=ALU.add).then_inc(biased, 1)
                dve.wait_ge(biased, b * 4 + 4)
                v.tensor_reduce(mx[:], sc[:, slot, :, lo:], AX.X, ALU.max).then_inc(stat, 1)
                dve.wait_ge(stat, b * ST + 1)
                v.tensor_tensor(mx[:], mx[:], sinks[:], ALU.max).then_inc(stat, 1)
                dve.wait_ge(stat, b * ST + 2)
                v.tensor_scalar(nm[:], mx[:], -1.0, None, ALU.mult).then_inc(nmd, 1)
                v.tensor_tensor(es[:], sinks[:], mx[:], ALU.subtract).then_inc(stat, 1)
                dve.wait_ge(expd, b * 9 + 9)
                v.tensor_tensor(sums[:], sums[:], es[:], ALU.add).then_inc(stat, 1)
                dve.wait_ge(stat, b * ST + 4)
                v.reciprocal(rd[:], sums[:]).then_inc(stat, 1)
                dve.wait_ge(stat, b * ST + 5)
                v.tensor_tensor(sc[:, slot, :, lo:], sc[:, slot, :, lo:],
                                rd[:].unsqueeze(2).to_broadcast([P, SWH, W2 - lo]), ALU.mult).then_inc(stat, 1)
                if not first:
                    dve.wait_ge(od, b * 1)
                dve.wait_ge(vt, b + 1)
                v.tensor_copy(vn[:, slot], c.ps[:, 4, 0:P]).then_inc(vrow, 1)
            in_turns(dve, turn)
            dve.wait_ge(k_turned, 1)
            v.tensor_copy(kr[:], c.ps[:, 4, P:2 * P]).then_inc(k_out, 1)

        @block.sync
        def _(sp):
            sp.wait_ge(vrow, NB)
            sp.dma_start(c.outs["p_cache_swa_v"].rearrange("e b w g d -> (e b w) (g d)"), vn[:, (NB - 1) % 2]
                         ).then_inc(stored, 16)
            sp.wait_ge(k_out, 1)
            sp.dma_start(c.outs["p_cache_swa_k"].rearrange("e b w g d -> (e b w) (g d)"), kr[:]).then_inc(stored, 16)
            sp.wait_ge(stored, 32)



def window_sample_phase(c, area):
    nc = c.nc
    G, J, U = KVH, SWH // KVH, DEC * KVH
    kc, vc = area("k_cache", [P, DEC, P]), area("v_cache", [P, DEC, P])
    kt = area("k_cache_cols", [P, DEC, P])
    news = area("new_rows", [DEC, 2, P])
    qg = area("q_groups", [P, J, DEC])
    sc, rel = area("sample_scores", [J, U, P]), area("sample_distance", [J, P])
    slope, sk = area("slopes", [J, G]), area("sample_sinks", [J, G])
    bias = area("sample_bias", [J, G, P])
    mx, es, sums = area("sample_max", [J, U]), area("sample_sink_exp", [J, U]), area("sample_sums", [J, U])
    pt = area("sample_probs", [P, U, J])
    s = lambda n: c.sem("ws_" + n)
    loaded, made, new_t, new_out, placed, kturn, kcopied, qd = map(s, (
        "loaded made new_turned new_out placed k_turned k_copied q_grouped").split())
    scored, actd, pturn, ptd, od, stored = map(s, "scored exp p_turned p_out o stored".split())
    steps, biasd = s("steps"), s("bias")
    LAST = 10
    by_unit = lambda ap: ap.rearrange("p (g b) -> p g b", g=G)
    with nc.Block() as block:
        @block.sync
        def _(sp):
            by_group = c.ins["sw_sinks"].rearrange("e (g j a) -> (e g) j a", g=G, a=1)
            for grp in range(G):
                sp.dma_start(sk[:, grp:grp + 1], by_group[grp]).then_inc(loaded, 16)
            for cache, name in ((kc, "cache_swa_k"), (vc, "cache_swa_v")):
                sp.dma_start(cache[0:P - 1], c.ins[name].rearrange("e b w g d -> w (e b) (g d)")[1:P]
                             ).then_inc(loaded, 16)
            sp.wait_ge(new_out, 1)
            for b in range(DEC):
                sp.dma_start(vc[P - 1:P, b, :], news[b:b + 1, 1, :]).then_inc(placed, 16)
            sp.wait_ge(loaded, 64)
            for n, (cache, name) in enumerate(((kc, "s_cache_swa_k"), (vc, "s_cache_swa_v"))):
                rows = c.outs[name].rearrange("e b w g d -> w (e b) (g d)")
                sp.dma_start(rows[0:P - 1], cache[0:P - 1]).then_inc(stored, 16)
                sp.dma_start(rows[P - 1], news[:, n, :]).then_inc(stored, 16)
            sp.wait_ge(stored, 64)

        @block.gpsimd
        def _(pool):
            g = nc.gpsimd
            g.iota(rel[:], pattern=[[-1, P]], base=P - 1, channel_multiplier=0, allow_small_or_imprecise_dtypes=True
                   ).then_inc(made, 1)
            g.memset(slope[:], 0.0).then_inc(made, 1)
            n = 2
            for j in range(J):
                for grp in range(G):
                    pool.wait_ge(made, n)
                    g.affine_select(out=slope[:, grp:grp + 1], in_=slope[:, grp:grp + 1], compare_op=ALU.not_equal,
                                    fill=-2.0 ** -(J * grp + j + 1), base=-j, pattern=[[0, 1]], channel_multiplier=1
                                    ).then_inc(made, 1)
                    n += 1

        @block.tensor
        def _(pe):
            t = nc.tensor
            for n in range(2):
                last = t.transpose(c.ps[0:DEC, 0, n * P:(n + 1) * P], c.proj[:, T_SK + n, SEQ:TOK], c.ident[:])
            last.then_inc(new_t, 1)
            pe.wait_ge(loaded, 64)
            for b in range(DEC):
                last = t.transpose(c.ps[:, 1 + b // 4, (b % 4) * P:(b % 4 + 1) * P - 1], kc[0:P - 1, b],
                                   c.ident[0:P - 1, 0:P - 1])
                if b % 4 == 3:
                    last.then_inc(kturn, 1)
            pe.wait_ge(kcopied, 3)
            pe.wait_ge(qd, 4)
            for grp in range(G):
                for b in range(DEC):
                    u = grp * DEC + b
                    rows = slice(grp * HD, (grp + 1) * HD)
                    last = t.matmul(c.ps[0:J, 3 + u // 4, (u % 4) * P:(u % 4 + 1) * P], qg[rows, :, b], kt[rows, b],
                                    start=True, stop=True)
            last.then_inc(scored, 1)
            pe.wait_ge(steps, LAST)
            for u in range(U):
                last = t.transpose(c.ps[:, 1, u * J:(u + 1) * J], sc[:, u], c.ident[0:J, 0:J])
            last.then_inc(pturn, 1)
            pe.wait_ge(ptd, 1)
            pe.wait_ge(placed, 16 * DEC)
            for b in range(DEC):
                for grp in range(G):
                    rows = slice(grp * HD, (grp + 1) * HD)
                    last = t.matmul(c.ps[rows, 2, b * J:(b + 1) * J], vc[:, b, rows], pt[:, grp * DEC + b], start=True,
                                    stop=True)
            last.then_inc(od, 1)

        @block.scalar
        def _(act):
            act.wait_ge(new_t, 1)
            nc.scalar.activation(news[:], c.ps[0:DEC, 0, 0:2 * P], ACT.Copy).then_inc(new_out, 1)
            nc.scalar.activation(kt[:, :, P - 1], c.proj[:, T_SK, SEQ:TOK], ACT.Copy).then_inc(kcopied, 1)
            for n in range(2):
                act.wait_ge(kturn, n + 1)
                nc.scalar.activation(kt[:, 4 * n:4 * n + 4, 0:P - 1],
                                     c.ps[:, 1 + n, :].rearrange("p (b n) -> p b n", n=P)[:, :, 0:P - 1], ACT.Copy
                                     ).then_inc(kcopied, 1)
            act.wait_ge(steps, 6)
            nc.scalar.activation(sc[:], sc[:], ACT.Exp).then_inc(actd, 1)
            nc.scalar.activation(es[:], es[:], ACT.Exp).then_inc(actd, 1)
            act.wait_ge(pturn, 1)
            nc.scalar.activation(pt[:], c.ps[:, 1, 0:U * J], ACT.Copy).then_inc(ptd, 1)

        @block.vector
        def _(dve):
            v = nc.vector
            own = Steps(steps)
            for grp in range(G):
                for r in range(2):
                    v.tensor_copy(qg[grp * HD:(grp + 1) * HD, r:J:2, :],
                                  c.proj[r * HD:(r + 1) * HD, T_SQ + 2 * grp:T_SQ + 2 * grp + 2, SEQ:TOK]
                                  ).then_inc(qd, 1)
            dve.wait_ge(made, 2 + J * G)
            for grp in range(G):
                v.tensor_scalar(bias[:, grp], rel[:], slope[:, grp:grp + 1], None, ALU.mult).then_inc(biasd, 1)
            dve.wait_ge(biasd, 2)
            dve.wait_ge(scored, 1)
            for grp in range(G):
                n = own(v.scalar_tensor_tensor(out=sc[:, grp * DEC:(grp + 1) * DEC, :],
                                               in0=c.ps[0:J, 3 + 2 * grp:5 + 2 * grp, :]
                                               .rearrange("p c (b n) -> p (c b) n", n=P),
                                               scalar=HD ** -0.5, in1=bias[:, grp].unsqueeze(1)
                                               .to_broadcast([J, DEC, P]), op0=ALU.mult, op1=ALU.add))
            dve.wait_ge(own.sem, n)
            n = own(v.tensor_reduce(mx[:], sc[:], AX.X, ALU.max))
            dve.wait_ge(own.sem, n)
            dve.wait_ge(loaded, 64)
            n = own(v.tensor_tensor(by_unit(mx[:]), by_unit(mx[:]), sk[:].unsqueeze(2).to_broadcast([J, G, DEC]),
                                    ALU.max))
            dve.wait_ge(own.sem, n)
            own(v.tensor_tensor(by_unit(es[:]), sk[:].unsqueeze(2).to_broadcast([J, G, DEC]), by_unit(mx[:]),
                                ALU.subtract))
            own(v.tensor_tensor(sc[:], sc[:], mx[:].unsqueeze(2).to_broadcast([J, U, P]), ALU.subtract))
            dve.wait_ge(actd, 2)
            n = own(v.tensor_reduce(sums[:], sc[:], AX.X, ALU.add))
            dve.wait_ge(own.sem, n)
            n = own(v.tensor_tensor(sums[:], sums[:], es[:], ALU.add))
            dve.wait_ge(own.sem, n)
            n = own(v.reciprocal(sums[:], sums[:]))
            dve.wait_ge(own.sem, n)
            n = own(v.tensor_tensor(sc[:], sc[:], sums[:].unsqueeze(2).to_broadcast([J, U, P]), ALU.mult))
            assert n == LAST
            dve.wait_ge(od, 1)
            for grp in range(G):
                for r in range(2):
                    own(v.tensor_copy(c.proj[r * HD:(r + 1) * HD, T_SQ + 2 * grp:T_SQ + 2 * grp + 2, SEQ:TOK],
                                      c.ps[grp * HD:(grp + 1) * HD, 2, 0:DEC * J]
                                      .rearrange("p (b j) -> p j b", j=J)[:, r:J:2, :]))





def finish_phase(c, name, o_first, z_first, halves, vcol, sq_first, factor_first, plain):
    nc = c.nc
    n = HEADS * halves
    s = lambda x: c.sem(f"{name}_{x}")
    silud, sqd, summed, logged, fact, normed, gated, upper, lower, plain_upper = map(s, (
        "silu squares summed logged factor normed gated upper lower plain_upper").split())

    def square(h, j):
        return c.proj[:, sq_first + h, :] if j == 0 else c.tmp[:, h % 2]
    with nc.Block() as block:
        @block.scalar
        def _(act):
            for t in range(n):
                z = c.proj[:, z_first + t, :]
                nc.scalar.activation(z, z, ACT.Silu).then_inc(silud, 1)

            for h in range(HEADS):
                act.wait_ge(summed, h + 1)
                nc.scalar.activation(chunked(c.proj[:, factor_first + h, :]), tile_psum(c, h % 2), ACT.Ln, bias=c.eps[:],
                                     scale=1.0 / (halves * P)).then_inc(logged, 1)
            for h in range(HEADS):
                r = c.proj[:, factor_first + h, :]
                act.wait_ge(logged, h + 1)
                nc.scalar.activation(r, r, ACT.Exp, scale=-0.5).then_inc(fact, 1)
            for i, t in enumerate(plain):
                nc.scalar.activation(c.act_hi[:, n + i, :], c.proj[:, t, :], ACT.Copy).then_inc(plain_upper, 1)
            for t in range(n):
                act.wait_ge(normed, t + 1)
                nc.scalar.activation(c.act_hi[:, t, :], c.proj[:, o_first + t, :], ACT.Copy).then_inc(upper, 1)

        @block.tensor
        def _(pe):
            for h in range(HEADS):
                pe.wait_ge(sqd, (h + 1) * halves)
                if h >= 2:
                    pe.wait_ge(logged, h - 1)
                for ch in range(NCH):
                    for j in range(halves):
                        last = nc.tensor.matmul(c.ps[:, 3 * (h % 2) + ch, 0:CW], c.ones[:],
                                                square(h, j)[:, ch * CW:(ch + 1) * CW], start=j == 0,
                                                stop=j == halves - 1)
                last.then_inc(summed, 1)

        @block.vector
        def _(dve):
            v = nc.vector

            def squares(h):
                for j in range(halves):
                    if j and h >= 2:
                        dve.wait_ge(summed, h - 1)
                    o = c.proj[:, o_first + h * halves + j, :]
                    v.tensor_tensor(square(h, j), o, o, ALU.mult).then_inc(sqd, 1)

            def low(t, src, sem, count):
                dve.wait_ge(sem, count)
                v.tensor_tensor(c.act_lo[:, t, :], c.proj[:, src, :], c.act_hi[:, t, :].bitcast(F32), ALU.subtract
                                ).then_inc(lower, 1)
            for h in range(HEADS):
                squares(h)
            for t in range(n):
                o = c.proj[:, o_first + t, :]
                dve.wait_ge(silud, t + 1)
                v.scalar_tensor_tensor(out=o, in0=o, scalar=c.vcols[:, vcol + t % halves:vcol + t % halves + 1],
                                       in1=c.proj[:, z_first + t, :], op0=ALU.mult, op1=ALU.mult).then_inc(gated, 1)
            for t in range(n):
                o = c.proj[:, o_first + t, :]
                dve.wait_ge(fact, t // halves + 1)
                dve.wait_ge(gated, t + 1)
                v.tensor_tensor(o, o, c.proj[:, factor_first + t // halves, :], ALU.mult).then_inc(normed, 1)
                if t:
                    low(t - 1, o_first + t - 1, upper, t)
            for i, t in enumerate(plain):
                low(n + i, t, plain_upper, i + 1)
            low(n - 1, o_first + n - 1, upper, n)



def gla_prepare_phase(c, area):
    nc = c.nc
    H = HEADS
    logs = c.gla_logs = area("log_decay", [P, H, TOK])
    build_masks = level_masks(c, area, delta=False)
    brief = area.passing("gla_prepare")
    wg = brief("gate_up", [RANK, H, P])
    y, t1 = brief("gate", [P, 2, TOK]), brief("gate_exp", [P, 2, TOK])
    mask = brief("chunk_mask", [P, TOK])
    s = lambda n: c.sem("gp_" + n)
    loaded, masked, proj, gated, low, expd, logd, summed, done = map(s, (
        "loaded masked projected gated low exp log summed done").split())
    with nc.Block() as block:
        @block.sync
        def _(sp):
            sp.dma_start(wg[:], c.ins["gla_w_gate_up"].rearrange("e r (h n) -> (e r) h n", h=H)).then_inc(loaded, 16)

        @block.gpsimd
        def _(pool):
            nc.gpsimd.memset(mask[:], 0.0).then_inc(masked, 1)
            pool.wait_ge(masked, 1)
            nc.gpsimd.memset(mask[:, 0:SEQ].rearrange("p (c n) -> p c n", n=CHUNK)[:, :, 1:CHUNK], 1.0
                             ).then_inc(masked, 1)
            build_masks(pool)

        @block.tensor
        def _(pe):
            pe.wait_ge(loaded, 16)
            for h in range(H):
                if h >= 2:
                    pe.wait_ge(gated, h - 1)
                for ch in range(NCH):
                    last = nc.tensor.matmul(c.ps[:, 3 * (h % 2) + ch, 0:CW], wg[:, h],
                                            c.proj[0:RANK, G_D, ch * CW:(ch + 1) * CW], start=True, stop=True)
                last.then_inc(proj, 1)

        @block.scalar
        def _(act):
            for h in range(H):
                e = t1[:, h % 2]
                act.wait_ge(low, h + 1)
                nc.scalar.activation(e, e, ACT.Exp).then_inc(expd, 1)
                act.wait_ge(expd, h + 1)
                nc.scalar.activation(e, e, ACT.Ln, bias=c.ones[:, 0:1]).then_inc(logd, 1)

        @block.vector
        def _(dve):
            v = nc.vector

            def start(h):
                yy, e = y[:, h % 2], t1[:, h % 2]
                dve.wait_ge(proj, h + 1)
                if h >= 2:
                    dve.wait_ge(done, h - 1)
                v.tensor_scalar(chunked(yy), tile_psum(c, h % 2), c.vcols[:, V_GB + h:V_GB + h + 1], None, ALU.add
                                ).then_inc(gated, 1)
                dve.wait_ge(gated, h + 1)
                v.scalar_tensor_tensor(out=e, in0=yy, scalar=-1.0, in1=yy, op0=ALU.mult, op1=ALU.min).then_inc(low, 1)
            start(0)
            dve.wait_ge(masked, 2)
            for h in range(H):
                yy, e = y[:, h % 2], t1[:, h % 2]
                if h + 1 < H:
                    start(h + 1)
                dve.wait_ge(logd, h + 1)
                v.scalar_tensor_tensor(out=yy, in0=yy, scalar=0.0, in1=e, op0=ALU.min, op1=ALU.subtract
                                       ).then_inc(summed, 1)
                dve.wait_ge(summed, h + 1)
                v.tensor_tensor_scan(logs[:, h], mask[:], yy, 0.0, ALU.mult, ALU.add).then_inc(done, 1)



def gla_phase(c, area):
    nc = c.nc
    H = HEADS
    logs, masks = c.gla_logs, c.level_masks
    state = c.gla_state = area("state", [P, H, GDV])

    def two(name):
        return area(name, [P, 2, H, P])
    qs, kd = area("q_cols", [P, H, P]), area("k_left", [P, H, P])
    ks, qeg, kdn, att, eg = (two(n) for n in ("k_cols", "q_decayed", "k_left_rows", "attention", "decay"))
    d, w = two("exponents"), two("level_factors")
    vs, vn = area("v_cols", [P, 2, 2 * H, P]), area("v_rows", [P, 2, 2 * H, P])
    s = lambda n: c.sem("gla_" + n)
    (staged, diffd, expd, factd, prodd, egd, kdd, kturn, vturn, kout, vout, attd, qegd, od, oout, dsd, stated
     ) = map(s, ("staged diff exp factors product decay k_left k_turned v_turned k_out v_out attention "
                 "q_decayed o o_out ds state").split())
    stored = s("stored")
    SCALE = P ** -0.5
    NX = LEVELS + 1
    B = [c.ps[:, n, :] for n in range(8)]

    def halves(ap, level):
        v = ap.rearrange("p h (b s) -> p h b s", s=2 * 2 ** level)
        half = 2 ** level
        return v[:, :, :, 0:half], v[:, :, :, half:]

    def third_on(b):
        return not is_first(b) and not is_first(b - 1)

    with nc.Block() as block:
        @block.gpsimd
        def _(pool):
            g = nc.gpsimd

            def turn(b, slot):
                if is_last(b):
                    return
                tok = bass.ds(b * P, P)
                if third_on(b):
                    reach(c, pool, kdd, b - 1)
                    reach(c, pool, vturn, b * 2 - 2)
                g.tensor_copy(ks[:, slot], c.proj[:, G_K:G_K + H, tok]).then_inc(staged, 1)
                g.tensor_copy(vs[:, slot], c.proj[:, G_V:G_V + 2 * H, tok]).then_inc(staged, 1)
                lg = logs[:, :, tok]
                for level in range(LEVELS):
                    if level >= 2:
                        reach(c, pool, factd, b * 2 * LEVELS + 2 * (level - 1))
                    elif not is_first(b):
                        if level == 0:
                            reach(c, pool, factd, b * 2 * LEVELS)
                        else:
                            reach(c, pool, kdd, b * 1)
                    early, late = halves(lg, level)
                    to_e, to_l = halves(d[:, (slot + level) % 2], level)
                    n = 2 ** level
                    meet = early[:, :, :, n - 1:n].to_broadcast([P, H, P // (2 * n), n])
                    g.tensor_tensor(to_e, meet, early, ALU.subtract).then_inc(diffd, 1)
                    g.tensor_tensor(to_l, late, meet, ALU.subtract).then_inc(diffd, 1)
                reach(c, pool, factd, b * 2 * LEVELS + 2 * (LEVELS - 1))
                by_chunk = lg.rearrange("p h (a n) -> p h a n", n=CHUNK)
                g.tensor_tensor(d[:, (slot + LEVELS) % 2].rearrange("p h (a n) -> p h a n", n=CHUNK),
                                by_chunk[:, :, :, CHUNK - 1:CHUNK].to_broadcast([P, H, 2, CHUNK]), by_chunk,
                                ALU.subtract).then_inc(diffd, 1)
            in_turns(pool, turn)

        @block.scalar
        def _(act):
            a = nc.scalar.activation

            def o_rows(c1, n):
                reach(c, act, od, c1 * 2 + (n + 1))
                a(c.proj[:, G_V:G_V + 2 * H, bass.ds(c1 * P + n * CHUNK, CHUNK)],
                  B[7].rearrange("p (t n) -> p t n", t=2 * H), ACT.Copy).then_inc(oout, 1)

            def turn(b, slot):
                chain = not is_first(b)
                if is_last(b):
                    o_rows(b - 1, 0)
                    o_rows(b - 1, 1)
                    return
                tok = bass.ds(b * P, P)
                if third_on(b):
                    reach(c, act, stated, b * 8 - 7)
                a(eg[:, slot], logs[:, :, tok], ACT.Exp, scale=1.0 / TAU).then_inc(egd, 1)
                for x in range(NX):
                    act.wait_ge(diffd, b * (2 * LEVELS + 1) + min(2 * x + 2, 2 * LEVELS + 1))
                    a(d[:, (slot + x) % 2], d[:, (slot + x) % 2], ACT.Exp, scale=1.0 / TAU).then_inc(expd, 1)
                    if x == 1:
                        for n in range(2):
                            act.wait_ge(vturn, b * 2 + (n + 1))
                            a(vn[:, slot, 4 * n:4 * n + 4], B[4 + n], ACT.Copy).then_inc(vout, 1)
                    if chain and x in (3, 6):
                        o_rows(b - 1, x // 4)
                act.wait_ge(kturn, b + 1)
                a(kdn[:, slot], B[6], ACT.Copy).then_inc(kout, 1)
            in_turns(act, turn)

        @block.tensor
        def _(pe):
            t = nc.tensor

            def output(c1, a, slot):
                part = slice(a * CHUNK, (a + 1) * CHUNK)
                if a == 0:
                    pe.wait_ge(attd, c1 * NX + NX)
                    pe.wait_ge(kout, c1 + 1)
                pe.wait_ge(stated, c1 * 8 + (4 * a + 1))
                if a or not is_first(c1):
                    pe.wait_ge(oout, c1 * 2 + a)
                for h in range(H):
                    for half in range(2):
                        i = 2 * h + half
                        o = B[7][:, i * CHUNK:(i + 1) * CHUNK]
                        t.matmul(o, state[:, h, half * P:(half + 1) * P], qeg[:, slot, h, part], start=True, stop=False)
                        last = t.matmul(o, vn[part, slot, i], att[part, slot, h, part], start=False, stop=True)
                last.then_inc(od, 1)

            def state_product(a, slot):
                part = slice(a * CHUNK, (a + 1) * CHUNK)
                for h in range(H):
                    last = t.matmul(B[2 + h // 2][:, (h % 2) * GDV:(h % 2 + 1) * GDV], kdn[part, slot, h],
                                    vn[part, slot, 2 * h:2 * h + 2], start=True, stop=True)
                last.then_inc(dsd, 1)

            def turn(b, slot):
                chain = not is_first(b)
                if is_last(b):
                    for a in range(2):
                        output(b - 1, a, 1 - slot)
                        state_product(a, 1 - slot)
                    return
                pe.wait_ge(staged, b * 2 + 2)
                if chain:
                    pe.wait_ge(vout, b * 2)
                for n in range(2):
                    for i in range(4):
                        last = t.transpose(B[4 + n][:, i * P:(i + 1) * P], vs[:, slot, 4 * n + i], c.ident[:])
                    last.then_inc(vturn, 1)
                pe.wait_ge(qegd, b * 2 + 1)
                if chain:
                    pe.wait_ge(attd, b * NX)
                for h in range(H):
                    last = t.matmul(B[0][:, h * P:(h + 1) * P], ks[:, slot, h], qs[:, h], start=True, stop=True)
                last.then_inc(prodd, 1)
                for level in range(LEVELS):
                    pe.wait_ge(factd, b * 2 * LEVELS + 2 * level + 2)
                    if level >= 1:
                        pe.wait_ge(attd, b * NX + level)
                    for h in range(H):
                        last = t.matmul(B[(level + 1) % 2][:, h * P:(h + 1) * P], w[:, level % 2, h],
                                        w[:, level % 2, h], start=True, stop=True)
                    last.then_inc(prodd, 1)
                    if chain and level in (1, 4):
                        output(b - 1, level // 3, 1 - slot)
                        state_product(level // 3, 1 - slot)
                pe.wait_ge(kdd, b + 1)
                if chain:
                    pe.wait_ge(kout, b * 1)
                for h in range(H):
                    last = t.transpose(B[6][:, h * P:(h + 1) * P], kd[:, h], c.ident[:])
                last.then_inc(kturn, 1)
            in_turns(pe, turn)

        @block.vector
        def _(dve):
            v = nc.vector
            v.memset(state[:], 0.0).then_inc(stated, 1)

            def new_state(c1, n, slot):
                dve.wait_ge(dsd, c1 * 2 + (n + 1))
                for h in range(H):
                    last = n * CHUNK + CHUNK - 1
                    v.scalar_tensor_tensor(out=state[:, h], in0=state[:, h], scalar=eg[:, slot, h, last:last + 1],
                                           in1=B[2 + h // 2][:, (h % 2) * GDV:(h % 2 + 1) * GDV],
                                           op0=ALU.mult, op1=ALU.add).then_inc(stated, 1)

            def turn(b, slot):
                chain = not is_first(b)
                if is_last(b):
                    new_state(b - 1, 0, 1 - slot)
                    new_state(b - 1, 1, 1 - slot)
                    return
                tok = bass.ds(b * P, P)
                dve.sem_inc(c.passed[dve.engine], 1)
                v.tensor_scalar(qs[:], c.proj[:, G_Q:G_Q + H, tok], SCALE, None, ALU.mult).then_inc(qegd, 1)
                dve.wait_ge(egd, b + 1)
                dve.wait_ge(qegd, b * 2 + 1)
                v.tensor_tensor(qeg[:, slot], qs[:], eg[:, slot], ALU.mult).then_inc(qegd, 1)
                dve.wait_ge(staged, b * 2 + 1)
                reach(c, dve, prodd, b * NX + 1)
                v.tensor_tensor(att[:, slot], B[0].rearrange("p (h n) -> p h n", h=H),
                                c.ident[:].unsqueeze(1).to_broadcast([P, H, P]), ALU.mult).then_inc(attd, 1)

                def select(level):
                    dve.wait_ge(attd, b * NX + (level + 1))
                    reach(c, dve, prodd, b * NX + (level + 2))
                    v.copy_predicated(att[:, slot], masks[:, level].bitcast(mybir.dt.uint32).unsqueeze(1)
                                      .to_broadcast([P, H, P]),
                                      B[(level + 1) % 2].rearrange("p (h n) -> p h n", h=H)).then_inc(attd, 1)
                for level in range(LEVELS):
                    dve.wait_ge(expd, b * NX + (level + 1))
                    if level >= 2:
                        dve.wait_ge(prodd, b * NX + level)
                    w_e, w_l = halves(w[:, level % 2], level)
                    e_e, e_l = halves(d[:, (slot + level) % 2], level)
                    k_e, _ = halves(ks[:, slot], level)
                    _, q_l = halves(qs[:], level)
                    v.tensor_tensor(w_e, k_e, e_e, ALU.mult).then_inc(factd, 1)
                    v.tensor_tensor(w_l, q_l, e_l, ALU.mult).then_inc(factd, 1)
                    if level >= 1:
                        select(level - 1)
                    if chain and level == 2:
                        new_state(b - 1, 0, 1 - slot)
                dve.wait_ge(expd, b * NX + NX)
                if chain:
                    dve.wait_ge(kturn, b * 1)
                v.tensor_tensor(kd[:], ks[:, slot], d[:, (slot + LEVELS) % 2], ALU.mult).then_inc(kdd, 1)
                if chain:
                    new_state(b - 1, 1, 1 - slot)
                select(LEVELS - 1)
            in_turns(dve, turn)

        @block.sync
        def _(sp):
            sp.wait_ge(stated, 1 + 8 * NB)
            sp.dma_start(c.outs["p_state_gla"].rearrange("o b h k v -> k (o b h) v"), state[:]).then_inc(stored, 16)
            sp.wait_ge(stored, 16)



def gla_sample_phase(c, area):
    nc = c.nc
    H, U = HEADS, DEC * HEADS
    states = area("sample_states", [P, U, GDV])
    eg, qe, prod = area("decay", [P, H, DEC]), area("q_decayed", [P, H, DEC]), area("qk", [P, H, DEC])
    dots, tmp = area("dots", [P, H, DEC]), area("dots_v", [P, H, 2, DEC])
    diag = area("v_diagonals", [P, 2, 2 * H, P])
    s = lambda n: c.sem("gs_" + n)
    PARTS = 4
    EACH = DEC // PARTS
    loaded = [s(f"loaded{n}") for n in range(PARTS)]
    egd, dotted, mult, decayed, diagd, wide, new, steps, stored = map(s, (
        "decay dotted multiplied decayed diag wide new steps stored").split())
    q, k = c.proj[:, G_Q:G_Q + H, SEQ:TOK], c.proj[:, G_K:G_K + H, SEQ:TOK]
    vv = c.proj[:, G_V:G_V + 2 * H, SEQ:TOK]
    vcopy = area("v", [P, 2 * H, DEC])
    with nc.Block() as block:
        @block.sync
        def _(sp):
            for n in range(PARTS):
                sp.dma_start(states[:, n * EACH * H:(n + 1) * EACH * H],
                             c.ins["state_gla"].rearrange("o b h k v -> k (o b h) v")[:, n * EACH * H:(n + 1) * EACH * H]
                             ).then_inc(loaded[n], 16)
            with sp.Fori(0, DEC, 1) as b:
                sp.wait_ge(new, b * H + H)
                sp.dma_start(c.outs["s_state_gla"].rearrange("o b h k v -> k (o b) h v")[:, bass.ds(b, 1)]
                             .rearrange("k b h v -> k (b h) v"), states[:, bass.ds(b * H, H), :]).then_inc(stored, 16)
            sp.wait_ge(stored, 16 * DEC)

        @block.scalar
        def _(act):
            nc.scalar.activation(eg[:], c.gla_logs[:, :, SEQ:TOK], ACT.Exp, scale=1.0 / TAU).then_inc(egd, 1)
            act.wait_ge(egd, 1)
            for b in range(DEC):
                act.wait_ge(mult, b // EACH + 1)
                for h in range(H):
                    u = b * H + h
                    nc.scalar.activation(states[:, u], states[:, u], ACT.Copy, scale=eg[:, h, b:b + 1]
                                         ).then_inc(decayed, 1)

        @block.tensor
        def _(pe):
            t = nc.tensor
            pe.wait_ge(steps, 2)
            t.matmul(c.ps[:, 0, 0:U], c.ones[:], prod[:], start=True, stop=True).then_inc(dotted, 1)
            pe.wait_ge(steps, 3)
            for n in range(PARTS):
                pe.wait_ge(loaded[n], 16)
                for b in range(n * EACH, (n + 1) * EACH):
                    for h in range(H):
                        for half in range(2):
                            col = (2 * h + half) * DEC + b
                            last = t.matmul(c.ps[:, 1, col:col + 1], states[:, b * H + h, half * P:(half + 1) * P],
                                            qe[:, h, b:b + 1], start=True, stop=True)
                last.then_inc(mult, 1)
                for b in range(n * EACH, (n + 1) * EACH):
                    pe.wait_ge(diagd, b + 1)
                    if b >= 2:
                        pe.wait_ge(new, H * (b - 1))
                    for m in range(2):
                        last = t.matmul(c.ps[:, 2 + 2 * (b % 2) + m, :], c.ones[:], diag[:, b % 2, 4 * m:4 * m + 4],
                                        start=True, stop=True)
                    last.then_inc(wide, 1)

        @block.vector
        def _(dve):
            v = nc.vector
            own = Steps(steps)
            SCALE = P ** -0.5
            own(v.tensor_copy(vcopy[:], vv))
            own(v.scalar_tensor_tensor(out=prod[:], in0=q, scalar=SCALE, in1=k, op0=ALU.mult, op1=ALU.mult))
            dve.wait_ge(egd, 1)
            own(v.scalar_tensor_tensor(out=qe[:], in0=q, scalar=SCALE, in1=eg[:], op0=ALU.mult, op1=ALU.mult))
            dve.wait_ge(dotted, 1)
            n = own(v.tensor_copy(dots[:], c.ps[:, 0, 0:U]))
            dve.wait_ge(own.sem, n)
            n = own(v.tensor_tensor(tmp[:], vcopy[:].rearrange("p (h a) b -> p h a b", a=2),
                                    dots[:].unsqueeze(2).to_broadcast([P, H, 2, DEC]), ALU.mult))

            def update(b):
                dve.wait_ge(wide, b + 1)
                dve.wait_ge(decayed, (b + 1) * H)
                for h in range(H):
                    v.scalar_tensor_tensor(out=states[:, b * H + h],
                                           in0=c.ps[:, 2 + 2 * (b % 2) + h // 2, (h % 2) * GDV:(h % 2 + 1) * GDV],
                                           scalar=k[:, h, b:b + 1], in1=states[:, b * H + h], op0=ALU.mult,
                                           op1=ALU.add).then_inc(new, 1)
            for b in range(DEC):
                if b >= 2:
                    dve.wait_ge(wide, b - 1)
                v.tensor_tensor(diag[:, b % 2], c.ident[:].unsqueeze(1).to_broadcast([P, 2 * H, P]),
                                vcopy[:, :, b:b + 1].to_broadcast([P, 2 * H, P]), ALU.mult).then_inc(diagd, 1)
                if b >= 1:
                    update(b - 1)
            update(DEC - 1)
            dve.wait_ge(own.sem, n)
            dve.wait_ge(mult, PARTS)
            own(v.tensor_tensor(vv, tmp[:].rearrange("p h a b -> p (h a) b"),
                                c.ps[:, 1, 0:2 * H * DEC].rearrange("p (t b) -> p t b", b=DEC), ALU.add))



def give_back(c, before):
    mine = [name for name in c.sems if name not in before]
    c.nc.clear_and_free_semaphores([c.sems.pop(name) for name in mine])
    c.nc.all_engine_barrier()


def even_mixer_phases(c):
    area = mixer_area(c, "delta")
    delta_prepare_phase(c, area)
    delta_phase(c, area.passing("delta_main"))
    delta_sample_phase(c, area.passing("delta_sample"))
    area = mixer_area(c, "window")
    window_masks_phase(c, area)
    window_phase(c, area)
    window_sample_phase(c, mixer_area(c, "window_sample"))
    finish_phase(c, "even_finish", T_Q, T_Z, 1, V_DN, T_K, T_V, range(T_SQ, T_SQ + 4))


def odd_mixer_phases(c):
    area = mixer_area(c, "gla")
    gla_prepare_phase(c, area)
    gla_phase(c, area.passing("gla_main"))
    gla_sample_phase(c, area.passing("gla_sample"))
    finish_phase(c, "odd_finish", G_V, G_R, 2, V_GN, G_K, G_Q, [])


def program(nc, ins, outs):
    with ExitStack() as es:
        c = make(nc, es, ins, outs)
        even_w = ins["even_w_in"][0]
        even_in = ([cols_view(even_w, t * P) for t in range(12)] + [cols_view(even_w, E_Z + t * P) for t in range(4)]
                   + [cols_view(even_w, E_Q + t * P) for t in range(4)] + [cols_view(even_w, E_K), cols_view(even_w, E_V)]
                   + [cols_view(even_w, E_A, 2 * HEADS)])
        even_out = [cols_view(ins["even_w_out"][0], t * P) for t in range(KT)]
        odd_in = ([cols_view(ins["gla_w_in"][0], t * P) for t in range(ODD_TILES - 1)]
                  + [cols_view(ins["gla_w_in"][0], O_DOWN, RANK)])
        odd_out = [cols_view(ins["gla_w_out"][0], t * P) for t in range(KT)]
        mlp_first = [[cols_view(ins["mlp_w_up"][layer], t * P) for t in range(2)] for layer in range(2)]

        setup_phase(c, even_in[:2])
        even_projection_phase(c, V_MIX, even_in, even_out[:2])
        kept = set(c.sems)
        even_mixer_phases(c)
        give_back(c, kept)
        output_projection_phase(c, even_out, mlp_first[0], 1)
        mlp_phase(c, V_MLP, 0, odd_in[:2])
        projection_phase(c, V_MIX + KT, odd_in, odd_out[:2], saves=2)
        odd_mixer_phases(c)
        output_projection_phase(c, odd_out, mlp_first[1], 2)
        mlp_phase(c, V_MLP + KT, 1, [])
        final_phase(c)


OUTPUTS = [("y_prompt", (1, SEQ, D)), ("y_sample", (DEC, 1, D)), ("p_state_dn", (1, 1, HEADS, P, P)),
           ("p_state_dn_conv", (1, 1, CONV - 1, 3 * HEADS * P)), ("p_cache_swa_k", (1, 1, P, KVH, HD)),
           ("p_cache_swa_v", (1, 1, P, KVH, HD)), ("p_state_gla", (1, 1, HEADS, P, GDV)),
           ("s_state_dn", (1, DEC, HEADS, P, P)), ("s_state_dn_conv", (1, DEC, CONV - 1, 3 * HEADS * P)),
           ("s_cache_swa_k", (1, DEC, P, KVH, HD)), ("s_cache_swa_v", (1, DEC, P, KVH, HD)),
           ("s_state_gla", (1, DEC, HEADS, P, GDV))]


def kernel(**inputs):
    import numpy as np
    import concourse.bacc as bacc
    from concourse.bass_utils import run_bass_kernel_spmd
    nc = bacc.Bacc("TRN2", target_bir_lowering=False, num_devices=1)
    arrays = {name: np.ascontiguousarray(a) for name, a in inputs.items()}
    ins = {name: nc.dram_tensor(name, a.shape, mybir.dt.from_np(a.dtype), kind="ExternalInput").ap()
           for name, a in arrays.items()}
    outs = {name: nc.dram_tensor("o_" + name, shape, F32, kind="ExternalOutput").ap() for name, shape in OUTPUTS}
    program(nc, ins, outs)
    result = run_bass_kernel_spmd(nc, [arrays], core_ids=[0]).results[0]
    return tuple(result["o_" + name] for name, _ in OUTPUTS)
```
